# Optimizing a Trainium2 kernel written in Bass

```python
import jax, jax.numpy as jnp
from jax import lax
import numpy as np

D_MODEL = 1024
BATCH = 1
SEQ = 2048
DEPTH = 1

CHUNK = 64
HEAD_DIM = 64
SB_WIDTH = D_MODEL // 2
N_SB_HEADS = SB_WIDTH // HEAD_DIM
POOL_WINDOWS = (2, 4, 8, 16)
N_POOL_GROUPS = len(POOL_WINDOWS)
POOL_WIDTH = D_MODEL // 2
POOL_GROUP_DIM = POOL_WIDTH // N_POOL_GROUPS
N_BRANCHES = 2
MIX_PROJ_WIDTH = 3 * SB_WIDTH + POOL_WIDTH + N_BRANCHES * D_MODEL
Q_BLOCK = 128
N_EXPERT_GROUPS = 4
EXPERTS_PER_GROUP = 8
N_EXPERTS = N_EXPERT_GROUPS * EXPERTS_PER_GROUP
TOP_K_INNER = 2
D_EXPERT = D_MODEL // 2
MOE_BLOCK = 256
N_MOD = 6
EPS = 1e-6

kernel_name = 'hybrid_stickbreak_pool_hmoe_block'

def rms_norm(x, g):
    xf = x.astype(jnp.float32)
    y = xf * lax.rsqrt(jnp.mean(xf * xf, axis=-1, keepdims=True) + EPS)
    return (y * g.astype(jnp.float32)).astype(x.dtype)

def modulate(h, shift, scale):
    return h * (1.0 + scale[:, None, :]) + shift[:, None, :]

def stick_breaking_attention(q, k, v):
    seq = q.shape[2]
    inv_sqrt_d = HEAD_DIM ** -0.5
    outs = []
    for blk in range(seq // Q_BLOCK):
        q0 = blk * Q_BLOCK
        kv = q0 + Q_BLOCK
        z = jnp.einsum('bhtd,bhsd->bhts', q[:, :, q0:kv], k[:, :, :kv]).astype(jnp.float32) * inv_sqrt_d
        t_pos = q0 + jnp.arange(Q_BLOCK)[:, None]
        s_pos = jnp.arange(kv)[None, :]
        past = s_pos < t_pos
        log_stay = jnp.where(past, jax.nn.log_sigmoid(-z), 0.0)
        log_between = lax.cumsum(log_stay, axis=3, reverse=True) - log_stay
        a = jnp.where(past, jnp.exp(jax.nn.log_sigmoid(z) + log_between), 0.0)
        outs.append(jnp.einsum('bhts,bhsd->bhtd', a.astype(v.dtype), v[:, :, :kv]))
    return jnp.concatenate(outs, axis=2)

def multiscale_pool(p):
    b, s, _ = p.shape
    pg = p.reshape(b, s, N_POOL_GROUPS, POOL_GROUP_DIM).astype(jnp.float32)
    cs = jnp.concatenate([jnp.zeros((b, 1, N_POOL_GROUPS, POOL_GROUP_DIM), jnp.float32),
                          jnp.cumsum(pg, axis=1)], axis=1)
    t = jnp.arange(s)
    outs = []
    for g, w in enumerate(POOL_WINDOWS):
        lo = jnp.maximum(t + 1 - w, 0)
        win_sum = cs[:, 1:, g] - cs[:, lo, g]
        count = (t + 1 - lo).astype(jnp.float32)
        outs.append(win_sum / count[None, :, None])
    pooled = jnp.stack(outs, axis=2)
    return (pooled - pg).astype(p.dtype)

def hybrid_mixer(h, w_in, pool_w, pool_scale, w_branch_sb, w_branch_pool, w_out):
    b, s, _ = h.shape
    proj = h @ w_in
    q, k, v, p, gate_sb, gate_pool = jnp.split(
        proj, [SB_WIDTH, 2 * SB_WIDTH, 3 * SB_WIDTH, 3 * SB_WIDTH + POOL_WIDTH,
               3 * SB_WIDTH + POOL_WIDTH + D_MODEL], axis=-1)

    def heads(a):
        return a.reshape(b, s, N_SB_HEADS, HEAD_DIM).transpose(0, 2, 1, 3)

    o_sb = stick_breaking_attention(heads(q), heads(k), heads(v))
    o_sb = o_sb.transpose(0, 2, 1, 3).reshape(b, s, SB_WIDTH)

    pooled = multiscale_pool(p).reshape(b, s, N_POOL_GROUPS, POOL_GROUP_DIM)
    o_pool = jnp.einsum('bsgc,gcd->bsgd', pooled, pool_w).reshape(b, s, POOL_WIDTH) * pool_scale

    merged = (jax.nn.sigmoid(gate_sb) * (o_sb @ w_branch_sb)
              + jax.nn.sigmoid(gate_pool) * (o_pool @ w_branch_pool))
    return merged @ w_out

def hierarchical_moe(h, w_rg, b_rg, w_re, b_re, w_gate, w_up, w_down):
    b, s, d = h.shape
    n = b * s
    t = h.reshape(n, d)
    rows = jnp.arange(n)
    grp_logits = (t @ w_rg).astype(jnp.float32) + b_rg.astype(jnp.float32)
    grp_prob = jax.nn.softmax(grp_logits, axis=-1)
    _, gsel = lax.top_k(grp_logits, 1)
    p_group = grp_prob[rows, gsel[:, 0]]
    exp_logits = jnp.einsum('nd,gde->nge', t, w_re).astype(jnp.float32) + b_re.astype(jnp.float32)
    in_group = exp_logits[rows, gsel[:, 0]]
    top_val, top_idx = lax.top_k(in_group, TOP_K_INNER)
    combine = p_group[:, None] * jax.nn.softmax(top_val, axis=-1)
    expert_id = gsel * EXPERTS_PER_GROUP + top_idx

    nk = n * TOP_K_INNER
    flat_e = expert_id.reshape(nk)
    flat_tok = jnp.repeat(rows, TOP_K_INNER)
    flat_w = combine.reshape(nk)
    order = jnp.argsort(flat_e)
    sorted_e = flat_e[order]
    counts = jnp.zeros((N_EXPERTS,), jnp.int32).at[flat_e].add(1)
    padded = ((counts + MOE_BLOCK - 1) // MOE_BLOCK) * MOE_BLOCK
    pad_end = jnp.cumsum(padded)
    pad_start = pad_end - padded
    start = jnp.cumsum(counts) - counts
    dest = pad_start[sorted_e] + (jnp.arange(nk) - start[sorted_e])
    n_slots = ((nk + MOE_BLOCK - 1) // MOE_BLOCK + N_EXPERTS) * MOE_BLOCK
    n_blocks = n_slots // MOE_BLOCK
    slot_tok = jnp.zeros((n_slots,), jnp.int32).at[dest].set(flat_tok[order])
    slot_w = jnp.zeros((n_slots,), flat_w.dtype).at[dest].set(flat_w[order])
    block_e = jnp.minimum(jnp.searchsorted(pad_end, jnp.arange(n_blocks) * MOE_BLOCK, side='right'),
                          N_EXPERTS - 1)
    xs = t[slot_tok].reshape(n_blocks, MOE_BLOCK, d)

    def expert_block(args):
        xb, e = args
        return (jax.nn.silu(xb @ w_gate[e]) * (xb @ w_up[e])) @ w_down[e]

    ys = lax.map(expert_block, (xs, block_e)).reshape(n_slots, d)
    out = jnp.zeros((n, d), t.dtype).at[slot_tok].add(ys * slot_w[:, None].astype(t.dtype))
    return out.reshape(b, s, d)

def setup_inputs(seed: int = 0) -> dict:
    key = jax.random.key(seed)
    ks = jax.random.split(key, 20)
    f32 = jnp.float32

    def nrm(k, shape, scale):
        return jax.random.normal(k, shape, f32) * scale

    L = DEPTH
    return {
        'x': nrm(ks[0], (BATCH, SEQ, D_MODEL), 1.0),
        'c': nrm(ks[1], (BATCH, D_MODEL), 1.0),
        'norm1_g': 1.0 + nrm(ks[2], (L, D_MODEL), 0.05),
        'norm2_g': 1.0 + nrm(ks[3], (L, D_MODEL), 0.05),
        'w_ada': nrm(ks[4], (L, D_MODEL, N_MOD * D_MODEL), 0.5 * D_MODEL ** -0.5),
        'b_ada': nrm(ks[5], (L, N_MOD * D_MODEL), 0.01),
        'w_in': nrm(ks[6], (L, D_MODEL, MIX_PROJ_WIDTH), D_MODEL ** -0.5),
        'pool_w': nrm(ks[7], (L, N_POOL_GROUPS, POOL_GROUP_DIM, POOL_GROUP_DIM), POOL_GROUP_DIM ** -0.5),
        'pool_scale': 1.0 + nrm(ks[8], (L, POOL_WIDTH), 0.1),
        'w_branch_sb': nrm(ks[9], (L, SB_WIDTH, D_MODEL), SB_WIDTH ** -0.5),
        'w_branch_pool': nrm(ks[10], (L, POOL_WIDTH, D_MODEL), POOL_WIDTH ** -0.5),
        'w_out': nrm(ks[11], (L, D_MODEL, D_MODEL), D_MODEL ** -0.5),
        'w_route_group': nrm(ks[12], (L, D_MODEL, N_EXPERT_GROUPS), D_MODEL ** -0.5),
        'b_route_group': nrm(ks[13], (L, N_EXPERT_GROUPS), 0.01),
        'w_route_expert': nrm(ks[14], (L, N_EXPERT_GROUPS, D_MODEL, EXPERTS_PER_GROUP), D_MODEL ** -0.5),
        'b_route_expert': nrm(ks[15], (L, N_EXPERT_GROUPS, EXPERTS_PER_GROUP), 0.01),
        'w_exp_gate': nrm(ks[16], (L, N_EXPERTS, D_MODEL, D_EXPERT), D_MODEL ** -0.5),
        'w_exp_up': nrm(ks[17], (L, N_EXPERTS, D_MODEL, D_EXPERT), D_MODEL ** -0.5),
        'w_exp_down': nrm(ks[18], (L, N_EXPERTS, D_EXPERT, D_MODEL), D_EXPERT ** -0.5),
        'norm_f_g': 1.0 + nrm(ks[19], (D_MODEL,), 0.05),
    }

def reference(x, c, norm1_g, norm2_g, w_ada, b_ada, w_in, pool_w, pool_scale,
              w_branch_sb, w_branch_pool, w_out, w_route_group, b_route_group,
              w_route_expert, b_route_expert, w_exp_gate, w_exp_up, w_exp_down, norm_f_g):
    c_act = jax.nn.silu(c)
    for layer in range(DEPTH):
        mods = c_act @ w_ada[layer] + b_ada[layer]
        shift1, scale1, gate1, shift2, scale2, gate2 = jnp.split(mods, N_MOD, axis=-1)
        h = modulate(rms_norm(x, norm1_g[layer]), shift1, scale1)
        x = x + gate1[:, None, :] * hybrid_mixer(
            h, w_in[layer], pool_w[layer], pool_scale[layer],
            w_branch_sb[layer], w_branch_pool[layer], w_out[layer])
        h = modulate(rms_norm(x, norm2_g[layer]), shift2, scale2)
        x = x + gate2[:, None, :] * hierarchical_moe(
            h, w_route_group[layer], b_route_group[layer], w_route_expert[layer],
            b_route_expert[layer], w_exp_gate[layer], w_exp_up[layer], w_exp_down[layer])
    return rms_norm(x, norm_f_g)


_drawn_inputs = setup_inputs


def setup_inputs(seed=0):
    import zlib

    import numpy as np

    out = dict(_drawn_inputs(seed))
    spreads = {}
    factors = {'norm1_g': 4.256,
     'norm2_g': 3.151,
     'b_ada': 4.518,
     'pool_scale': 3.355,
     'b_route_group': 8.0,
     'b_route_expert': 8.0}
    for name, (base, spread) in spreads.items():
        noise = np.random.default_rng([zlib.crc32(name.encode()), seed]).standard_normal(out[name].shape)
        drawn = base * np.exp(spread * noise) if base else spread * noise
        out[name] = __import__('jax').numpy.asarray(drawn.astype(out[name].dtype))
    for name, factor in factors.items():
        out[name] = (out[name] * factor).astype(out[name].dtype)
    return out
```

```python
from contextlib import ExitStack

import concourse.bass as bass
from concourse import mybir

ALU = mybir.AluOpType
ACT = mybir.ActivationFunctionType
AX_X = mybir.AxisListType.X
F32 = mybir.dt.float32
I32 = mybir.dt.int32
U32 = mybir.dt.uint32
ds = bass.ds

P = 128
SEQ, D = 2048, 1024
KD = D // P
TILES = SEQ // P
BANK = 512
HD = 64
SBW = D // 2
PAIRS = SBW // P
POOLW = D // 2
GROUPS = 4
WINDOWS = (2, 4, 8, 16)
PAD = 16
EPS = 1e-6
EG, EPG = 4, 8
NE = EG * EPG
F = D // 2
KF = F // P
BLOCKS = 2 * SEQ // P + NE
SLOTS = BLOCKS * P
K_OFF, V_OFF, P_OFF, GS_OFF, GP_OFF = SBW, 2 * SBW, 3 * SBW, 3 * SBW + POOLW, 3 * SBW + POOLW + D


class Scope:

    def __init__(self, nc, stack, tag):
        self.nc, self.stack, self.tag = nc, stack, tag

    def sb(self, name, shape, dt=F32):
        return self.stack.enter_context(self.nc.sbuf_tensor(f"{self.tag}_{name}", shape, dt))

    def ps(self, name, shape, dt=F32):
        return self.stack.enter_context(self.nc.psum_tensor(f"{self.tag}_{name}", shape, dt))

    def sem(self, name):
        return self.stack.enter_context(self.nc.semaphore(f"{self.tag}_{name}"))

    def sems(self, name, n):
        return [self.sem(f"{name}{k}") for k in range(n)]


def constants_phase(nc, const):
    with ExitStack() as stack:
        s = Scope(nc, stack, "cst")
        filled, cut, ints, floats = s.sem("filled"), s.sem("cut"), s.sem("ints"), s.sem("floats")
        iota_i = s.sb("iota_i", [P, 64], I32)
        block = stack.enter_context(nc.Block())

        @block.gpsimd
        def _(pool):
            pool.memset(const["ident"][:], 0.0).then_inc(filled, 1)
            pool.memset(const["step"][:], 0.0).then_inc(filled, 1)
            pool.memset(const["corner"][:], 0.0).then_inc(filled, 1)
            pool.memset(const["before"][:], 1.0).then_inc(filled, 1)
            pool.memset(const["ones"][:], 1.0).then_inc(filled, 1)
            pool.memset(const["causal"][:], 0.0).then_inc(filled, 1)
            pool.memset(const["eps"][:], EPS).then_inc(filled, 1)
            pool.wait_ge(filled, 7)
            pool.affine_select(out=const["ident"][:], in_=const["ident"][:], compare_op=ALU.not_equal,
                               fill=1.0, base=0, pattern=[[-1, P]], channel_multiplier=1).then_inc(cut, 1)
            pool.affine_select(out=const["step"][:], in_=const["step"][:], compare_op=ALU.not_equal,
                               fill=-1.0, base=0, pattern=[[-1, P]], channel_multiplier=1).then_inc(cut, 1)
            pool.wait_ge(cut, 2)
            pool.affine_select(out=const["step"][:], in_=const["step"][:], compare_op=ALU.not_equal,
                               fill=1.0, base=-1, pattern=[[-1, P]], channel_multiplier=1).then_inc(cut, 1)
            pool.affine_select(out=const["corner"][:], in_=const["corner"][:], compare_op=ALU.not_equal,
                               fill=1.0, base=P - 1, pattern=[[-1, P]], channel_multiplier=P).then_inc(cut, 1)
            pool.affine_select(out=const["before"][:], in_=const["before"][:], compare_op=ALU.is_gt,
                               fill=0.0, base=0, pattern=[[1, P]], channel_multiplier=-1).then_inc(cut, 1)
            pool.affine_select(out=const["causal"][:, 0:P], in_=const["causal"][:, 0:P],
                               compare_op=ALU.is_gt, fill=1.0, base=0, pattern=[[1, P]],
                               channel_multiplier=-1).then_inc(cut, 1)
            pool.iota(iota_i[:], [[1, 64]], base=0, channel_multiplier=0).then_inc(ints, 1)
            pool.iota(const["rows"][:], [[P, TILES]], base=0, channel_multiplier=1).then_inc(ints, 1)
            pool.wait_ge(ints, 2)
            pool.tensor_copy(const["iota"][:], iota_i[:]).then_inc(floats, 1)
            pool.wait_ge(cut, 6)
            pool.wait_ge(floats, 1)


def modulation_phase(nc, ins, mods):
    SLOTS_W, N = 3, 6 * D // BANK
    with ExitStack() as stack:
        s = Scope(nc, stack, "ada")
        w = s.sb("w", [P, SLOTS_W, KD, BANK])
        c_col, c_sig, c_act = s.sb("c_col", [P, KD]), s.sb("c_sig", [P, KD]), s.sb("c_act", [P, KD])
        c_wide = s.sb("c_wide", [P, KD, P])
        ones = s.sb("ones", [P, P])
        g = s.sb("g", [P, 2, D])
        out = s.ps("out", [P, SLOTS_W, BANK])
        w_loaded = s.sems("w_loaded", SLOTS_W)
        c_loaded, b_loaded, g_loaded = s.sem("c_loaded"), s.sem("b_loaded"), s.sem("g_loaded")
        ones_set, sig_done, act_done, wide_done = s.sem("ones_set"), s.sem("sig_done"), s.sem("act_done"), s.sem("wide_done")
        product_done, added = s.sem("product_done"), s.sem("added")
        w_ada = ins["w_ada"][0].rearrange("(p k) n -> p k n", k=KD)
        block = stack.enter_context(nc.Block())

        @block.sync
        def _(sp):
            sp.dma_start(c_col[:], ins["c"][0].rearrange("(p k) -> p k", k=KD)).then_inc(c_loaded, 16)
            sp.dma_start(mods[:], ins["b_ada"][0:1].partition_broadcast(P)).then_inc(b_loaded, 16)
            with sp.Fori(0, N // SLOTS_W) as i:
                for u in range(SLOTS_W):
                    sp.wait_ge(product_done, i * SLOTS_W + u + 1)
                    sp.dma_start(w[:, u], w_ada[:, :, ds(i * (SLOTS_W * BANK) + u * BANK, BANK)]).then_inc(w_loaded[u], 16)

        @block.gpsimd
        def _(pool):
            pool.dma_start(g[:, 0], ins["norm1_g"][0:1].partition_broadcast(P)).then_inc(g_loaded, 16)
            pool.dma_start(g[:, 1], ins["norm2_g"][0:1].partition_broadcast(P)).then_inc(g_loaded, 16)

        @block.scalar
        def _(act):
            act.wait_ge(c_loaded, 16)
            act.activation(c_sig[:], c_col[:], ACT.Sigmoid).then_inc(sig_done, 1)

        @block.tensor
        def _(pe):
            pe.sem_inc(product_done, SLOTS_W)
            pe.wait_ge(wide_done, KD)
            with pe.Fori(0, N // SLOTS_W) as i:
                for u in range(SLOTS_W):
                    pe.wait_ge(w_loaded[u], i * 16 + 16)
                    pe.wait_ge(added, i * SLOTS_W + u + 1)
                    for k in range(KD):
                        mm = pe.matmul(out[:, u], c_wide[:, k], w[:, u, k], start=(k == 0), stop=(k == KD - 1))
                    mm.then_inc(product_done, 1)

        @block.vector
        def _(dve):
            dve.sem_inc(added, SLOTS_W)
            dve.memset(ones[:], 1.0).then_inc(ones_set, 1)
            dve.wait_ge(sig_done, 1)
            dve.tensor_tensor(c_act[:], c_col[:], c_sig[:], ALU.mult).then_inc(act_done, 1)
            dve.wait_ge(ones_set, 1)
            dve.wait_ge(act_done, 1)
            for k in range(KD):
                dve.tensor_scalar(c_wide[:, k], ones[:], c_act[:, k:k + 1], None, ALU.mult).then_inc(wide_done, 1)
            dve.wait_ge(b_loaded, 16)
            with dve.Fori(0, N // SLOTS_W) as i:
                for u in range(SLOTS_W):
                    dve.wait_ge(product_done, i * SLOTS_W + (SLOTS_W + u + 1))
                    part = mods[:, ds(i * (SLOTS_W * BANK) + u * BANK, BANK)]
                    dve.tensor_tensor(part, part, out[:, u], ALU.add).then_inc(added, 1)
            dve.wait_ge(added, SLOTS_W + N)
            dve.wait_ge(g_loaded, 32)
            for j in range(2):
                scale = mods[:, (3 * j + 1) * D:(3 * j + 2) * D]
                dve.scalar_tensor_tensor(scale, scale, 1.0, g[:, j], ALU.add, ALU.mult).then_inc(act_done, 1)
            dve.wait_ge(act_done, 3)


def norm1_phase(nc, ins, const, mods, hT):
    with ExitStack() as stack:
        s = Scope(nc, stack, "n1")
        x, h = s.sb("x", [P, 2, D]), s.sb("h", [P, 2, D])
        junk = s.sb("junk", [P, D])
        ssq, rms, rstd = s.sb("ssq", [P, 2]), s.sb("rms", [P, 2]), s.sb("rstd", [P, 2])
        turned = s.ps("turned", [P, 2, KD * P])
        x_loaded = s.sems("x_loaded", 2)
        ssq_done, rms_done, rstd_done = s.sem("ssq_done"), s.sem("rms_done"), s.sem("rstd_done")
        scaled, turn_done, hT_done = s.sem("scaled"), s.sem("turn_done"), s.sem("hT_done")
        h_done = s.sem("h_done")
        shift, scale = mods[:, 0:D], mods[:, D:2 * D]
        block = stack.enter_context(nc.Block())

        @block.sync
        def _(sp):
            with sp.Fori(0, TILES // 2) as i:
                for u in range(2):
                    sp.wait_ge(scaled, 2 * i + u + 1)
                    sp.dma_start(x[:, u], ins["x"][0, ds(i * (2 * P) + u * P, P), :]).then_inc(x_loaded[u], 16)

        @block.scalar
        def _(act):
            def square(i, u):
                act.wait_ge(x_loaded[u], i * 16 + 16)
                act.activation(junk[:], x[:, u], ACT.Square, accum_out=ssq[:, u:u + 1]).then_inc(ssq_done, 1)
                act.wait_ge(ssq_done, 2 * i + u + 1)
                act.activation(rms[:, u:u + 1], ssq[:, u:u + 1], ACT.Sqrt, bias=const["eps"][:],
                               scale=1.0 / D).then_inc(rms_done, 1)

            def evacuate(i, u):
                act.wait_ge(turn_done, 2 * i + (u + 3))
                act.copy(hT[:, :, ds(i * (2 * P) + u * P, P)], turned[:, u].rearrange("p (k t) -> p k t", k=KD)).then_inc(hT_done, 1)

            act.sem_inc(hT_done, 2)
            square(0, 0)
            with act.Fori(0, TILES // 2 - 1) as i:
                square(i, 1)
                evacuate(i, 0)
                square(i + 1, 0)
                evacuate(i, 1)
            square(TILES // 2 - 1, 1)
            evacuate(TILES // 2 - 1, 0)
            evacuate(TILES // 2 - 1, 1)
            act.wait_ge(hT_done, 2 + TILES)

        @block.vector
        def _(dve):
            dve.sem_inc(scaled, 2)
            with dve.Fori(0, TILES // 2) as i:
                for u in range(2):
                    dve.wait_ge(rms_done, 2 * i + u + 1)
                    dve.reciprocal(rstd[:, u:u + 1], rms[:, u:u + 1]).then_inc(rstd_done, 1)
                    dve.wait_ge(rstd_done, 2 * i + u + 1)
                    dve.wait_ge(turn_done, 2 * i + u + 1)
                    dve.scalar_tensor_tensor(h[:, u], x[:, u], rstd[:, u:u + 1], scale, ALU.mult, ALU.mult).then_inc(scaled, 1)
                    dve.wait_ge(scaled, 2 * i + (u + 3))
                    dve.tensor_tensor(h[:, u], h[:, u], shift, ALU.add).then_inc(h_done, 1)

        @block.tensor
        def _(pe):
            pe.sem_inc(turn_done, 2)
            with pe.Fori(0, TILES // 2) as i:
                for u in range(2):
                    pe.wait_ge(h_done, 2 * i + u + 1)
                    pe.wait_ge(hT_done, 2 * i + u + 1)
                    for k in range(KD):
                        mm = pe.transpose(turned[:, u, k * P:(k + 1) * P], h[:, u, k * P:(k + 1) * P], const["ident"][:])
                    mm.then_inc(turn_done, 1)


def attention_phase(nc, ins, const, hT, o_dram):
    CHUNK = BANK // P
    steps = []
    for q in range(TILES):
        for k in range(q, TILES, CHUNK):
            steps.append((q, k, min(CHUNK, TILES - k), k == q, k + CHUNK >= TILES))
    N = len(steps)
    JOBS = 16
    W_JOBS = 12
    last_step = {q: n for n, (q, _, _, _, last) in enumerate(steps) if last}
    with ExitStack() as stack:
        s = Scope(nc, stack, "att")
        w = s.sb("w", [P, 3, KD, P])
        qT, kT = s.sb("qT", [P, SEQ]), s.sb("kT", [P, SEQ])
        v, dv = s.sb("v", [P, TILES + 1, P]), s.sb("dv", [P, TILES, P])
        stay = s.sb("stay", [P, 2, 2, BANK])
        prod = s.sb("prod", [P, 2, 2, BANK])
        prodT = [[s.sb(f"prodT{u}{h}", [P, BANK]) for h in range(2)] for u in range(2)]
        o = s.sb("o", [P, 2, P])
        z = s.ps("z", [P, 4, BANK])
        turned = s.ps("turned", [P, 2, BANK])
        acc = s.ps("acc", [P, 2, BANK])
        w_loaded, v_pad = s.sem("w_loaded"), s.sem("v_pad")
        proj_done, copied_act, copied_dve = s.sem("proj_done"), s.sem("copied_act"), s.sem("copied_dve")
        z_done, stay_done, prod_done = s.sem("z_done"), s.sem("stay_done"), s.sem("prod_done")
        turn_done, prodT_done, pv_done = s.sem("turn_done"), s.sem("prodT_done"), s.sem("pv_done")
        o_done, o_stored = s.sem("o_done"), s.sems("o_stored", 2)
        w_in = ins["w_in"][0].rearrange("(k p) n -> p k n", p=P)
        block = stack.enter_context(nc.Block())

        def at(g, n, h):
            return g * (2 * N) + (2 * n + h + 1)

        @block.gpsimd
        def _(pool):
            pool.memset(v[:, TILES], 0.0).then_inc(v_pad, 1)

            def load(g):
                for j, off in enumerate((0, K_OFF, V_OFF)):
                    pool.dma_start(w[:, j], w_in[:, :, ds(g * P + off, P)]).then_inc(w_loaded, 16)

            load(0)
            with pool.Fori(1, PAIRS) as g:
                pool.wait_ge(proj_done, g * JOBS - (JOBS - W_JOBS))
                load(g)

        @block.tensor
        def _(pe):
            def bank_free(g, n):
                if n >= 4:
                    pe.wait_ge(copied_dve if n % 2 else copied_act, g * (JOBS // 2) + ((n - 4) // 2 + 1))

            pe.wait_ge(v_pad, 1)
            with pe.Fori(0, PAIRS) as g:
                pe.wait_ge(w_loaded, g * 48 + 48)
                for n in range(JOBS):
                    bank_free(g, n)
                    c = n % 4
                    if n < 8:
                        for k in range(KD):
                            mm = pe.matmul(z[:, c], w[:, n // 4, k], hT[:, k, c * BANK:(c + 1) * BANK],
                                           start=(k == 0), stop=(k == KD - 1))
                    elif n < 12:
                        for t in range(4):
                            at_t = (4 * c + t) * P
                            for k in range(KD):
                                mm = pe.matmul(z[:, c, t * P:(t + 1) * P], hT[:, k, at_t:at_t + P], w[:, 2, k],
                                               start=(k == 0), stop=(k == KD - 1))
                    else:
                        if n == 12:
                            pe.wait_ge(copied_act, g * (JOBS // 2) + 6)
                            pe.wait_ge(copied_dve, g * (JOBS // 2) + 6)
                        pe.matmul(z[:, c], const["step"][:], v[:, 4 * c:4 * c + 4].rearrange("p t n -> p (t n)"),
                                  start=True, stop=False)
                        mm = pe.matmul(z[:, c], const["corner"][:],
                                       v[:, 4 * c + 1:4 * c + 5].rearrange("p t n -> p (t n)"),
                                       start=False, stop=True)
                    mm.then_inc(proj_done, 1)
                pe.wait_ge(copied_act, g * (JOBS // 2) + JOBS // 2)
                pe.wait_ge(copied_dve, g * (JOBS // 2) + JOBS // 2)

                def scores(n):
                    q, k, m, _, _ = steps[n]
                    for h in range(2):
                        if n >= 2:
                            pe.wait_ge(stay_done, at(g, n - 2, h))
                        pe.matmul(z[:, 2 * (n % 2) + h, 0:m * P], qT[h * HD:(h + 1) * HD, q * P:(q + 1) * P],
                                  kT[h * HD:(h + 1) * HD, k * P:(k + m) * P], start=True, stop=True).then_inc(z_done, 1)

                def turn(n):
                    m = steps[n][2]
                    for h in range(2):
                        pe.wait_ge(prod_done, at(g, n, h))
                        if n >= 1:
                            pe.wait_ge(prodT_done, at(g, n - 1, h))
                        for b in range(m):
                            mm = pe.transpose(turned[:, h, b * P:(b + 1) * P], prod[:, h, n % 2, b * P:(b + 1) * P],
                                              const["ident"][:])
                        mm.then_inc(turn_done, 1)

                def weigh(n):
                    q, k, m, first, last = steps[n]
                    for h in range(2):
                        if first and q:
                            pe.wait_ge(o_done, g * TILES + q)
                        pe.wait_ge(prodT_done, at(g, n, h))
                        if first:
                            pe.matmul(acc[:, h, 0:HD], const["ones"][0:1, :], v[0:1, q, h * HD:(h + 1) * HD],
                                      start=True, stop=False)
                        for b in range(m):
                            mm = pe.matmul(acc[:, h, 0:HD], prodT[n % 2][h][:, b * P:(b + 1) * P],
                                           dv[:, k + b, h * HD:(h + 1) * HD], start=False, stop=(last and b == m - 1))
                        mm.then_inc(pv_done, 1)

                scores(0)
                for n in range(N):
                    if n + 1 < N:
                        scores(n + 1)
                    turn(n)
                    if n >= 1:
                        weigh(n - 1)
                weigh(N - 1)

        def copy_job(eng, copy, g, n):
            c = n % 4
            eng.wait_ge(proj_done, g * JOBS + (n + 1))
            if n < 8:
                out = (qT, kT)[n // 4][:, c * BANK:(c + 1) * BANK]
            else:
                out = (v, dv)[(n - 8) // 4][:, 4 * c:4 * c + 4].rearrange("p t n -> p (t n)")
            return copy(out, z[:, c])

        @block.scalar
        def _(act):
            with act.Fori(0, PAIRS) as g:
                for n in range(0, JOBS, 2):
                    copy_job(act, act.copy, g, n).then_inc(copied_act, 1)

                def stays(n):
                    m = steps[n][2]
                    for h in range(2):
                        act.wait_ge(z_done, at(g, n, h))
                        if n >= 2:
                            act.wait_ge(prod_done, at(g, n - 2, h))
                        act.activation(stay[:, h, n % 2, 0:m * P], z[:, 2 * (n % 2) + h, 0:m * P], ACT.Sigmoid,
                                       scale=-HD ** -0.5).then_inc(stay_done, 1)

                stays(0)
                for n in range(N):
                    if n + 1 < N:
                        stays(n + 1)
                    m = steps[n][2]
                    for h in range(2):
                        act.wait_ge(turn_done, at(g, n, h))
                        if n >= 2:
                            act.wait_ge(pv_done, at(g, n - 2, h))
                        act.copy(prodT[n % 2][h][:, 0:m * P], turned[:, h, 0:m * P]).then_inc(prodT_done, 1)

        @block.vector
        def _(dve):
            with dve.Fori(0, PAIRS) as g:
                for n in range(1, JOBS, 2):
                    copy_job(dve, dve.tensor_copy, g, n).then_inc(copied_dve, 1)

                def copy_o(q):
                    dve.wait_ge(pv_done, at(g, last_step[q], 1))
                    dve.wait_ge(o_stored[q % 2], g * (8 * TILES) + 16 * (q // 2 + 1))
                    dve.tensor_copy(o[:, q % 2].rearrange("p (h n) -> p h n", h=2), acc[:, :, 0:HD]).then_inc(o_done, 1)

                for n, (q, k, m, first, last) in enumerate(steps):
                    for h in range(2):
                        dve.wait_ge(stay_done, at(g, n, h))
                        if n >= 2:
                            dve.wait_ge(turn_done, at(g, n - 2, h))
                        start = 1.0
                        if n >= 1:
                            dve.wait_ge(prod_done, at(g, n - 1, h))
                        if not first:
                            start = prod[:, h, (n - 1) % 2, BANK - 1:BANK]
                        mask = const["causal"][:, 0:m * P] if first else const["causal"][:, P:P + 1].to_broadcast([P, m * P])
                        dve.tensor_tensor_scan(prod[:, h, n % 2, 0:m * P], stay[:, h, n % 2, 0:m * P], mask, start,
                                               ALU.mult, ALU.max).then_inc(prod_done, 1)
                    for q_done, n_done in last_step.items():
                        if n_done == n - 2:
                            copy_o(q_done)
                for q_done, n_done in last_step.items():
                    if n_done >= N - 2:
                        copy_o(q_done)

        @block.sync
        def _(sp):
            sp.sem_inc(o_stored[0], 16)
            sp.sem_inc(o_stored[1], 16)
            with sp.Fori(0, PAIRS) as g:
                for q in range(TILES):
                    sp.wait_ge(o_done, g * TILES + (q + 1))
                    sp.dma_start(o_dram[q * P:(q + 1) * P, ds(g * P, P)], o[:, q % 2]).then_inc(o_stored[q % 2], 16)
            for u in range(2):
                sp.wait_ge(o_stored[u], 16 + 8 * TILES * PAIRS)


def pool_phase(nc, ins, const, hT, opT_dram):
    L = SEQ + PAD
    CH = SEQ // BANK
    with ExitStack() as stack:
        s = Scope(nc, stack, "pool")
        w = s.sb("w", [P, 2, KD, P])
        w2 = s.sb("w2", [P, GROUPS, P])
        p_scale = s.sb("p_scale", [P, GROUPS])
        pT = s.sb("pT", [P, 2, L])
        sums = s.sb("sums", [P, 2, L])
        mean = s.sb("mean", [P, 2, SEQ])
        inv = s.sb("inv", [P, PAD])
        opT = s.sb("opT", [P, SEQ])
        proj, mapped = s.ps("proj", [P, 4, BANK]), s.ps("mapped", [P, 4, BANK])
        w_loaded, small_loaded, filled = s.sems("w_loaded", 2), s.sem("small_loaded"), s.sem("filled")
        proj_done, pT_done, dve_done = s.sem("proj_done"), s.sem("pT_done"), s.sem("dve_done")
        mean_done, map_done, opT_done, stored = s.sem("mean_done"), s.sem("map_done"), s.sem("opT_done"), s.sem("stored")
        w_in = ins["w_in"][0].rearrange("(k p) n -> p k n", p=P)
        block = stack.enter_context(nc.Block())

        @block.sync
        def _(sp):
            sp.dma_start(w2[:], ins["pool_w"][0].rearrange("g c n -> c g n")).then_inc(small_loaded, 16)
            sp.dma_start(p_scale[:], ins["pool_scale"][0].rearrange("(g p) -> p g", p=P), allow_slow_non_contiguous=True).then_inc(small_loaded, 16)
            for g in range(GROUPS):
                if g >= 2:
                    sp.wait_ge(proj_done, CH * (g - 1))
                sp.dma_start(w[:, g % 2], w_in[:, :, P_OFF + g * P:P_OFF + (g + 1) * P]).then_inc(w_loaded[g % 2], 16)
            for g in range(GROUPS):
                sp.wait_ge(opT_done, CH * (g + 1))
                sp.dma_start(opT_dram[g * P:(g + 1) * P, :], opT[:]).then_inc(stored, 16)
            sp.wait_ge(stored, 16 * GROUPS)

        @block.tensor
        def _(pe):
            def project(g):
                pe.wait_ge(w_loaded[g % 2], 16 * (g // 2 + 1))
                for c in range(CH):
                    if g:
                        pe.wait_ge(pT_done, CH * (g - 1) + c + 1)
                    for k in range(KD):
                        mm = pe.matmul(proj[:, c], w[:, g % 2, k], hT[:, k, c * BANK:(c + 1) * BANK],
                                       start=(k == 0), stop=(k == KD - 1))
                    mm.then_inc(proj_done, 1)

            def map_group(g):
                if g == 0:
                    pe.wait_ge(small_loaded, 32)
                pe.wait_ge(mean_done, g + 1)
                for c in range(CH):
                    if g:
                        pe.wait_ge(opT_done, CH * (g - 1) + c + 1)
                    pe.matmul(mapped[:, c], w2[:, g], mean[:, g % 2, c * BANK:(c + 1) * BANK],
                              start=True, stop=True).then_inc(map_done, 1)

            for g in range(GROUPS):
                project(g)
                if g:
                    map_group(g - 1)
            map_group(GROUPS - 1)

        @block.scalar
        def _(act):
            def take(g):
                for c in range(CH):
                    act.wait_ge(proj_done, CH * g + c + 1)
                    if g >= 2:
                        act.wait_ge(mean_done, g - 1)
                    act.copy(pT[:, g % 2, c * BANK:(c + 1) * BANK], proj[:, c]).then_inc(pT_done, 1)

            def finish(g):
                if g == 0:
                    act.wait_ge(small_loaded, 32)
                else:
                    act.wait_ge(stored, 16 * g)
                for c in range(CH):
                    act.wait_ge(map_done, CH * g + c + 1)
                    act.mul(opT[:, c * BANK:(c + 1) * BANK], mapped[:, c], p_scale[:, g:g + 1]).then_inc(opT_done, 1)

            for g in range(GROUPS):
                take(g)
                if g:
                    finish(g - 1)
            finish(GROUPS - 1)

        @block.gpsimd
        def _(pool):
            for b in (pT, sums):
                for u in range(2):
                    pool.memset(b[:, u, SEQ:L], 0.0).then_inc(filled, 1)
            for j in range(PAD):
                pool.memset(inv[:, j:j + 1], 1.0 / (PAD - j)).then_inc(filled, 1)

        @block.vector
        def _(dve):
            done = 0

            def chained(ins_):
                nonlocal done
                done += 1
                ins_.then_inc(dve_done, 1)
                dve.wait_ge(dve_done, done)

            dve.wait_ge(filled, 4 + PAD)
            for g, width in enumerate(WINDOWS):
                dve.wait_ge(pT_done, CH * (g + 1))
                p = pT[:, g % 2]
                src = p
                for level in range(g + 1):
                    out = sums[:, level % 2]
                    chained(dve.tensor_tensor(out[:, 0:SEQ], src[:, 0:SEQ], src[:, 1 << level:SEQ + (1 << level)], ALU.add))
                    src = out
                if g >= 2:
                    dve.wait_ge(map_done, CH * (g - 1))
                m, tail = mean[:, g % 2], width - 1
                chained(dve.scalar_tensor_tensor(m[:, 0:SEQ - tail], src[:, 0:SEQ - tail], 1.0 / width,
                                                 p[:, 0:SEQ - tail], ALU.mult, ALU.subtract))
                chained(dve.tensor_tensor(m[:, SEQ - tail:SEQ], src[:, SEQ - tail:SEQ], inv[:, PAD - tail:PAD], ALU.mult))
                dve.tensor_tensor(m[:, SEQ - tail:SEQ], m[:, SEQ - tail:SEQ], p[:, SEQ - tail:SEQ],
                                  ALU.subtract).then_inc(mean_done, 1)


def merge_phase(nc, ins, const, mods, hT, o_dram, opT_dram, x2_dram):
    NB, TB = SEQ // BANK, BANK // P
    KS = SBW // P
    with ExitStack() as stack:
        s = Scope(nc, stack, "mix")
        w_out = s.sb("w_out", [P, KD, D])
        wg = s.sb("wg", [P, 2, 2, KD, P])
        wb = s.sb("wb", [P, 2, 2, KS, P])
        o, oT, opT = s.sb("o", [P, TB, SBW]), s.sb("oT", [P, KS, BANK]), s.sb("opT", [P, KS, BANK])
        mT = s.sb("mT", [P, KD, BANK])
        gate, part = s.sb("gate", [P, 2, BANK]), s.sb("part", [P, 2, BANK])
        x = s.sb("x", [P, 2, D])
        prod = s.ps("prod", [P, 4, BANK])
        pair = s.ps("pair", [P, 2, BANK])
        turned = s.ps("turned", [P, 2, BANK])
        w_out_loaded, w_out_scaled = s.sem("w_out_loaded"), s.sem("w_out_scaled")
        w_loaded, o_loaded, opT_loaded = s.sems("w_loaded", 2), s.sem("o_loaded"), s.sem("opT_loaded")
        x_loaded, stored = s.sems("x_loaded", 2), s.sems("stored", 2)
        turn_done, oT_done = s.sem("turn_done"), s.sem("oT_done")
        prod_done, gate_done, part_done, mT_done = s.sem("prod_done"), s.sem("gate_done"), s.sem("part_done"), s.sem("mT_done")
        out_done, x2_done = s.sem("out_done"), s.sem("x2_done")
        w_in = ins["w_in"][0].rearrange("(k p) n -> p k n", p=P)
        w_sb = ins["w_branch_sb"][0].rearrange("(k p) n -> p k n", p=P)
        w_pl = ins["w_branch_pool"][0].rearrange("(k p) n -> p k n", p=P)
        block = stack.enter_context(nc.Block())

        @block.sync
        def _(sp):
            sp.dma_start(w_out[:], ins["w_out"][0].rearrange("(k p) n -> p k n", p=P)).then_inc(w_out_loaded, 16)
            with sp.Fori(0, NB) as b:
                for d in range(KD):
                    sp.wait_ge(prod_done, b * (4 * KD) + 4 * (d + 1))
                    for j, (off, wbr) in enumerate(((GS_OFF, w_sb), (GP_OFF, w_pl))):
                        sp.dma_start(wg[:, d % 2, j], w_in[:, :, off + d * P:off + (d + 1) * P]).then_inc(w_loaded[d % 2], 16)
                        sp.dma_start(wb[:, d % 2, j], wbr[:, :, d * P:(d + 1) * P]).then_inc(w_loaded[d % 2], 16)

        @block.gpsimd
        def _(pool):
            pool.dma_start(o[:], o_dram[0:BANK].rearrange("(t p) n -> p t n", p=P)).then_inc(o_loaded, 16)
            pool.dma_start(opT[:], opT_dram[:, 0:BANK].rearrange("(k p) n -> p k n", p=P)).then_inc(opT_loaded, 16)

            def tokens(b):
                for t in range(TB):
                    pool.wait_ge(stored[t % 2], b * (8 * TB) + 16 * (t // 2 + 1))
                    pool.dma_start(x[:, t % 2], ins["x"][0, ds(b * BANK + t * P, P), :]).then_inc(x_loaded[t % 2], 16)

            with pool.Fori(1, NB) as b:
                pool.wait_ge(turn_done, b * TB)
                pool.dma_start(o[:], o_dram[ds(b * BANK, BANK)].rearrange("(t p) n -> p t n", p=P)).then_inc(o_loaded, 16)
                pool.wait_ge(prod_done, b * (4 * KD) + 8)
                pool.dma_start(opT[:], opT_dram[:, ds(b * BANK, BANK)].rearrange("(k p) n -> p k n", p=P)).then_inc(opT_loaded, 16)
                tokens(b - 1)
            tokens(NB - 1)

        @block.tensor
        def _(pe):
            pe.sem_inc(prod_done, 8)
            with pe.Fori(0, NB) as b:
                pe.wait_ge(o_loaded, b * 16 + 16)
                for t in range(TB):
                    pe.wait_ge(oT_done, b * TB + (t + 1))
                    for k in range(KS):
                        mm = pe.transpose(turned[:, t % 2, k * P:(k + 1) * P], o[:, t, k * P:(k + 1) * P], const["ident"][:])
                    mm.then_inc(turn_done, 1)
                for d in range(KD):
                    pe.wait_ge(w_loaded[d % 2], b * (32 * KD) + 64 * (d // 2 + 1))
                    for j in range(2):
                        pe.wait_ge(gate_done, b * (2 * KD) + (2 * d + j + 1))
                        for k in range(KD):
                            mm = pe.matmul(prod[:, 2 * j], wg[:, d % 2, j, k], hT[:, k, ds(b * BANK, BANK)],
                                           start=(k == 0), stop=(k == KD - 1))
                        mm.then_inc(prod_done, 1)
                        if d == 0 and j == 0:
                            pe.wait_ge(oT_done, b * TB + (TB + 2))
                        if d == 0 and j == 1:
                            pe.wait_ge(opT_loaded, b * 16 + 16)
                        pe.wait_ge(part_done, b * (2 * KD) + (2 * d + j + 1))
                        for k in range(KS):
                            mm = pe.matmul(prod[:, 2 * j + 1], wb[:, d % 2, j, k], (oT, opT)[j][:, k],
                                           start=(k == 0), stop=(k == KS - 1))
                        mm.then_inc(prod_done, 1)
                pe.wait_ge(w_out_scaled, KD)
                pe.wait_ge(mT_done, b * KD + (KD + 1))
                for t in range(TB):
                    for j in range(2):
                        pe.wait_ge(x2_done, b * (2 * TB) + (2 * t + j + 1))
                        for k in range(KD):
                            mm = pe.matmul(pair[:, j], mT[:, k, t * P:(t + 1) * P], w_out[:, k, j * BANK:(j + 1) * BANK],
                                           start=(k == 0), stop=(k == KD - 1))
                        mm.then_inc(out_done, 1)

        @block.scalar
        def _(act):
            act.sem_inc(oT_done, 2)
            act.sem_inc(gate_done, 2)
            for u in range(2):
                act.sem_inc(stored[u], 16)
            with act.Fori(0, NB) as b:
                act.wait_ge(prod_done, b * (4 * KD) + 8)
                for t in range(TB):
                    act.wait_ge(turn_done, b * TB + (t + 1))
                    act.copy(oT[:, :, t * P:(t + 1) * P], turned[:, t % 2].rearrange("p (k t) -> p k t", k=KS)).then_inc(oT_done, 1)
                for d in range(KD):
                    for j in range(2):
                        act.wait_ge(prod_done, b * (4 * KD) + (8 + 4 * d + 2 * j + 1))
                        act.wait_ge(part_done, b * (2 * KD) + (2 * d + j + 1))
                        act.activation(gate[:, j], prod[:, 2 * j], ACT.Sigmoid).then_inc(gate_done, 1)
                for t in range(TB):
                    act.wait_ge(x2_done, b * (2 * TB) + (2 * t + 4))
                    act.dma_start(x2_dram[ds(b * BANK + t * P, P), :], x[:, t % 2]).then_inc(stored[t % 2], 16)
            for u in range(2):
                act.wait_ge(stored[u], 16 + 8 * TB * NB)

        @block.vector
        def _(dve):
            dve.sem_inc(mT_done, 1)
            dve.sem_inc(part_done, 2)
            dve.sem_inc(x2_done, 2)
            dve.wait_ge(w_out_loaded, 16)
            for k in range(KD):
                dve.tensor_tensor(w_out[:, k], w_out[:, k], mods[:, 2 * D:3 * D], ALU.mult).then_inc(w_out_scaled, 1)
            with dve.Fori(0, NB) as b:
                for d in range(KD):
                    for j in range(2):
                        dve.wait_ge(mT_done, b * KD + (d + 1))
                        dve.wait_ge(gate_done, b * (2 * KD) + (2 * d + j + 3))
                        dve.wait_ge(prod_done, b * (4 * KD) + (8 + 4 * d + 2 * j + 2))
                        dve.tensor_tensor(part[:, j], gate[:, j], prod[:, 2 * j + 1], ALU.mult).then_inc(part_done, 1)
                    dve.wait_ge(part_done, b * (2 * KD) + (2 * d + 4))
                    dve.tensor_tensor(mT[:, d], part[:, 0], part[:, 1], ALU.add).then_inc(mT_done, 1)
                for t in range(TB):
                    dve.wait_ge(x_loaded[t % 2], b * (8 * TB) + 16 * (t // 2 + 1))
                    for j in range(2):
                        dve.wait_ge(out_done, b * (2 * TB) + (2 * t + j + 1))
                        half = x[:, t % 2, j * BANK:(j + 1) * BANK]
                        dve.tensor_tensor(half, half, pair[:, j], ALU.add).then_inc(x2_done, 1)


def route_phase(nc, ins, const, mods, logits, x2_dram, h2_dram):
    with ExitStack() as stack:
        s = Scope(nc, stack, "rt")
        x, h = s.sb("x", [P, 2, D]), s.sb("h", [P, 2, D])
        hT = [s.sb(f"hT{u}", [P, KD, P]) for u in range(2)]
        wr = s.sb("wr", [P, KD, EG + NE])
        bias = s.sb("bias", [P, EG + NE])
        junk = s.sb("junk", [P, D])
        ssq, rms, rstd = s.sb("ssq", [P, 2]), s.sb("rms", [P, 2]), s.sb("rstd", [P, 2])
        turned = s.ps("turned", [P, 2, KD * P])
        routed = s.ps("routed", [P, 2, BANK])
        x_loaded, wr_loaded, stored = s.sems("x_loaded", 2), s.sem("wr_loaded"), s.sems("stored", 2)
        ssq_done, rms_done, rstd_done, h_done = s.sem("ssq_done"), s.sem("rms_done"), s.sem("rstd_done"), s.sem("h_done")
        scaled, turn_done, hT_done, route_done, logits_done = (s.sem("scaled"), s.sem("turn_done"), s.sem("hT_done"),
                                                               s.sem("route_done"), s.sem("logits_done"))
        shift, scale = mods[:, 3 * D:4 * D], mods[:, 4 * D:5 * D]
        block = stack.enter_context(nc.Block())

        @block.sync
        def _(sp):
            sp.dma_start(wr[:, :, 0:EG], ins["w_route_group"][0].rearrange("(k p) n -> p k n", p=P)).then_inc(wr_loaded, 16)
            for g in range(EG):
                sp.dma_start(wr[:, :, EG + g * EPG:EG + (g + 1) * EPG],
                             ins["w_route_expert"][0, g].rearrange("(k p) n -> p k n", p=P)).then_inc(wr_loaded, 16)
            sp.dma_start(bias[:, 0:EG], ins["b_route_group"][0:1].partition_broadcast(P)).then_inc(wr_loaded, 16)
            sp.dma_start(bias[:, EG:], ins["b_route_expert"][0:1].rearrange("a g e -> a (g e)").partition_broadcast(P)).then_inc(wr_loaded, 16)
            for u in range(2):
                sp.sem_inc(stored[u], 16)
            with sp.Fori(0, TILES // 2) as i:
                for u in range(2):
                    sp.wait_ge(h_done, 2 * i + u + 1)
                    sp.dma_start(h2_dram[ds(i * (2 * P) + u * P, P), :], h[:, u]).then_inc(stored[u], 16)
            for u in range(2):
                sp.wait_ge(stored[u], 16 + 8 * TILES)

        @block.gpsimd
        def _(pool):
            with pool.Fori(0, TILES // 2) as i:
                for u in range(2):
                    pool.wait_ge(scaled, 2 * i + u + 1)
                    pool.dma_start(x[:, u], x2_dram[ds(i * (2 * P) + u * P, P), :]).then_inc(x_loaded[u], 16)

        @block.scalar
        def _(act):
            def square(i, u):
                act.wait_ge(x_loaded[u], i * 16 + 16)
                act.activation(junk[:], x[:, u], ACT.Square, accum_out=ssq[:, u:u + 1]).then_inc(ssq_done, 1)
                act.wait_ge(ssq_done, 2 * i + u + 1)
                act.activation(rms[:, u:u + 1], ssq[:, u:u + 1], ACT.Sqrt, bias=const["eps"][:],
                               scale=1.0 / D).then_inc(rms_done, 1)

            def evacuate(i, u):
                act.wait_ge(turn_done, 2 * i + (u + 3))
                act.wait_ge(route_done, 2 * i + (u + 1))
                act.copy(hT[u][:].rearrange("p k t -> p (k t)"), turned[:, u]).then_inc(hT_done, 1)

            act.sem_inc(hT_done, 2)
            square(0, 0)
            with act.Fori(0, TILES // 2 - 1) as i:
                square(i, 1)
                evacuate(i, 0)
                square(i + 1, 0)
                evacuate(i, 1)
            square(TILES // 2 - 1, 1)
            evacuate(TILES // 2 - 1, 0)
            evacuate(TILES // 2 - 1, 1)

        @block.vector
        def _(dve):
            def normalise(i, u):
                dve.wait_ge(rms_done, 2 * i + u + 1)
                dve.reciprocal(rstd[:, u:u + 1], rms[:, u:u + 1]).then_inc(rstd_done, 1)
                dve.wait_ge(rstd_done, 2 * i + u + 1)
                dve.wait_ge(turn_done, 2 * i + u + 1)
                dve.wait_ge(stored[u], i * 16 + 16)
                dve.scalar_tensor_tensor(h[:, u], x[:, u], rstd[:, u:u + 1], scale, ALU.mult, ALU.mult).then_inc(scaled, 1)
                dve.wait_ge(scaled, 2 * i + (u + 3))
                dve.tensor_tensor(h[:, u], h[:, u], shift, ALU.add).then_inc(h_done, 1)

            def take(i, u):
                dve.wait_ge(route_done, 2 * i + (u + 3))
                dve.tensor_tensor(logits[:, ds(2 * i + u, 1), :].rearrange("p a n -> p (a n)"), routed[:, u, 0:EG + NE],
                                  bias[:], ALU.add).then_inc(logits_done, 1)

            dve.sem_inc(scaled, 2)
            dve.sem_inc(logits_done, 2)
            dve.wait_ge(wr_loaded, 16 * (EG + 3))
            normalise(0, 0)
            with dve.Fori(0, TILES // 2 - 1) as i:
                normalise(i, 1)
                take(i, 0)
                normalise(i + 1, 0)
                take(i, 1)
            normalise(TILES // 2 - 1, 1)
            take(TILES // 2 - 1, 0)
            take(TILES // 2 - 1, 1)
            dve.wait_ge(logits_done, 2 + TILES)

        @block.tensor
        def _(pe):
            def turn(i, u):
                pe.wait_ge(h_done, 2 * i + u + 1)
                pe.wait_ge(hT_done, 2 * i + u + 1)
                for k in range(KD):
                    mm = pe.transpose(turned[:, u, k * P:(k + 1) * P], h[:, u, k * P:(k + 1) * P], const["ident"][:])
                mm.then_inc(turn_done, 1)

            def route(i, u):
                pe.wait_ge(hT_done, 2 * i + (u + 3))
                pe.wait_ge(logits_done, 2 * i + (u + 1))
                for k in range(KD):
                    mm = pe.matmul(routed[:, u, 0:EG + NE], hT[u][:, k], wr[:, k], start=(k == 0), stop=(k == KD - 1))
                mm.then_inc(route_done, 1)

            pe.sem_inc(turn_done, 2)
            pe.sem_inc(route_done, 2)
            pe.wait_ge(wr_loaded, 16 * (EG + 3))
            turn(0, 0)
            with pe.Fori(0, TILES // 2 - 1) as i:
                turn(i, 1)
                route(i, 0)
                turn(i + 1, 0)
                route(i, 1)
            turn(TILES // 2 - 1, 1)
            route(TILES // 2 - 1, 0)
            route(TILES // 2 - 1, 1)


def dispatch_phase(nc, const, logits, weight, slot, block_expert, slot_row_dram):
    T = TILES
    with ExitStack() as stack:
        s = Scope(nc, stack, "dsp")
        gl, el = logits[:, :, 0:EG], logits[:, :, EG:].rearrange("p t (g e) -> p t g e", g=EG)
        gmax, gsum, p_group, index = s.sb("gmax", [P, T, 1]), s.sb("gsum", [P, T, 1]), s.sb("p_group", [P, T, 1]), s.sb("index", [P, T, 1])
        tmp4, g_hot = s.sb("tmp4", [P, T, EG]), s.sb("g_hot", [P, T, EG])
        inner, tmp8 = s.sb("inner", [P, T, EPG]), s.sb("tmp8", [P, T, EPG])
        e_hot = s.sb("e_hot", [P, 2, T, EPG])
        best = s.sb("best", [P, 2, T, 1])
        gap = s.sb("gap", [P, 2, T])
        hot = s.sb("hot", [P, 2, T, NE])
        either, earlier = s.sb("either", [P, T, NE]), s.sb("earlier", [P, T + 1, NE])
        place, picked = s.sb("place", [P, T, NE]), s.sb("picked", [P, 2, T, NE])
        count_i, filled_i = s.sb("count_i", [P, NE], I32), s.sb("filled_i", [P, NE], I32)
        filled, end, base = s.sb("filled", [P, NE]), s.sb("end", [P, NE]), s.sb("base", [P, NE])
        slot_f = s.sb("slot_f", [P, 2, T])
        over = s.sb("over", [P, BLOCKS, NE])
        expert_f = s.sb("expert_f", [P, BLOCKS])
        zero_rows = s.sb("zero_rows", [P, SLOTS // P], U32)
        rank, total = s.ps("rank", [P, BANK]), s.ps("total", [P, BANK])
        done, zeroed, zero_stored, scattered = s.sem("done"), s.sem("zeroed"), s.sem("zero_stored"), s.sem("scattered")
        exp_done, weight_done, ranked = s.sem("exp_done"), s.sem("weight_done"), s.sem("ranked")
        at = {}
        count = [0]
        block = stack.enter_context(nc.Block())

        @block.vector
        def _(dve):
            def step(ins_, name=None):
                count[0] += 1
                ins_.then_inc(done, 1)
                dve.wait_ge(done, count[0])
                if name:
                    at[name] = count[0]

            def first_best(values, top, n, hot_out):
                tmp = (tmp4 if n == EG else tmp8)[:]
                step(dve.tensor_tensor(tmp, values, top.to_broadcast([P, T, n]), ALU.is_equal))
                places = const["iota"][:, 0:n].unsqueeze(1).to_broadcast([P, T, n])
                step(dve.scalar_tensor_tensor(hot_out, places, -float(n), tmp, ALU.add, ALU.mult))
                step(dve.tensor_reduce(index[:], hot_out, AX_X, ALU.min))
                step(dve.tensor_scalar(index[:], index[:], float(n), None, ALU.add))
                step(dve.tensor_tensor(hot_out, places, index[:].to_broadcast([P, T, n]), ALU.is_equal))

            step(dve.memset(zero_rows[:], 0), "zero_rows")
            step(dve.tensor_reduce(gmax[:], gl, AX_X, ALU.max))
            step(dve.tensor_tensor(tmp4[:], gl, gmax[:].to_broadcast([P, T, EG]), ALU.subtract), "group_gap")
            dve.wait_ge(exp_done, 1)
            step(dve.tensor_reduce(gsum[:], tmp4[:], AX_X, ALU.add))
            step(dve.reciprocal(p_group[:], gsum[:]))
            first_best(gl, gmax[:], EG, g_hot[:])
            step(dve.tensor_tensor(inner[:], el[:, :, 0], g_hot[:, :, 0:1].to_broadcast([P, T, EPG]), ALU.mult))
            for g in range(1, EG):
                step(dve.tensor_tensor(tmp8[:], el[:, :, g], g_hot[:, :, g:g + 1].to_broadcast([P, T, EPG]), ALU.mult))
                step(dve.tensor_tensor(inner[:], inner[:], tmp8[:], ALU.add))
            for j in range(2):
                step(dve.tensor_reduce(best[:, j], inner[:], AX_X, ALU.max))
                first_best(inner[:], best[:, j], EPG, e_hot[:, j])
                if j == 0:
                    step(dve.scalar_tensor_tensor(inner[:], e_hot[:, 0], -1e30, inner[:], ALU.mult, ALU.add))
            for j in range(2):
                step(dve.tensor_tensor(gap[:, j], best[:, j, :, 0], best[:, 1 - j, :, 0], ALU.subtract), "best_gap")
            for j in range(2):
                for g in range(EG):
                    step(dve.tensor_tensor(hot[:, j, :, g * EPG:(g + 1) * EPG], e_hot[:, j],
                                           g_hot[:, :, g:g + 1].to_broadcast([P, T, EPG]), ALU.mult))
            step(dve.tensor_tensor(either[:], hot[:, 0], hot[:, 1], ALU.add))
            step(dve.memset(earlier[:, 0], 0.0))
            for t in range(T):
                step(dve.tensor_tensor(earlier[:, t + 1], earlier[:, t], either[:, t], ALU.add), "counted")
            dve.wait_ge(weight_done, 1)
            for j in range(2):
                step(dve.tensor_tensor(weight[:, j], gap[:, j], p_group[:, :, 0], ALU.mult))
            dve.wait_ge(ranked, 1)
            step(dve.tensor_scalar(count_i[:], total[:, 0:NE], float(P - 1), None, ALU.add))
            step(dve.tensor_scalar(filled_i[:], count_i[:], 7, None, ALU.arith_shift_right))
            step(dve.tensor_copy(filled[:], filled_i[:]))
            zero = const["causal"][:, P:P + 1]
            step(dve.tensor_tensor_scan(end[:], filled[:], zero.to_broadcast([P, NE]), 0.0, ALU.add, ALU.add))
            step(dve.tensor_tensor(base[:], end[:], filled[:], ALU.subtract))
            step(dve.scalar_tensor_tensor(place[:], base[:].unsqueeze(1).to_broadcast([P, T, NE]), float(P),
                                          rank[:].rearrange("p (t e) -> p t e", t=T), ALU.mult, ALU.add))
            for j in range(2):
                step(dve.tensor_tensor(picked[:, j], place[:], hot[:, j], ALU.mult))
                step(dve.tensor_reduce(slot_f[:, j].unsqueeze(2), picked[:, j], AX_X, ALU.add))
                step(dve.tensor_copy(slot[:, j], slot_f[:, j]), "slots")
            n = BLOCKS
            step(dve.tensor_tensor(over[:], end[:].unsqueeze(1).to_broadcast([P, n, NE]),
                                   const["iota"][:, 0:n].unsqueeze(2).to_broadcast([P, n, NE]), ALU.is_le))
            step(dve.tensor_reduce(expert_f[:].unsqueeze(2), over[:], AX_X, ALU.add))
            step(dve.tensor_scalar(block_expert[:, 0:n], expert_f[:], float(NE - 1), None, ALU.min))
            step(dve.tensor_scalar(count_i[:, 0:1], end[:, NE - 1:NE], -1.0, None, ALU.add))
            step(dve.tensor_scalar(block_expert[:, n:n + 1], count_i[:, 0:1], 1, None, ALU.arith_shift_right))
            step(dve.tensor_scalar(block_expert[:, n + 1:n + 2], block_expert[:, n:n + 1], -2.0, BLOCKS - 2.0, ALU.mult, ALU.add))

        @block.scalar
        def _(act):
            act.wait_ge(done, at["group_gap"])
            act.activation(tmp4[:], tmp4[:], ACT.Exp).then_inc(exp_done, 1)
            act.wait_ge(done, at["best_gap"])
            act.activation(gap[:], gap[:], ACT.Sigmoid).then_inc(weight_done, 1)

        @block.tensor
        def _(pe):
            pe.wait_ge(done, at["counted"])
            pe.matmul(rank[:], const["before"][:], either[:].rearrange("p t e -> p (t e)"), start=True, stop=False)
            pe.matmul(rank[:], const["ones"][:], earlier[:, 0:T].rearrange("p t e -> p (t e)"), start=False, stop=True)
            pe.matmul(total[:, 0:NE], const["ones"][:], earlier[:, T], start=True, stop=True).then_inc(ranked, 1)

        @block.gpsimd
        def _(pool):
            pool.wait_ge(done, at["zero_rows"])
            pool.dma_start(slot_row_dram.rearrange("(p n) a -> p (n a)", p=P), zero_rows[:]).then_inc(zero_stored, 16)
            pool.wait_ge(zero_stored, 16)
            pool.wait_ge(done, at["slots"])
            for j in range(2):
                for t in range(T):
                    pool.indirect_dma_start(slot_row_dram, bass.IndirectOffsetOnAxis(ap=slot[:, j, t:t + 1], axis=0),
                                            const["rows"][:, t:t + 1], None).then_inc(scattered, 16)
            pool.wait_ge(scattered, 16 * 2 * T)


def experts_phase(nc, ins, const, mods, block_expert, slot_row_dram, h2_dram, y_dram):
    ZERO_COLS = 256
    with ExitStack() as stack:
        s = Scope(nc, stack, "moe")
        wg, wu = s.sb("wg", [P, 2, KD, F]), s.sb("wu", [P, 2, KD, F])
        wd = s.sb("wd", [P, 2, KF, D])
        row = [s.sb(f"row{u}", [P, 1], U32) for u in range(2)]
        h = [s.sb(f"h{u}", [P, D]) for u in range(2)]
        hT = [s.sb(f"hT{u}", [P, KD, P]) for u in range(2)]
        sig, gated, act_h = s.sb("sig", [P, F]), s.sb("gated", [P, F]), s.sb("act_h", [P, F])
        act_hT = s.sb("act_hT", [P, KF, P])
        y = s.sb("y", [P, 2, D])
        zero = s.sb("zero", [P, ZERO_COLS])
        gu = s.ps("gu", [P, 2, BANK])
        turned = s.ps("turned", [P, KD * P])
        turned2 = s.ps("turned2", [P, BANK])
        down = s.ps("down", [P, D])
        row_loaded, h_loaded = s.sems("row_loaded", 2), s.sems("h_loaded", 2)
        gu_loaded, d_loaded, stored = s.sems("gu_loaded", 2), s.sems("d_loaded", 2), s.sems("stored", 2)
        turn_done, hT_done, gu_done, sig_done = s.sem("turn_done"), s.sem("hT_done"), s.sem("gu_done"), s.sem("sig_done")
        gated_done, act_done = s.sem("gated_done"), s.sem("act_done")
        turn2_done, act_hT_done, down_done, y_done = s.sem("turn2_done"), s.sem("act_hT_done"), s.sem("down_done"), s.sem("y_done")
        zero_set, zero_stored = s.sem("zero_set"), s.sem("zero_stored")
        w_gate = ins["w_exp_gate"][0].rearrange("e (p k) n -> e p k n", k=KD)
        w_up = ins["w_exp_up"][0].rearrange("e (p k) n -> e p k n", k=KD)
        w_down = ins["w_exp_down"][0].rearrange("e (p k) n -> e p k n", k=KF)
        block = stack.enter_context(nc.Block())

        def all_blocks(eng, body):
            pairs = eng.value_load(block_expert[0:1, BLOCKS:BLOCKS + 1], min_val=SEQ // P - 1, max_val=BLOCKS // 2 - 1)
            body(0, 0, 0, True, False)
            with eng.Fori(0, pairs) as j:
                body(2 * j + 1, 1, j, False, False)
                body(2 * j + 2, 0, j + 1, False, False)
            body(2 * pairs + 1, 1, pairs, False, True)
            return pairs

        @block.sync
        def _(sp):
            def load(n, u, i, first, last):
                e = sp.value_load(block_expert[0:1, ds(n, 1)], min_val=0, max_val=NE - 1)
                sp.wait_ge(gu_done, n + 1)
                for w, src in ((wg, w_gate), (wu, w_up)):
                    sp.dma_start(w[:, u], src[ds(e, 1)].rearrange("e p k n -> (e p) k n")).then_inc(gu_loaded[u], 16)
                sp.wait_ge(down_done, n + 1)
                sp.dma_start(wd[:, u], w_down[ds(e, 1)].rearrange("e p k n -> (e p) k n")).then_inc(d_loaded[u], 16)

            all_blocks(sp, load)
            sp.wait_ge(zero_set, 1)
            idle = sp.value_load(block_expert[0:1, BLOCKS + 1:BLOCKS + 2], min_val=0, max_val=BLOCKS - 2 * SEQ // P)
            with sp.Fori(0, idle + 1) as n:
                sp.dma_start(y_dram[ds((BLOCKS - n) * P, P), :].rearrange("p (r n) -> p r n", n=ZERO_COLS),
                             zero[:].unsqueeze(1).to_broadcast([P, D // ZERO_COLS, ZERO_COLS])).then_inc(zero_stored, 16)
            sp.wait_ge(zero_stored, 16 * idle + 16)
            sp.nop(nofuse=True)

        @block.gpsimd
        def _(pool):
            def gather(n, u, i, first, last):
                pool.wait_ge(turn_done, n + 1)
                pool.dma_start(row[u][:], slot_row_dram[ds(n * P, P)]).then_inc(row_loaded[u], 16)
                pool.wait_ge(row_loaded[u], 16 * i + 16)
                pool.nop(nofuse=True)
                pool.indirect_dma_start(h[u][:], None, h2_dram, bass.IndirectOffsetOnAxis(ap=row[u][:], axis=0)).then_inc(h_loaded[u], 16)

            all_blocks(pool, gather)

        @block.tensor
        def _(pe):
            def turn(n, u, i):
                pe.wait_ge(h_loaded[u], 16 * i + 16)
                pe.wait_ge(hT_done, n + 1)
                for k in range(KD):
                    mm = pe.transpose(turned[:, k * P:(k + 1) * P], h[u][:].rearrange("p (c k) -> p k c", k=KD)[:, k],
                                      const["ident"][:])
                mm.then_inc(turn_done, 1)

            def gate_up(n, u, i):
                pe.wait_ge(hT_done, n + 2)
                pe.wait_ge(gu_loaded[u], 32 * i + 32)
                pe.wait_ge(act_done, n + 1)
                for j, w in enumerate((wg, wu)):
                    for k in range(KD):
                        mm = pe.matmul(gu[:, j], hT[u][:, k], w[:, u, k], start=(k == 0), stop=(k == KD - 1))
                mm.then_inc(gu_done, 1)

            def turn_hidden(n):
                pe.wait_ge(act_done, n + 2)
                pe.wait_ge(act_hT_done, n + 1)
                for k in range(KF):
                    mm = pe.transpose(turned2[:, k * P:(k + 1) * P], act_h[:].rearrange("p (f k) -> p k f", k=KF)[:, k],
                                      const["ident"][:])
                mm.then_inc(turn2_done, 1)

            def down_product(n, u, i):
                pe.wait_ge(act_hT_done, n + 2)
                pe.wait_ge(d_loaded[u], 16 * i + 16)
                pe.wait_ge(y_done, n + 1)
                for c in range(D // BANK):
                    for k in range(KF):
                        mm = pe.matmul(down[:, c * BANK:(c + 1) * BANK], act_hT[:, k], wd[:, u, k, c * BANK:(c + 1) * BANK],
                                       start=(k == 0), stop=(k == KF - 1))
                mm.then_inc(down_done, 1)

            def work(n, u, i, first, last):
                gate_up(n, u, i)
                if not first:
                    turn_hidden(n - 1)
                if not last:
                    turn(n + 1, 1 - u, i + u)
                if not first:
                    down_product(n - 1, 1 - u, i - 1 + u)

            pe.sem_inc(turn_done, 2)
            pe.sem_inc(gu_done, 2)
            pe.sem_inc(down_done, 2)
            turn(0, 0, 0)
            pairs = all_blocks(pe, work)
            turn_hidden(2 * pairs + 1)
            down_product(2 * pairs + 1, 1, pairs)

        @block.scalar
        def _(act):
            def copy_hT(n, u):
                act.wait_ge(turn_done, n + 3)
                act.wait_ge(gu_done, n + 1)
                act.copy(hT[u][:].rearrange("p k t -> p (k t)"), turned[:]).then_inc(hT_done, 1)

            def store(n, u):
                act.wait_ge(y_done, n + 2)
                act.dma_start(y_dram[ds(n * P, P), :], y[:, u]).then_inc(stored[u], 16)

            def work(n, u, i, first, last):
                act.wait_ge(gu_done, n + 3)
                act.wait_ge(gated_done, n + 1)
                act.activation(sig[:], gu[:, 0], ACT.Sigmoid).then_inc(sig_done, 1)
                if not last:
                    copy_hT(n + 1, 1 - u)
                if not first:
                    store(n - 1, 1 - u)

            act.sem_inc(hT_done, 1)
            for u in range(2):
                act.sem_inc(stored[u], 16)
            copy_hT(0, 0)
            pairs = all_blocks(act, work)
            store(2 * pairs + 1, 1)
            for u in range(2):
                act.wait_ge(stored[u], 16 * pairs + 32)
            act.nop(nofuse=True)

        @block.vector
        def _(dve):
            def copy_act_hT(n):
                dve.wait_ge(turn2_done, n + 1)
                dve.wait_ge(down_done, n + 2)
                dve.tensor_copy(act_hT[:].rearrange("p k t -> p (k t)"), turned2[:]).then_inc(act_hT_done, 1)

            def take(n, u, i):
                dve.wait_ge(down_done, n + 3)
                dve.wait_ge(stored[u], 16 * i + 16)
                dve.tensor_tensor(y[:, u], down[:], mods[:, 5 * D:6 * D], ALU.mult).then_inc(y_done, 1)

            def work(n, u, i, first, last):
                if not first:
                    copy_act_hT(n - 1)
                dve.wait_ge(sig_done, n + 1)
                dve.tensor_tensor(gated[:], sig[:], gu[:, 0], ALU.mult).then_inc(gated_done, 1)
                dve.wait_ge(gated_done, n + 2)
                dve.tensor_tensor(act_h[:], gated[:], gu[:, 1], ALU.mult).then_inc(act_done, 1)
                if not first:
                    take(n - 1, 1 - u, i - 1 + u)

            dve.memset(zero[:], 0.0).then_inc(zero_set, 1)
            dve.sem_inc(gated_done, 1)
            dve.sem_inc(act_done, 1)
            dve.sem_inc(act_hT_done, 1)
            dve.sem_inc(y_done, 1)
            pairs = all_blocks(dve, work)
            copy_act_hT(2 * pairs + 1)
            take(2 * pairs + 1, 1, pairs)


def final_phase(nc, ins, const, weight, slot, x2_dram, y_dram, out):
    with ExitStack() as stack:
        s = Scope(nc, stack, "fin")
        B = 3
        ya = [s.sb(f"ya{u}", [P, D]) for u in range(B)]
        yb = [s.sb(f"yb{u}", [P, D]) for u in range(B)]
        x, res = s.sb("x", [P, B, D]), s.sb("res", [P, B, D])
        g, junk = s.sb("g", [P, D]), s.sb("junk", [P, D])
        ssq, rms, rstd = s.sb("ssq", [P, TILES]), s.sb("rms", [P, TILES]), s.sb("rstd", [P, TILES])
        x_loaded, y_loaded, g_loaded, stored = s.sems("x_loaded", B), s.sems("y_loaded", B), s.sem("g_loaded"), s.sems("stored", B)
        first_done, sum_done, x3_done, ssq_done = s.sem("first_done"), s.sem("sum_done"), s.sem("x3_done"), s.sem("ssq_done")
        rms_done, rstd_done, res_done = s.sem("rms_done"), s.sem("rstd_done"), s.sem("res_done")
        block = stack.enter_context(nc.Block())

        @block.gpsimd
        def _(pool):
            for t in range(TILES):
                if t >= B:
                    pool.wait_ge(x3_done, t - B + 1)
                for j, y in enumerate((ya, yb)):
                    pool.indirect_dma_start(y[t % B][:], None, y_dram,
                                            bass.IndirectOffsetOnAxis(ap=slot[:, j, t:t + 1], axis=0)).then_inc(y_loaded[t % B], 16)

        @block.sync
        def _(sp):
            sp.dma_start(g[:], ins["norm_f_g"].unsqueeze(0).partition_broadcast(P)).then_inc(g_loaded, 16)
            for t in range(TILES):
                if t >= B:
                    sp.wait_ge(res_done, t - B + 1)
                    sp.dma_start(out[0, (t - B) * P:(t - B + 1) * P, :], res[:, t % B]).then_inc(stored[t % B], 16)
                sp.dma_start(x[:, t % B], x2_dram[t * P:(t + 1) * P, :]).then_inc(x_loaded[t % B], 16)
            for t in range(TILES - B, TILES):
                sp.wait_ge(res_done, t + 1)
                sp.dma_start(out[0, t * P:(t + 1) * P, :], res[:, t % B]).then_inc(stored[t % B], 16)
            for u in range(B):
                sp.wait_ge(stored[u], 16 * len(range(u, TILES, B)))

        @block.scalar
        def _(act):
            def first(t):
                act.wait_ge(y_loaded[t % B], 32 * (t // B + 1))
                act.mul(ya[t % B][:], ya[t % B][:], weight[:, 0, t:t + 1]).then_inc(first_done, 1)

            first(0)
            for t in range(TILES):
                if t + 1 < TILES:
                    first(t + 1)
                act.wait_ge(x3_done, t + 1)
                act.activation(junk[:], x[:, t % B], ACT.Square, accum_out=ssq[:, t:t + 1]).then_inc(ssq_done, 1)
                act.wait_ge(ssq_done, t + 1)
                act.activation(rms[:, t:t + 1], ssq[:, t:t + 1], ACT.Sqrt, bias=const["eps"][:],
                               scale=1.0 / D).then_inc(rms_done, 1)

        @block.vector
        def _(dve):
            def combine(t):
                u = t % B
                dve.wait_ge(first_done, t + 1)
                dve.scalar_tensor_tensor(yb[u][:], yb[u][:], weight[:, 1, t:t + 1], ya[u][:], ALU.mult, ALU.add).then_inc(sum_done, 1)
                dve.wait_ge(sum_done, t + 1)
                dve.wait_ge(x_loaded[u], 16 * (t // B + 1))
                dve.tensor_tensor(x[:, u], x[:, u], yb[u][:], ALU.add).then_inc(x3_done, 1)

            def normalise(t):
                u = t % B
                dve.wait_ge(rms_done, t + 1)
                dve.reciprocal(rstd[:, t:t + 1], rms[:, t:t + 1]).then_inc(rstd_done, 1)
                dve.wait_ge(rstd_done, t + 1)
                if t >= B:
                    dve.wait_ge(stored[u], 16 * (t // B))
                dve.scalar_tensor_tensor(res[:, u], x[:, u], rstd[:, t:t + 1], g[:], ALU.mult, ALU.mult).then_inc(res_done, 1)

            dve.wait_ge(g_loaded, 16)
            combine(0)
            for t in range(TILES):
                if t + 1 < TILES:
                    combine(t + 1)
                normalise(t)


def hybrid_layer_kernel(nc, ins, out):
    o_dram = nc.dram_tensor("o_rows", [SEQ, SBW], F32, kind="Internal").ap()
    opT_dram = nc.dram_tensor("opT_rows", [POOLW, SEQ], F32, kind="Internal").ap()
    x2_dram = nc.dram_tensor("x2_rows", [SEQ, D], F32, kind="Internal").ap()
    h2_dram = nc.dram_tensor("h2_rows", [SEQ, D], F32, kind="Internal").ap()
    y_dram = nc.dram_tensor("y_rows", [(BLOCKS + 1) * P, D], F32, kind="Internal").ap()
    slot_row_dram = nc.dram_tensor("slot_rows", [SLOTS, 1], U32, kind="Internal").ap()
    with ExitStack() as stack:
        s = Scope(nc, stack, "all")
        const = {
            "ident": s.sb("ident", [P, P]), "step": s.sb("step", [P, P]), "corner": s.sb("corner", [P, P]),
            "before": s.sb("before", [P, P]), "ones": s.sb("ones", [P, P]), "causal": s.sb("causal", [P, BANK]),
            "eps": s.sb("eps", [P, 1]), "iota": s.sb("iota", [P, 64]), "rows": s.sb("rows", [P, TILES], U32),
        }
        mods = s.sb("mods", [P, 6 * D])
        logits = s.sb("logits", [P, TILES, EG + NE])
        weight, slot = s.sb("weight", [P, 2, TILES]), s.sb("slot", [P, 2, TILES], U32)
        block_expert = s.sb("block_expert", [P, BLOCKS + 2], I32)
        constants_phase(nc, const)
        modulation_phase(nc, ins, mods)
        with nc.sbuf_tensor("hT", [P, KD, SEQ], F32) as hT:
            norm1_phase(nc, ins, const, mods, hT)
            attention_phase(nc, ins, const, hT, o_dram)
            pool_phase(nc, ins, const, hT, opT_dram)
            merge_phase(nc, ins, const, mods, hT, o_dram, opT_dram, x2_dram)
        route_phase(nc, ins, const, mods, logits, x2_dram, h2_dram)
        dispatch_phase(nc, const, logits, weight, slot, block_expert, slot_row_dram)
        experts_phase(nc, ins, const, mods, block_expert, slot_row_dram, h2_dram, y_dram)
        final_phase(nc, ins, const, weight, slot, x2_dram, y_dram, out)


_INS = ["x", "c", "norm1_g", "norm2_g", "w_ada", "b_ada", "w_in", "pool_w", "pool_scale", "w_branch_sb",
        "w_branch_pool", "w_out", "w_route_group", "b_route_group", "w_route_expert", "b_route_expert",
        "w_exp_gate", "w_exp_up", "w_exp_down", "norm_f_g"]


def kernel(**inputs):
    import numpy as np
    import concourse.bacc as bacc
    from concourse.bass_utils import run_bass_kernel_spmd

    nc = bacc.Bacc("TRN2", target_bir_lowering=False, num_devices=1)
    arrays, ins = {}, {}
    for name in _INS:
        a = np.asarray(inputs[name])
        if name == "x":
            a = a[:, ::-1]
        a = np.ascontiguousarray(a)
        arrays[f"in_{name}"] = a
        ins[name] = nc.dram_tensor(f"in_{name}", a.shape, mybir.dt.from_np(a.dtype), kind="ExternalInput").ap()
    out = nc.dram_tensor("out_rows", (1, SEQ, D), F32, kind="ExternalOutput").ap()
    hybrid_layer_kernel(nc, ins, out)
    result = run_bass_kernel_spmd(nc, [arrays], core_ids=[0])
    return np.ascontiguousarray(result.results[0]["out_rows"][:, ::-1])
```

```python
from contextlib import ExitStack

import concourse.bass as bass
from concourse import mybir

ALU = mybir.AluOpType
ACT = mybir.ActivationFunctionType
AX_X = mybir.AxisListType.X
F32 = mybir.dt.float32
I32 = mybir.dt.int32
U32 = mybir.dt.uint32
F32R = mybir.dt.float32r
ds = bass.ds

P = 128
SEQ, D = 2048, 1024
KD = D // P
TILES = SEQ // P
BANK = 512
HD = 64
SBW = D // 2
PAIRS = SBW // P
POOLW = D // 2
GROUPS = 4
WINDOWS = (2, 4, 8, 16)
PAD = 16
EPS = 1e-6
EG, EPG = 4, 8
NE = EG * EPG
F = D // 2
KF = F // P
BLOCKS = 2 * SEQ // P + NE
SLOTS = (BLOCKS + 1) * P
K_OFF, V_OFF, P_OFF, GS_OFF, GP_OFF = SBW, 2 * SBW, 3 * SBW, 3 * SBW + POOLW, 3 * SBW + POOLW + D


class Scope:

    numbers = []

    def __init__(self, nc, stack, tag):
        self.nc, self.stack, self.tag = nc, stack, tag

    def sb(self, name, shape, dt=F32):
        return self.stack.enter_context(self.nc.sbuf_tensor(f"{self.tag}_{name}", shape, dt))

    def ps(self, name, shape, dt=F32):
        return self.stack.enter_context(self.nc.psum_tensor(f"{self.tag}_{name}", shape, dt))

    def sem(self, name):
        handle = self.stack.enter_context(self.nc.semaphore(f"{self.tag}_{name}"))
        self.numbers.append(handle.num)
        return handle

    def sems(self, name, n):
        return [self.sem(f"{name}{k}") for k in range(n)]


def clear_phase(nc):
    numbers = sorted(Scope.numbers)
    first, end = numbers[0], numbers[-1] + 1
    assert numbers == list(range(first, end))
    with nc.Block() as block:
        @block.gpsimd
        def _(pool):
            pool.sem_clear(range(first, end))


def constants_phase(nc, const):
    with ExitStack() as stack:
        s = Scope(nc, stack, "cst")
        filled, cut, ints, floats = s.sem("filled"), s.sem("cut"), s.sem("ints"), s.sem("floats")
        iota_i = s.sb("iota_i", [P, 64], I32)
        block = stack.enter_context(nc.Block())

        @block.gpsimd
        def _(pool):
            pool.memset(const["ident"][:], 0.0).then_inc(filled, 1)
            pool.memset(const["step"][:], 0.0).then_inc(filled, 1)
            pool.memset(const["corner"][:], 0.0).then_inc(filled, 1)
            pool.memset(const["before"][:], 1.0).then_inc(filled, 1)
            pool.memset(const["ones"][:], 1.0).then_inc(filled, 1)
            pool.memset(const["causal"][:], 0.0).then_inc(filled, 1)
            pool.memset(const["eps"][:], EPS).then_inc(filled, 1)
            pool.wait_ge(filled, 7)
            pool.affine_select(out=const["ident"][:], in_=const["ident"][:], compare_op=ALU.not_equal,
                               fill=1.0, base=0, pattern=[[-1, P]], channel_multiplier=1).then_inc(cut, 1)
            pool.affine_select(out=const["step"][:], in_=const["step"][:], compare_op=ALU.not_equal,
                               fill=-1.0, base=0, pattern=[[-1, P]], channel_multiplier=1).then_inc(cut, 1)
            pool.wait_ge(cut, 2)
            pool.affine_select(out=const["step"][:], in_=const["step"][:], compare_op=ALU.not_equal,
                               fill=1.0, base=-1, pattern=[[-1, P]], channel_multiplier=1).then_inc(cut, 1)
            pool.affine_select(out=const["corner"][:], in_=const["corner"][:], compare_op=ALU.not_equal,
                               fill=1.0, base=P - 1, pattern=[[-1, P]], channel_multiplier=P).then_inc(cut, 1)
            pool.affine_select(out=const["before"][:], in_=const["before"][:], compare_op=ALU.is_gt,
                               fill=0.0, base=0, pattern=[[1, P]], channel_multiplier=-1).then_inc(cut, 1)
            pool.affine_select(out=const["causal"][:, 0:P], in_=const["causal"][:, 0:P],
                               compare_op=ALU.is_gt, fill=1.0, base=0, pattern=[[1, P]],
                               channel_multiplier=-1).then_inc(cut, 1)
            pool.iota(iota_i[:], [[1, 64]], base=0, channel_multiplier=0).then_inc(ints, 1)
            pool.iota(const["rows"][:], [[P, TILES]], base=0, channel_multiplier=1).then_inc(ints, 1)
            pool.wait_ge(ints, 2)
            pool.tensor_copy(const["iota"][:], iota_i[:]).then_inc(floats, 1)
            pool.wait_ge(cut, 6)
            pool.wait_ge(floats, 1)


def modulation_phase(nc, ins, mod1, mod2, gate2):
    SLOTS_W, N = 3, 6 * D // BANK
    with ExitStack() as stack:
        s = Scope(nc, stack, "ada")
        w = s.sb("w", [P, SLOTS_W, KD, BANK])
        c_col, c_sig, c_act = s.sb("c_col", [P, KD]), s.sb("c_sig", [P, KD]), s.sb("c_act", [P, KD])
        c_wide = s.sb("c_wide", [P, KD, P])
        ones = s.sb("ones", [P, P])
        g = s.sb("g", [P, 2, D])
        out = s.ps("out", [P, SLOTS_W, BANK])
        w_loaded = s.sems("w_loaded", SLOTS_W)
        c_loaded, b_loaded, g_loaded = s.sem("c_loaded"), s.sem("b_loaded"), s.sem("g_loaded")
        ones_set, sig_done, act_done, wide_done = s.sem("ones_set"), s.sem("sig_done"), s.sem("act_done"), s.sem("wide_done")
        product_done, added = s.sem("product_done"), s.sem("added")
        w_ada = ins["w_ada"][0].rearrange("(p k) n -> p k n", k=KD)
        block = stack.enter_context(nc.Block())

        @block.sync
        def _(sp):
            sp.dma_start(c_col[:], ins["c"][0].rearrange("(p k) -> p k", k=KD)).then_inc(c_loaded, 16)
            sp.dma_start(mod1[:], ins["b_ada"][0:1, 0:2 * D].partition_broadcast(P)).then_inc(b_loaded, 16)
            sp.dma_start(mod2[:], ins["b_ada"][0:1, 2 * D:5 * D].partition_broadcast(P)).then_inc(b_loaded, 16)
            sp.dma_start(gate2[:], ins["b_ada"][0:1, 5 * D:].partition_broadcast(P)).then_inc(b_loaded, 16)
            with sp.Fori(0, N // SLOTS_W) as i:
                for u in range(SLOTS_W):
                    sp.wait_ge(product_done, i * SLOTS_W + u + 1)
                    sp.dma_start(w[:, u], w_ada[:, :, ds(i * (SLOTS_W * BANK) + u * BANK, BANK)]).then_inc(w_loaded[u], 16)

        @block.scalar
        def _(act):
            act.dma_start(g[:, 0], ins["norm1_g"][0:1].partition_broadcast(P)).then_inc(g_loaded, 16)
            act.dma_start(g[:, 1], ins["norm2_g"][0:1].partition_broadcast(P)).then_inc(g_loaded, 16)
            act.wait_ge(c_loaded, 16)
            act.activation(c_sig[:], c_col[:], ACT.Sigmoid).then_inc(sig_done, 1)

        @block.tensor
        def _(pe):
            pe.sem_inc(product_done, SLOTS_W)
            pe.wait_ge(wide_done, KD)
            with pe.Fori(0, N // SLOTS_W) as i:
                for u in range(SLOTS_W):
                    pe.wait_ge(w_loaded[u], i * 16 + 16)
                    pe.wait_ge(added, i * SLOTS_W + u + 1)
                    for k in range(KD):
                        mm = pe.matmul(out[:, u], c_wide[:, k], w[:, u, k], start=(k == 0), stop=(k == KD - 1))
                    mm.then_inc(product_done, 1)

        @block.vector
        def _(dve):
            dve.sem_inc(added, SLOTS_W)
            dve.memset(ones[:], 1.0).then_inc(ones_set, 1)
            dve.wait_ge(sig_done, 1)
            dve.tensor_tensor(c_act[:], c_col[:], c_sig[:], ALU.mult).then_inc(act_done, 1)
            dve.wait_ge(ones_set, 1)
            dve.wait_ge(act_done, 1)
            for k in range(KD):
                dve.tensor_scalar(c_wide[:, k], ones[:], c_act[:, k:k + 1], None, ALU.mult).then_inc(wide_done, 1)
            dve.wait_ge(b_loaded, 48)
            for n in range(N):
                dve.wait_ge(product_done, SLOTS_W + n + 1)
                out_row, at = (mod1, 0) if n * BANK < 2 * D else (mod2, 2 * D) if n * BANK < 5 * D else (gate2, 5 * D)
                part = out_row[:, n * BANK - at:(n + 1) * BANK - at]
                dve.tensor_tensor(part, part, out[:, n % SLOTS_W], ALU.add).then_inc(added, 1)
            dve.wait_ge(added, SLOTS_W + N)
            dve.wait_ge(g_loaded, 32)
            for j, scale in enumerate((mod1[:, D:2 * D], mod2[:, 2 * D:3 * D])):
                dve.scalar_tensor_tensor(scale, scale, 1.0, g[:, j], ALU.add, ALU.mult).then_inc(act_done, 1)
            dve.wait_ge(act_done, 3)


def norm1_phase(nc, ins, const, mod1, hT):
    with ExitStack() as stack:
        s = Scope(nc, stack, "n1")
        x, h = s.sb("x", [P, 2, D]), s.sb("h", [P, 2, D])
        junk = s.sb("junk", [P, D])
        ssq, rms, rstd = s.sb("ssq", [P, 2]), s.sb("rms", [P, 2]), s.sb("rstd", [P, 2])
        turned = s.ps("turned", [P, 2, KD * P])
        x_loaded = s.sems("x_loaded", 2)
        ssq_done, rms_done, rstd_done = s.sem("ssq_done"), s.sem("rms_done"), s.sem("rstd_done")
        scaled, turn_done, hT_done = s.sem("scaled"), s.sem("turn_done"), s.sem("hT_done")
        h_done = s.sem("h_done")
        shift, scale = mod1[:, 0:D], mod1[:, D:2 * D]
        block = stack.enter_context(nc.Block())

        @block.sync
        def _(sp):
            with sp.Fori(0, TILES // 2) as i:
                for u in range(2):
                    sp.wait_ge(scaled, 2 * i + u + 1)
                    sp.dma_start(x[:, u], ins["x"][0, ds(i * (2 * P) + u * P, P), :]).then_inc(x_loaded[u], 16)

        @block.scalar
        def _(act):
            def square(i, u):
                act.wait_ge(x_loaded[u], i * 16 + 16)
                act.activation(junk[:], x[:, u], ACT.Square, accum_out=ssq[:, u:u + 1]).then_inc(ssq_done, 1)
                act.wait_ge(ssq_done, 2 * i + u + 1)
                act.activation(rms[:, u:u + 1], ssq[:, u:u + 1], ACT.Sqrt, bias=const["eps"][:],
                               scale=1.0 / D).then_inc(rms_done, 1)

            def evacuate(i, u):
                act.wait_ge(turn_done, 2 * i + (u + 3))
                act.copy(hT[:, :, ds(i * (2 * P) + u * P, P)], turned[:, u].rearrange("p (k t) -> p k t", k=KD)).then_inc(hT_done, 1)

            act.sem_inc(hT_done, 2)
            square(0, 0)
            with act.Fori(0, TILES // 2 - 1) as i:
                square(i, 1)
                evacuate(i, 0)
                square(i + 1, 0)
                evacuate(i, 1)
            square(TILES // 2 - 1, 1)
            evacuate(TILES // 2 - 1, 0)
            evacuate(TILES // 2 - 1, 1)
            act.wait_ge(hT_done, 2 + TILES)

        @block.vector
        def _(dve):
            dve.sem_inc(scaled, 2)
            with dve.Fori(0, TILES // 2) as i:
                for u in range(2):
                    dve.wait_ge(rms_done, 2 * i + u + 1)
                    dve.reciprocal(rstd[:, u:u + 1], rms[:, u:u + 1]).then_inc(rstd_done, 1)
                    dve.wait_ge(rstd_done, 2 * i + u + 1)
                    dve.wait_ge(turn_done, 2 * i + u + 1)
                    dve.scalar_tensor_tensor(h[:, u], x[:, u], rstd[:, u:u + 1], scale, ALU.mult, ALU.mult).then_inc(scaled, 1)
                    dve.wait_ge(scaled, 2 * i + (u + 3))
                    dve.tensor_tensor(h[:, u], h[:, u], shift, ALU.add).then_inc(h_done, 1)

        @block.tensor
        def _(pe):
            pe.sem_inc(turn_done, 2)
            with pe.Fori(0, TILES // 2) as i:
                for u in range(2):
                    pe.wait_ge(h_done, 2 * i + u + 1)
                    pe.wait_ge(hT_done, 2 * i + u + 1)
                    for k in range(KD):
                        mm = pe.transpose(turned[:, u, k * P:(k + 1) * P], h[:, u, k * P:(k + 1) * P], const["ident"][:])
                    mm.then_inc(turn_done, 1)


def attention_phase(nc, ins, const, hT, o_dram):
    CHUNK = BANK // P
    steps = []
    for q in range(TILES):
        for k in range(q, TILES, CHUNK):
            steps.append((q, k, min(CHUNK, TILES - k), k == q, k + CHUNK >= TILES))
    N = len(steps)
    JOBS = 16
    W_JOBS = 12
    last_step = {q: n for n, (q, _, _, _, last) in enumerate(steps) if last}
    with ExitStack() as stack:
        s = Scope(nc, stack, "att")
        w = s.sb("w", [P, 3, KD, P])
        qT, kT = s.sb("qT", [P, SEQ]), s.sb("kT", [P, SEQ])
        v, dv = s.sb("v", [P, TILES + 1, P]), s.sb("dv", [P, TILES, P])
        stay = s.sb("stay", [P, 2, 2, BANK])
        prod = s.sb("prod", [P, 2, 2, BANK])
        prodT = [[s.sb(f"prodT{u}{h}", [P, BANK]) for h in range(2)] for u in range(2)]
        o = s.sb("o", [P, 2, P])
        z = s.ps("z", [P, 4, BANK])
        turned = s.ps("turned", [P, 2, BANK])
        acc = s.ps("acc", [P, 2, BANK])
        w_loaded, v_pad = s.sem("w_loaded"), s.sem("v_pad")
        proj_done, copied_act, copied_dve = s.sem("proj_done"), s.sem("copied_act"), s.sem("copied_dve")
        z_done, stay_done, prod_done = s.sem("z_done"), s.sem("stay_done"), s.sem("prod_done")
        turn_done, prodT_done, pv_done = s.sem("turn_done"), s.sem("prodT_done"), s.sem("pv_done")
        o_done, o_stored = s.sem("o_done"), s.sems("o_stored", 2)
        w_in = ins["w_in"][0].rearrange("(k p) n -> p k n", p=P)
        block = stack.enter_context(nc.Block())

        def at(g, n, h):
            return g * (2 * N) + (2 * n + h + 1)

        @block.gpsimd
        def _(pool):
            pool.memset(v[:, TILES], 0.0).then_inc(v_pad, 1)

        @block.tensor
        def _(pe):
            def bank_free(g, n):
                if n >= 4:
                    pe.wait_ge(copied_dve if n % 2 else copied_act, g * (JOBS // 2) + ((n - 4) // 2 + 1))

            pe.wait_ge(v_pad, 1)
            with pe.Fori(0, PAIRS) as g:
                pe.wait_ge(w_loaded, g * 48 + 48)
                for n in range(JOBS):
                    bank_free(g, n)
                    c = n % 4
                    if n < 8:
                        for k in range(KD):
                            mm = pe.matmul(z[:, c], w[:, n // 4, k], hT[:, k, c * BANK:(c + 1) * BANK],
                                           start=(k == 0), stop=(k == KD - 1))
                    elif n < 12:
                        for t in range(4):
                            at_t = (4 * c + t) * P
                            for k in range(KD):
                                mm = pe.matmul(z[:, c, t * P:(t + 1) * P], hT[:, k, at_t:at_t + P], w[:, 2, k],
                                               start=(k == 0), stop=(k == KD - 1))
                    else:
                        if n == 12:
                            pe.wait_ge(copied_act, g * (JOBS // 2) + 6)
                            pe.wait_ge(copied_dve, g * (JOBS // 2) + 6)
                        pe.matmul(z[:, c], const["step"][:], v[:, 4 * c:4 * c + 4].rearrange("p t n -> p (t n)"),
                                  start=True, stop=False)
                        mm = pe.matmul(z[:, c], const["corner"][:],
                                       v[:, 4 * c + 1:4 * c + 5].rearrange("p t n -> p (t n)"),
                                       start=False, stop=True)
                    mm.then_inc(proj_done, 1)
                pe.wait_ge(copied_act, g * (JOBS // 2) + JOBS // 2)
                pe.wait_ge(copied_dve, g * (JOBS // 2) + JOBS // 2)

                def scores(n):
                    q, k, m, _, _ = steps[n]
                    for h in range(2):
                        if n >= 2:
                            pe.wait_ge(stay_done, at(g, n - 2, h))
                        pe.matmul(z[:, 2 * (n % 2) + h, 0:m * P], qT[h * HD:(h + 1) * HD, q * P:(q + 1) * P],
                                  kT[h * HD:(h + 1) * HD, k * P:(k + m) * P], start=True, stop=True).then_inc(z_done, 1)

                def turn(n):
                    m = steps[n][2]
                    for h in range(2):
                        pe.wait_ge(prod_done, at(g, n, h))
                        if n >= 1:
                            pe.wait_ge(prodT_done, at(g, n - 1, h))
                        for b in range(m):
                            mm = pe.transpose(turned[:, h, b * P:(b + 1) * P], prod[:, h, n % 2, b * P:(b + 1) * P],
                                              const["ident"][:])
                        mm.then_inc(turn_done, 1)

                def weigh(n):
                    q, k, m, first, last = steps[n]
                    for h in range(2):
                        if first and q:
                            pe.wait_ge(o_done, g * TILES + q)
                        pe.wait_ge(prodT_done, at(g, n, h))
                        if first:
                            pe.matmul(acc[:, h, 0:HD], const["ones"][0:1, :], v[0:1, q, h * HD:(h + 1) * HD],
                                      start=True, stop=False)
                        for b in range(m):
                            mm = pe.matmul(acc[:, h, 0:HD], prodT[n % 2][h][:, b * P:(b + 1) * P],
                                           dv[:, k + b, h * HD:(h + 1) * HD], start=False, stop=(last and b == m - 1))
                        mm.then_inc(pv_done, 1)

                scores(0)
                for n in range(N):
                    if n + 1 < N:
                        scores(n + 1)
                    turn(n)
                    if n >= 1:
                        weigh(n - 1)
                weigh(N - 1)

        def copy_job(eng, copy, g, n):
            c = n % 4
            eng.wait_ge(proj_done, g * JOBS + (n + 1))
            if n < 8:
                out = (qT, kT)[n // 4][:, c * BANK:(c + 1) * BANK]
            else:
                out = (v, dv)[(n - 8) // 4][:, 4 * c:4 * c + 4].rearrange("p t n -> p (t n)")
            return copy(out, z[:, c])

        @block.scalar
        def _(act):
            with act.Fori(0, PAIRS) as g:
                for n in range(0, JOBS, 2):
                    copy_job(act, act.copy, g, n).then_inc(copied_act, 1)

                def stays(n):
                    m = steps[n][2]
                    for h in range(2):
                        act.wait_ge(z_done, at(g, n, h))
                        if n >= 2:
                            act.wait_ge(prod_done, at(g, n - 2, h))
                        act.activation(stay[:, h, n % 2, 0:m * P], z[:, 2 * (n % 2) + h, 0:m * P], ACT.Sigmoid,
                                       scale=-HD ** -0.5).then_inc(stay_done, 1)

                stays(0)
                for n in range(N):
                    if n + 1 < N:
                        stays(n + 1)
                    m = steps[n][2]
                    for h in range(2):
                        act.wait_ge(turn_done, at(g, n, h))
                        if n >= 2:
                            act.wait_ge(pv_done, at(g, n - 2, h))
                        act.copy(prodT[n % 2][h][:, 0:m * P], turned[:, h, 0:m * P]).then_inc(prodT_done, 1)

        @block.vector
        def _(dve):
            with dve.Fori(0, PAIRS) as g:
                for n in range(1, JOBS, 2):
                    copy_job(dve, dve.tensor_copy, g, n).then_inc(copied_dve, 1)

                def copy_o(q):
                    dve.wait_ge(pv_done, at(g, last_step[q], 1))
                    dve.wait_ge(o_stored[q % 2], g * (8 * TILES) + 16 * (q // 2 + 1))
                    dve.tensor_copy(o[:, q % 2].rearrange("p (h n) -> p h n", h=2), acc[:, :, 0:HD]).then_inc(o_done, 1)

                for n, (q, k, m, first, last) in enumerate(steps):
                    for h in range(2):
                        dve.wait_ge(stay_done, at(g, n, h))
                        if n >= 2:
                            dve.wait_ge(turn_done, at(g, n - 2, h))
                        start = 1.0
                        if n >= 1:
                            dve.wait_ge(prod_done, at(g, n - 1, h))
                        if not first:
                            start = prod[:, h, (n - 1) % 2, BANK - 1:BANK]
                        mask = const["causal"][:, 0:m * P] if first else const["causal"][:, P:P + 1].to_broadcast([P, m * P])
                        dve.tensor_tensor_scan(prod[:, h, n % 2, 0:m * P], stay[:, h, n % 2, 0:m * P], mask, start,
                                               ALU.mult, ALU.max).then_inc(prod_done, 1)
                    for q_done, n_done in last_step.items():
                        if n_done == n - 2:
                            copy_o(q_done)
                for q_done, n_done in last_step.items():
                    if n_done >= N - 2:
                        copy_o(q_done)

        @block.sync
        def _(sp):
            sp.sem_inc(o_stored[0], 16)
            sp.sem_inc(o_stored[1], 16)

            def load(g):
                for j, off in enumerate((0, K_OFF, V_OFF)):
                    sp.dma_start(w[:, j], w_in[:, :, ds(g * P + off, P)]).then_inc(w_loaded, 16)

            load(0)
            with sp.Fori(0, PAIRS) as g:
                sp.wait_ge(proj_done, g * JOBS + W_JOBS)
                sp.nop(nofuse=True)
                with sp.If(g < PAIRS - 1):
                    load(g + 1)
                for q in range(TILES):
                    sp.wait_ge(o_done, g * TILES + (q + 1))
                    sp.dma_start(o_dram[q * P:(q + 1) * P, ds(g * P, P)], o[:, q % 2]).then_inc(o_stored[q % 2], 16)
            for u in range(2):
                sp.wait_ge(o_stored[u], 16 + 8 * TILES * PAIRS)


def pool_phase(nc, ins, const, hT, opT_dram):
    L = SEQ + PAD
    CH = SEQ // BANK
    with ExitStack() as stack:
        s = Scope(nc, stack, "pool")
        w = s.sb("w", [P, 2, KD, P])
        w2 = s.sb("w2", [P, GROUPS, P])
        p_scale = s.sb("p_scale", [P, GROUPS])
        pT = s.sb("pT", [P, 2, L])
        sums = s.sb("sums", [P, 2, L])
        mean = s.sb("mean", [P, 2, SEQ])
        inv = s.sb("inv", [P, PAD])
        opT = s.sb("opT", [P, SEQ])
        proj, mapped = s.ps("proj", [P, 4, BANK]), s.ps("mapped", [P, 4, BANK])
        w_loaded, small_loaded, filled = s.sems("w_loaded", 2), s.sem("small_loaded"), s.sem("filled")
        proj_done, pT_done, dve_done = s.sem("proj_done"), s.sem("pT_done"), s.sem("dve_done")
        mean_done, map_done, opT_done, stored = s.sem("mean_done"), s.sem("map_done"), s.sem("opT_done"), s.sem("stored")
        w_in = ins["w_in"][0].rearrange("(k p) n -> p k n", p=P)
        block = stack.enter_context(nc.Block())

        @block.sync
        def _(sp):
            sp.dma_start(w2[:], ins["pool_w"][0].rearrange("g c n -> c g n")).then_inc(small_loaded, 16)
            sp.dma_start(p_scale[:], ins["pool_scale"][0].rearrange("(g p) -> p g", p=P), allow_slow_non_contiguous=True).then_inc(small_loaded, 16)
            for g in range(GROUPS):
                if g >= 2:
                    sp.wait_ge(proj_done, CH * (g - 1))
                sp.dma_start(w[:, g % 2], w_in[:, :, P_OFF + g * P:P_OFF + (g + 1) * P]).then_inc(w_loaded[g % 2], 16)
            for g in range(GROUPS):
                sp.wait_ge(opT_done, CH * (g + 1))
                sp.dma_start(opT_dram[g * P:(g + 1) * P, :], opT[:]).then_inc(stored, 16)
            sp.wait_ge(stored, 16 * GROUPS)

        @block.tensor
        def _(pe):
            def project(g):
                pe.wait_ge(w_loaded[g % 2], 16 * (g // 2 + 1))
                for c in range(CH):
                    if g:
                        pe.wait_ge(pT_done, CH * (g - 1) + c + 1)
                    for k in range(KD):
                        mm = pe.matmul(proj[:, c], w[:, g % 2, k], hT[:, k, c * BANK:(c + 1) * BANK],
                                       start=(k == 0), stop=(k == KD - 1))
                    mm.then_inc(proj_done, 1)

            def map_group(g):
                if g == 0:
                    pe.wait_ge(small_loaded, 32)
                pe.wait_ge(mean_done, g + 1)
                for c in range(CH):
                    if g:
                        pe.wait_ge(opT_done, CH * (g - 1) + c + 1)
                    pe.matmul(mapped[:, c], w2[:, g], mean[:, g % 2, c * BANK:(c + 1) * BANK],
                              start=True, stop=True).then_inc(map_done, 1)

            for g in range(GROUPS):
                project(g)
                if g:
                    map_group(g - 1)
            map_group(GROUPS - 1)

        @block.scalar
        def _(act):
            def take(g):
                for c in range(CH):
                    act.wait_ge(proj_done, CH * g + c + 1)
                    if g >= 2:
                        act.wait_ge(mean_done, g - 1)
                    act.copy(pT[:, g % 2, c * BANK:(c + 1) * BANK], proj[:, c]).then_inc(pT_done, 1)

            def finish(g):
                if g == 0:
                    act.wait_ge(small_loaded, 32)
                else:
                    act.wait_ge(stored, 16 * g)
                for c in range(CH):
                    act.wait_ge(map_done, CH * g + c + 1)
                    act.mul(opT[:, c * BANK:(c + 1) * BANK], mapped[:, c], p_scale[:, g:g + 1]).then_inc(opT_done, 1)

            for g in range(GROUPS):
                take(g)
                if g:
                    finish(g - 1)
            finish(GROUPS - 1)

        @block.gpsimd
        def _(pool):
            for b in (pT, sums):
                for u in range(2):
                    pool.memset(b[:, u, SEQ:L], 0.0).then_inc(filled, 1)
            for j in range(PAD):
                pool.memset(inv[:, j:j + 1], 1.0 / (PAD - j)).then_inc(filled, 1)

        @block.vector
        def _(dve):
            done = 0

            def chained(ins_):
                nonlocal done
                done += 1
                ins_.then_inc(dve_done, 1)
                dve.wait_ge(dve_done, done)

            dve.wait_ge(filled, 4 + PAD)
            for g, width in enumerate(WINDOWS):
                dve.wait_ge(pT_done, CH * (g + 1))
                p = pT[:, g % 2]
                src = p
                for level in range(g + 1):
                    out = sums[:, level % 2]
                    chained(dve.tensor_tensor(out[:, 0:SEQ], src[:, 0:SEQ], src[:, 1 << level:SEQ + (1 << level)], ALU.add))
                    src = out
                if g >= 2:
                    dve.wait_ge(map_done, CH * (g - 1))
                m, tail = mean[:, g % 2], width - 1
                chained(dve.scalar_tensor_tensor(m[:, 0:SEQ - tail], src[:, 0:SEQ - tail], 1.0 / width,
                                                 p[:, 0:SEQ - tail], ALU.mult, ALU.subtract))
                chained(dve.tensor_tensor(m[:, SEQ - tail:SEQ], src[:, SEQ - tail:SEQ], inv[:, PAD - tail:PAD], ALU.mult))
                dve.tensor_tensor(m[:, SEQ - tail:SEQ], m[:, SEQ - tail:SEQ], p[:, SEQ - tail:SEQ],
                                  ALU.subtract).then_inc(mean_done, 1)


def branches_phase(nc, ins, const, hT, o_dram, opT_dram, mT_dram):
    NB, TB, KS = SEQ // BANK, BANK // P, SBW // P
    UNITS = 2 * KD
    with ExitStack() as stack:
        s = Scope(nc, stack, "mix")
        PARTS = ("high", "low")
        raw_g, raw_b = s.sb("raw_g", [P, 2, KD, P]), s.sb("raw_b", [P, 2, KS, P])
        wg = [[s.sb(f"wg{j}_{part}", [P, KD, P], F32R) for part in PARTS] for j in range(2)]
        wb = [[s.sb(f"wb{j}_{part}", [P, KS, P], F32R) for part in PARTS] for j in range(2)]
        o, op = s.sb("o", [P, 2, SBW]), s.sb("op", [P, 2, BANK])
        hTb = [s.sb(f"hT_{part}", [P, KD, BANK], F32R) for part in PARTS]
        oT = [s.sb(f"oT_{part}", [P, KS, BANK], F32R) for part in PARTS]
        opT = [s.sb(f"opT_{part}", [P, KS, BANK], F32R) for part in PARTS]
        gate, part = s.sb("gate", [P, 2, BANK]), s.sb("part", [P, 2, BANK])
        mT = s.sb("mT", [P, BANK])
        gate_ps, branch_ps, turned = s.ps("gate_ps", [P, 2, BANK]), s.ps("branch_ps", [P, 2, BANK]), s.ps("turned", [P, 2, BANK])
        w_loaded, o_loaded, op_loaded, stored = s.sems("w_loaded", 2), s.sems("o_loaded", 2), s.sems("op_loaded", 2), s.sem("stored")
        w_high, wg_low, w_low = s.sem("w_high"), s.sem("wg_low"), s.sem("w_low")
        hT_high, hT_low, oT_high, oT_low = s.sem("hT_high"), s.sem("hT_low"), s.sem("oT_high"), s.sem("oT_low")
        opT_high, opT_low = s.sem("opT_high"), s.sem("opT_low")
        turn_done, gate_mm, branch_mm = s.sem("turn_done"), s.sem("gate_mm"), s.sem("branch_mm")
        gate_done, part_done, mT_done = s.sem("gate_done"), s.sem("part_done"), s.sem("mT_done")
        w_in = ins["w_in"][0].rearrange("(k p) n -> p k n", p=P)
        w_sb = ins["w_branch_sb"][0].rearrange("(k p) n -> p k n", p=P)
        w_pl = ins["w_branch_pool"][0].rearrange("(k p) n -> p k n", p=P)
        block = stack.enter_context(nc.Block())

        @block.sync
        def _(sp):
            with sp.Fori(0, NB) as b:
                with sp.Fori(0, KD) as d:
                    for j, (off, wbr) in enumerate(((GS_OFF, w_sb), (GP_OFF, w_pl))):
                        sp.wait_ge(w_low, b * UNITS + 2 * d + (j + 1))
                        sp.dma_start(raw_g[:, j], w_in[:, :, ds(d * P + off, P)]).then_inc(w_loaded[j], 16)
                        sp.dma_start(raw_b[:, j], wbr[:, :, ds(d * P, P)]).then_inc(w_loaded[j], 16)

        @block.gpsimd
        def _(pool):
            with pool.Fori(0, NB) as b:
                for t in range(TB):
                    pool.wait_ge(turn_done, b * TB + (t + 1))
                    pool.dma_start(o[:, t % 2], o_dram[ds(b * BANK + t * P, P), :]).then_inc(o_loaded[t % 2], 16)
                for k in range(KS):
                    pool.wait_ge(opT_low, b * KS + (k + 1))
                    pool.dma_start(op[:, k % 2], opT_dram[k * P:(k + 1) * P, ds(b * BANK, BANK)]).then_inc(op_loaded[k % 2], 16)

        @block.tensor
        def _(pe):
            def product(to, w, x, blocks, before=None):
                for k in range(blocks):
                    if before:
                        before(k)
                    pe.matmul(to, w[0][:, k], x[0][:, k], start=(k == 0), stop=False)
                    pe.matmul(to, w[0][:, k], x[1][:, k], start=False, stop=False)
                    mm = pe.matmul(to, w[1][:, k], x[0][:, k], start=False, stop=(k == blocks - 1))
                return mm

            def unit(b, d, j, first, between=None):
                n = b * UNITS + 2 * d + j
                pe.wait_ge(w_low, n + 3)
                pe.wait_ge(gate_done, n + 1)
                before = (lambda k: pe.wait_ge(hT_low, b * KD + (k + 1))) if first and j == 0 else None
                product(gate_ps[:, j], wg[j], hTb, KD, before).then_inc(gate_mm, 1)
                if between:
                    between(b)
                pe.wait_ge(part_done, n + 1)
                if first:
                    pe.wait_ge((oT_low, opT_low)[j], b * KS + (TB + (0, 2)[j]))
                product(branch_ps[:, j], wb[j], (oT, opT)[j], KS).then_inc(branch_mm, 1)

            pe.sem_inc(turn_done, 2)
            pe.sem_inc(branch_mm, 2)
            pe.sem_inc(gate_mm, 1)
            def turn(b):
                for t in range(TB):
                    pe.wait_ge(o_loaded[t % 2], b * (8 * TB) + 16 * (t // 2 + 1))
                    if t >= 2:
                        pe.wait_ge(oT_low, b * TB + (t - 1))
                    for k in range(KS):
                        mm = pe.transpose(turned[:, t % 2, k * P:(k + 1) * P], o[:, t % 2, k * P:(k + 1) * P], const["ident"][:])
                    mm.then_inc(turn_done, 1)

            with pe.Fori(0, NB) as b:
                unit(b, 0, 0, True, between=turn)
                unit(b, 0, 1, True)
                with pe.Fori(1, KD) as d:
                    for j in range(2):
                        unit(b, d, j, False)

        def all_units(eng, split_hT, start, unit, split, finish, hT_before):
            def tokens(b, more):
                start(b)
                with eng.Fori(0, KD - 1) as d:
                    for j in range(2):
                        unit(b, d, j)
                        split(b * UNITS + 2 * d + (j + 2), j, b * KD + d + 1)
                    finish(b, d)
                unit(b, KD - 1, 0)
                if not hT_before:
                    unit(b, KD - 1, 1)
                if more:
                    split_hT(b + 1)
                    split(b * UNITS + UNITS, 0, b * KD + KD)
                if hT_before:
                    unit(b, KD - 1, 1)
                if more:
                    split(b * UNITS + (UNITS + 1), 1, b * KD + KD)
                finish(b, KD - 1)

            split_hT(0)
            with eng.Fori(0, NB - 1) as b:
                tokens(b, True)
            tokens(NB - 1, False)

        def columns(b, k):
            return hT[:, k, b * BANK:(b + 1) * BANK] if isinstance(b, int) else hT[:, k, ds(b * BANK, BANK)]

        @block.scalar
        def _(act):
            def split(n, j, i):
                act.wait_ge(w_loaded[j], i * 32 + 32)
                act.wait_ge(branch_mm, n + 1)
                act.copy(wg[j][0][:], raw_g[:, j]).then_inc(w_high, 1)
                act.copy(wb[j][0][:], raw_b[:, j]).then_inc(w_high, 1)

            def split_hT(b):
                act.wait_ge(gate_mm, b * UNITS + 1)
                for k in range(KD):
                    act.copy(hTb[0][:, k], columns(b, k)).then_inc(hT_high, 1)

            def start(b):
                act.wait_ge(branch_mm, b * UNITS + 2)
                for t in range(TB):
                    act.wait_ge(turn_done, b * TB + (t + 3))
                    act.copy(oT[0][:, :, t * P:(t + 1) * P], turned[:, t % 2].rearrange("p (k t) -> p k t", k=KS)).then_inc(oT_high, 1)
                for k in range(KS):
                    act.wait_ge(op_loaded[k % 2], b * (8 * KS) + 16 * (k // 2 + 1))
                    act.copy(opT[0][:, k], op[:, k % 2]).then_inc(opT_high, 1)

            def unit(b, d, j):
                n = b * UNITS + 2 * d + j
                act.wait_ge(gate_mm, n + 2)
                act.wait_ge(part_done, n + 1)
                act.activation(gate[:, j], gate_ps[:, j], ACT.Sigmoid).then_inc(gate_done, 1)

            def finish(b, d):
                act.wait_ge(mT_done, b * KD + d + 2)
                act.dma_start(mT_dram[ds(d * P, P) if not isinstance(d, int) else slice(d * P, (d + 1) * P), ds(b * BANK, BANK)],
                              mT[:]).then_inc(stored, 16)

            act.sem_inc(stored, 16)
            act.sem_inc(gate_done, 2)
            for j in range(2):
                split(j, j, 0)
            all_units(act, split_hT, start, unit, split, finish, False)
            act.wait_ge(stored, 16 + 16 * KD * NB)

        @block.vector
        def _(dve):
            def low(out, source, high, done):
                dve.tensor_tensor(out, source, high.bitcast(F32), ALU.subtract).then_inc(done, 1)

            def split(n, j, i):
                dve.wait_ge(w_high, 2 * n + 1)
                dve.tensor_tensor(wg[j][1][:], raw_g[:, j], wg[j][0][:].bitcast(F32), ALU.subtract).then_inc(wg_low, 1)
                dve.wait_ge(w_high, 2 * n + 2)
                dve.wait_ge(wg_low, n + 1)
                dve.tensor_tensor(wb[j][1][:], raw_b[:, j], wb[j][0][:].bitcast(F32), ALU.subtract).then_inc(w_low, 1)

            def split_hT(b):
                for k in range(KD):
                    dve.wait_ge(hT_high, b * KD + (k + 1))
                    low(hTb[1][:, k], columns(b, k), hTb[0][:, k], hT_low)

            def start(b):
                for t in range(TB):
                    dve.wait_ge(oT_high, b * TB + (t + 1))
                    low(oT[1][:, :, t * P:(t + 1) * P], turned[:, t % 2].rearrange("p (k t) -> p k t", k=KS),
                        oT[0][:, :, t * P:(t + 1) * P], oT_low)
                for k in range(KS):
                    dve.wait_ge(opT_high, b * KS + (k + 1))
                    low(opT[1][:, k], op[:, k % 2], opT[0][:, k], opT_low)

            def unit(b, d, j):
                n = b * UNITS + 2 * d + j
                dve.wait_ge(gate_done, n + 3)
                dve.wait_ge(branch_mm, n + 3)
                dve.wait_ge(mT_done, b * KD + d + 1)
                dve.tensor_tensor(part[:, j], gate[:, j], branch_ps[:, j], ALU.mult).then_inc(part_done, 1)
                if j == 1:
                    dve.wait_ge(part_done, n + 3)
                    dve.wait_ge(stored, b * (16 * KD) + d * 16 + 16)
                    dve.tensor_tensor(mT[:], part[:, 0], part[:, 1], ALU.add).then_inc(mT_done, 1)

            dve.sem_inc(w_low, 2)
            dve.sem_inc(opT_low, 2)
            dve.sem_inc(part_done, 2)
            dve.sem_inc(mT_done, 1)
            for j in range(2):
                split(j, j, 0)
            all_units(dve, split_hT, start, unit, split, lambda b, d: None, True)


def output_phase(nc, ins, const, mod2, logits, mT_dram, x2_dram, h2_dram):
    with ExitStack() as stack:
        s = Scope(nc, stack, "out")
        PARTS = ("high", "low")
        raw_w = s.sb("raw_w", [P, 2, D])
        w = [s.sb(f"w_{part}", [P, KD, D], F32R) for part in PARTS]
        raw_m = s.sb("raw_m", [P, 2, KD, P])
        mT = [[s.sb(f"mT{u}_{part}", [P, KD, P], F32R) for part in PARTS] for u in range(2)]
        x, h, scaled_out = s.sb("x", [P, 2, D]), s.sb("h", [P, 2, D]), s.sb("scaled_out", [P, D])
        hT = [s.sb(f"hT{u}", [P, KD, P]) for u in range(2)]
        wr = s.sb("wr", [P, KD, EG + NE])
        bias = s.sb("bias", [P, EG + NE])
        junk = s.sb("junk", [P, D])
        ssq, rms, rstd = s.sb("ssq", [P, 2]), s.sb("rms", [P, 2]), s.sb("rstd", [P, 2])
        proj = s.ps("proj", [P, 2, D])
        turned = s.ps("turned", [P, KD * P])
        routed = s.ps("routed", [P, 2, BANK])
        w_loaded, m_loaded, x_loaded, wr_loaded = s.sems("w_loaded", 2), s.sems("m_loaded", 2), s.sems("x_loaded", 2), s.sem("wr_loaded")
        w_high, w_low, m_high, m_low = s.sem("w_high"), s.sem("w_low"), s.sem("m_high"), s.sem("m_low")
        x2_stored, h_stored = s.sems("x2_stored", 2), s.sems("h_stored", 2)
        proj_done, gate_done, x2_done = s.sem("proj_done"), s.sem("gate_done"), s.sem("x2_done")
        ssq_done, rms_done, rstd_done, h_done = s.sem("ssq_done"), s.sem("rms_done"), s.sem("rstd_done"), s.sem("h_done")
        normed, turn_done, hT_done, route_done, logits_done = (s.sem("normed"), s.sem("turn_done"), s.sem("hT_done"),
                                                               s.sem("route_done"), s.sem("logits_done"))
        gate1, shift, scale = mod2[:, 0:D], mod2[:, D:2 * D], mod2[:, 2 * D:3 * D]
        w_out = ins["w_out"][0].rearrange("(k p) n -> p k n", p=P)
        merged = mT_dram.rearrange("(k p) t -> p k t", p=P)
        block = stack.enter_context(nc.Block())

        @block.gpsimd
        def _(pool):
            def load(i, u):
                pool.wait_ge(m_low, 2 * i + (u + 1))
                pool.dma_start(raw_m[:, u], merged[:, :, ds(i * (2 * P) + u * P, P)]).then_inc(m_loaded[u], 16)
                pool.wait_ge(normed, 2 * i + (u + 1))
                pool.wait_ge(x2_stored[u], i * 16 + 16)
                pool.dma_start(x[:, u], ins["x"][0, ds(i * (2 * P) + u * P, P), :]).then_inc(x_loaded[u], 16)

            with pool.Fori(0, TILES // 2) as i:
                for u in range(2):
                    load(i, u)

        @block.sync
        def _(sp):
            for k in range(KD):
                if k >= 2:
                    sp.wait_ge(w_low, k - 1)
                sp.dma_start(raw_w[:, k % 2], w_out[:, k]).then_inc(w_loaded[k % 2], 16)
            sp.dma_start(wr[:, :, 0:EG], ins["w_route_group"][0].rearrange("(k p) n -> p k n", p=P)).then_inc(wr_loaded, 16)
            for g in range(EG):
                sp.dma_start(wr[:, :, EG + g * EPG:EG + (g + 1) * EPG],
                             ins["w_route_expert"][0, g].rearrange("(k p) n -> p k n", p=P)).then_inc(wr_loaded, 16)
            sp.dma_start(bias[:, 0:EG], ins["b_route_group"][0:1].partition_broadcast(P)).then_inc(wr_loaded, 16)
            sp.dma_start(bias[:, EG:], ins["b_route_expert"][0:1].rearrange("a g e -> a (g e)").partition_broadcast(P)).then_inc(wr_loaded, 16)
            for u in range(2):
                sp.sem_inc(x2_stored[u], 16)
                sp.sem_inc(h_stored[u], 16)
            with sp.Fori(0, TILES // 2) as i:
                for u in range(2):
                    sp.wait_ge(x2_done, 2 * i + (u + 2))
                    sp.dma_start(x2_dram[ds(i * (2 * P) + u * P, P), :], x[:, u]).then_inc(x2_stored[u], 16)
                    sp.wait_ge(h_done, 2 * i + (u + 1))
                    sp.dma_start(h2_dram[ds(i * (2 * P) + u * P, P), :], h[:, u]).then_inc(h_stored[u], 16)
            for u in range(2):
                sp.wait_ge(x2_stored[u], 16 + 8 * TILES)
                sp.wait_ge(h_stored[u], 16 + 8 * TILES)

        @block.tensor
        def _(pe):
            def project(i, u, first=False):
                pe.wait_ge(m_low, 2 * i + (u + 3))
                pe.wait_ge(gate_done, 2 * i + (u + 1))
                for k in range(KD):
                    if first:
                        pe.wait_ge(w_low, k + 1)
                    for a, b in ((0, 0), (0, 1), (1, 0)):
                        for c in range(D // BANK):
                            mm = pe.matmul(proj[:, u, c * BANK:(c + 1) * BANK], mT[u][a][:, k], w[b][:, k, c * BANK:(c + 1) * BANK],
                                           start=(k == 0 and a + b == 0), stop=(k == KD - 1 and a == 1))
                mm.then_inc(proj_done, 1)

            def turn(i, u):
                pe.wait_ge(h_done, 2 * i + (u + 1))
                pe.wait_ge(hT_done, 2 * i + (u + 1))
                for k in range(KD):
                    mm = pe.transpose(turned[:, k * P:(k + 1) * P], h[:, u, k * P:(k + 1) * P], const["ident"][:])
                mm.then_inc(turn_done, 1)

            def route(i, u):
                pe.wait_ge(hT_done, 2 * i + (u + 2))
                pe.wait_ge(logits_done, 2 * i + (u + 1))
                for k in range(KD):
                    mm = pe.matmul(routed[:, u, 0:EG + NE], hT[u][:, k], wr[:, k], start=(k == 0), stop=(k == KD - 1))
                mm.then_inc(route_done, 1)

            for sem in (proj_done, turn_done, route_done):
                pe.sem_inc(sem, 2)
            project(0, 0, first=True)
            project(0, 1)
            turn(0, 0)
            pe.wait_ge(wr_loaded, 16 * (EG + 3))
            with pe.Fori(1, TILES // 2) as i:
                project(i, 0)
                turn(i - 1, 1)
                route(i - 1, 0)
                project(i, 1)
                turn(i, 0)
                route(i - 1, 1)
            turn(TILES // 2 - 1, 1)
            route(TILES // 2 - 1, 0)
            route(TILES // 2 - 1, 1)

        @block.scalar
        def _(act):
            def split(i, u):
                act.wait_ge(m_loaded[u], i * 16 + 16)
                act.wait_ge(proj_done, 2 * i + (u + 1))
                act.copy(mT[u][0][:], raw_m[:, u]).then_inc(m_high, 1)

            def square(i, u):
                act.wait_ge(x2_done, 2 * i + (u + 2))
                act.activation(junk[:], x[:, u], ACT.Square, accum_out=ssq[:, u:u + 1]).then_inc(ssq_done, 1)
                act.wait_ge(ssq_done, 2 * i + (u + 1))
                act.activation(rms[:, u:u + 1], ssq[:, u:u + 1], ACT.Sqrt, bias=const["eps"][:],
                               scale=1.0 / D).then_inc(rms_done, 1)

            def copy_hT(i, u):
                act.wait_ge(turn_done, 2 * i + (u + 3))
                act.wait_ge(route_done, 2 * i + (u + 1))
                act.copy(hT[u][:].rearrange("p k t -> p (k t)"), turned[:]).then_inc(hT_done, 1)

            act.sem_inc(hT_done, 1)
            split(0, 0)
            for k in range(KD):
                act.wait_ge(w_loaded[k % 2], 16 * (k // 2 + 1))
                act.copy(w[0][:, k], raw_w[:, k % 2]).then_inc(w_high, 1)
            split(0, 1)
            square(0, 0)
            split(1, 0)
            with act.Fori(0, TILES // 2 - 2) as i:
                square(i, 1)
                copy_hT(i, 0)
                split(i + 1, 1)
                square(i + 1, 0)
                copy_hT(i, 1)
                split(i + 2, 0)
            i = TILES // 2 - 2
            square(i, 1)
            copy_hT(i, 0)
            split(i + 1, 1)
            square(i + 1, 0)
            copy_hT(i, 1)
            square(i + 1, 1)
            copy_hT(i + 1, 0)
            copy_hT(i + 1, 1)

        @block.vector
        def _(dve):
            def low(out, source, high, done):
                dve.tensor_tensor(out, source, high.bitcast(F32), ALU.subtract).then_inc(done, 1)

            def split(i, u):
                dve.wait_ge(m_high, 2 * i + (u + 1))
                low(mT[u][1][:], raw_m[:, u], mT[u][0][:], m_low)

            def add(i, u):
                dve.wait_ge(proj_done, 2 * i + (u + 3))
                dve.wait_ge(x2_done, 2 * i + (u + 1))
                dve.tensor_tensor(scaled_out[:], proj[:, u], gate1, ALU.mult).then_inc(gate_done, 1)
                dve.wait_ge(gate_done, 2 * i + (u + 3))
                dve.wait_ge(x_loaded[u], i * 16 + 16)
                dve.tensor_tensor(x[:, u], x[:, u], scaled_out[:], ALU.add).then_inc(x2_done, 1)

            def normalise(i, u):
                dve.wait_ge(rms_done, 2 * i + (u + 1))
                dve.reciprocal(rstd[:, u:u + 1], rms[:, u:u + 1]).then_inc(rstd_done, 1)
                dve.wait_ge(rstd_done, 2 * i + (u + 1))
                dve.wait_ge(turn_done, 2 * i + (u + 1))
                dve.wait_ge(h_stored[u], i * 16 + 16)
                dve.scalar_tensor_tensor(h[:, u], x[:, u], rstd[:, u:u + 1], scale, ALU.mult, ALU.mult).then_inc(normed, 1)
                dve.wait_ge(normed, 2 * i + (u + 3))
                dve.tensor_tensor(h[:, u], h[:, u], shift, ALU.add).then_inc(h_done, 1)

            def take(i, u):
                dve.wait_ge(route_done, 2 * i + (u + 3))
                dve.tensor_tensor(logits[:, ds(2 * i + u, 1), :].rearrange("p a n -> p (a n)"), routed[:, u, 0:EG + NE],
                                  bias[:], ALU.add).then_inc(logits_done, 1)

            dve.sem_inc(m_low, 2)
            dve.sem_inc(gate_done, 2)
            dve.sem_inc(x2_done, 1)
            dve.sem_inc(normed, 2)
            dve.sem_inc(logits_done, 2)
            split(0, 0)
            for k in range(KD):
                dve.wait_ge(w_high, k + 1)
                low(w[1][:, k], raw_w[:, k % 2], w[0][:, k], w_low)
            split(0, 1)
            dve.wait_ge(wr_loaded, 16 * (EG + 3))
            add(0, 0)
            normalise(0, 0)
            split(1, 0)
            add(0, 1)
            normalise(0, 1)
            split(1, 1)
            with dve.Fori(1, TILES // 2 - 1) as i:
                add(i, 0)
                normalise(i, 0)
                split(i + 1, 0)
                take(i - 1, 0)
                add(i, 1)
                normalise(i, 1)
                split(i + 1, 1)
                take(i - 1, 1)
            i = TILES // 2 - 1
            add(i, 0)
            normalise(i, 0)
            take(i - 1, 0)
            add(i, 1)
            normalise(i, 1)
            take(i - 1, 1)
            take(i, 0)
            take(i, 1)
            dve.wait_ge(logits_done, 2 + TILES)


def dispatch_phase(nc, const, logits, weight, slot, tables, slot_row_dram):
    T = TILES
    with ExitStack() as stack:
        s = Scope(nc, stack, "dsp")
        gl, el = logits[:, :, 0:EG], logits[:, :, EG:].rearrange("p t (g e) -> p t g e", g=EG)
        gmax, gsum, p_group, index = s.sb("gmax", [P, T, 1]), s.sb("gsum", [P, T, 1]), s.sb("p_group", [P, T, 1]), s.sb("index", [P, T, 1])
        tmp4, g_hot = s.sb("tmp4", [P, T, EG]), s.sb("g_hot", [P, T, EG])
        inner, tmp8 = s.sb("inner", [P, T, EPG]), s.sb("tmp8", [P, T, EPG])
        e_hot = s.sb("e_hot", [P, 2, T, EPG])
        best = s.sb("best", [P, 2, T, 1])
        gap = s.sb("gap", [P, 2, T])
        hot = s.sb("hot", [P, 2, T, NE])
        either, earlier = s.sb("either", [P, T, NE]), s.sb("earlier", [P, T + 1, NE])
        place, picked = s.sb("place", [P, T, NE]), s.sb("picked", [P, 2, T, NE])
        count_i, filled_i = s.sb("count_i", [P, NE], I32), s.sb("filled_i", [P, NE], I32)
        filled, end, base = s.sb("filled", [P, NE]), s.sb("end", [P, NE]), s.sb("base", [P, NE])
        slot_f = s.sb("slot_f", [P, 2, T])
        over = s.sb("over", [P, BLOCKS, NE])
        expert_f, new_f, ordinal_f = s.sb("expert_f", [P, BLOCKS]), s.sb("new_f", [P, BLOCKS]), s.sb("ordinal_f", [P, BLOCKS])
        zero_rows = s.sb("zero_rows", [P, SLOTS // P], U32)
        rank, total = s.ps("rank", [P, BANK]), s.ps("total", [P, BANK])
        done, zeroed, zero_stored, scattered = s.sem("done"), s.sem("zeroed"), s.sem("zero_stored"), s.sem("scattered")
        exp_done, weight_done, ranked = s.sem("exp_done"), s.sem("weight_done"), s.sem("ranked")
        at = {}
        count = [0]
        block = stack.enter_context(nc.Block())

        @block.vector
        def _(dve):
            def step(ins_, name=None):
                count[0] += 1
                ins_.then_inc(done, 1)
                dve.wait_ge(done, count[0])
                if name:
                    at[name] = count[0]

            def first_best(values, top, n, hot_out):
                tmp = (tmp4 if n == EG else tmp8)[:]
                step(dve.tensor_tensor(tmp, values, top.to_broadcast([P, T, n]), ALU.is_equal))
                places = const["iota"][:, 0:n].unsqueeze(1).to_broadcast([P, T, n])
                step(dve.scalar_tensor_tensor(hot_out, places, -float(n), tmp, ALU.add, ALU.mult))
                step(dve.tensor_reduce(index[:], hot_out, AX_X, ALU.min))
                step(dve.tensor_scalar(index[:], index[:], float(n), None, ALU.add))
                step(dve.tensor_tensor(hot_out, places, index[:].to_broadcast([P, T, n]), ALU.is_equal))

            step(dve.memset(zero_rows[:], 0), "zero_rows")
            step(dve.tensor_reduce(gmax[:], gl, AX_X, ALU.max))
            step(dve.tensor_tensor(tmp4[:], gl, gmax[:].to_broadcast([P, T, EG]), ALU.subtract), "group_gap")
            dve.wait_ge(exp_done, 1)
            step(dve.tensor_reduce(gsum[:], tmp4[:], AX_X, ALU.add))
            step(dve.reciprocal(p_group[:], gsum[:]))
            first_best(gl, gmax[:], EG, g_hot[:])
            step(dve.tensor_tensor(inner[:], el[:, :, 0], g_hot[:, :, 0:1].to_broadcast([P, T, EPG]), ALU.mult))
            for g in range(1, EG):
                step(dve.tensor_tensor(tmp8[:], el[:, :, g], g_hot[:, :, g:g + 1].to_broadcast([P, T, EPG]), ALU.mult))
                step(dve.tensor_tensor(inner[:], inner[:], tmp8[:], ALU.add))
            for j in range(2):
                step(dve.tensor_reduce(best[:, j], inner[:], AX_X, ALU.max))
                first_best(inner[:], best[:, j], EPG, e_hot[:, j])
                if j == 0:
                    step(dve.scalar_tensor_tensor(inner[:], e_hot[:, 0], -1e30, inner[:], ALU.mult, ALU.add))
            for j in range(2):
                step(dve.tensor_tensor(gap[:, j], best[:, j, :, 0], best[:, 1 - j, :, 0], ALU.subtract), "best_gap")
            for j in range(2):
                for g in range(EG):
                    step(dve.tensor_tensor(hot[:, j, :, g * EPG:(g + 1) * EPG], e_hot[:, j],
                                           g_hot[:, :, g:g + 1].to_broadcast([P, T, EPG]), ALU.mult))
            step(dve.tensor_tensor(either[:], hot[:, 0], hot[:, 1], ALU.add))
            step(dve.memset(earlier[:, 0], 0.0))
            for t in range(T):
                step(dve.tensor_tensor(earlier[:, t + 1], earlier[:, t], either[:, t], ALU.add), "counted")
            dve.wait_ge(weight_done, 1)
            for j in range(2):
                step(dve.tensor_tensor(weight[:, j], gap[:, j], p_group[:, :, 0], ALU.mult))
            dve.wait_ge(ranked, 1)
            step(dve.tensor_scalar(count_i[:], total[:, 0:NE], float(P - 1), None, ALU.add))
            step(dve.tensor_scalar(filled_i[:], count_i[:], 7, None, ALU.arith_shift_right))
            step(dve.tensor_copy(filled[:], filled_i[:]))
            zero = const["causal"][:, P:P + 1]
            step(dve.tensor_tensor_scan(end[:], filled[:], zero.to_broadcast([P, NE]), 0.0, ALU.add, ALU.add))
            step(dve.tensor_tensor(base[:], end[:], filled[:], ALU.subtract))
            step(dve.scalar_tensor_tensor(place[:], base[:].unsqueeze(1).to_broadcast([P, T, NE]), float(P),
                                          rank[:].rearrange("p (t e) -> p t e", t=T), ALU.mult, ALU.add))
            for j in range(2):
                step(dve.tensor_tensor(picked[:, j], place[:], hot[:, j], ALU.mult))
                step(dve.tensor_reduce(slot_f[:, j].unsqueeze(2), picked[:, j], AX_X, ALU.add))
                step(dve.tensor_copy(slot[:, j], slot_f[:, j]), "slots")
            n = BLOCKS
            step(dve.tensor_tensor(over[:], end[:].unsqueeze(1).to_broadcast([P, n, NE]),
                                   const["iota"][:, 0:n].unsqueeze(2).to_broadcast([P, n, NE]), ALU.is_le))
            step(dve.tensor_reduce(expert_f[:].unsqueeze(2), over[:], AX_X, ALU.add))
            step(dve.tensor_scalar(expert_f[:], expert_f[:], float(NE - 1), None, ALU.min))
            step(dve.tensor_copy(tables["expert"][:, 0:n], expert_f[:]))
            step(dve.memset(new_f[:], 1.0))
            step(dve.tensor_tensor(new_f[:, 1:n], expert_f[:, 1:n], expert_f[:, 0:n - 1], ALU.not_equal))
            step(dve.scalar_tensor_tensor(new_f[:], const["iota"][:, 0:n], end[:, NE - 1:NE], new_f[:], ALU.is_lt, ALU.mult))
            for name in ("expert", "new", "ordinal"):
                step(dve.memset(tables[name][:, n:n + 1], 0))
            step(dve.tensor_copy(tables["new"][:, 0:n], new_f[:]))
            step(dve.tensor_tensor_scan(ordinal_f[:], new_f[:], zero.to_broadcast([P, n]), 0.0, ALU.add, ALU.add))
            step(dve.tensor_copy(tables["ordinal"][:, 0:n], ordinal_f[:]))
            step(dve.tensor_scalar(count_i[:, 0:1], end[:, NE - 1:NE], -1.0, None, ALU.add))
            step(dve.tensor_scalar(tables["blocks"][:, 0:1], count_i[:, 0:1], 1, None, ALU.arith_shift_right))
            step(dve.tensor_scalar(tables["blocks"][:, 1:2], tables["blocks"][:, 0:1], -2.0, BLOCKS - 2.0, ALU.mult, ALU.add))

        @block.scalar
        def _(act):
            act.wait_ge(done, at["group_gap"])
            act.activation(tmp4[:], tmp4[:], ACT.Exp).then_inc(exp_done, 1)
            act.wait_ge(done, at["best_gap"])
            act.activation(gap[:], gap[:], ACT.Sigmoid).then_inc(weight_done, 1)

        @block.tensor
        def _(pe):
            pe.wait_ge(done, at["counted"])
            pe.matmul(rank[:], const["before"][:], either[:].rearrange("p t e -> p (t e)"), start=True, stop=False)
            pe.matmul(rank[:], const["ones"][:], earlier[:, 0:T].rearrange("p t e -> p (t e)"), start=False, stop=True)
            pe.matmul(total[:, 0:NE], const["ones"][:], earlier[:, T], start=True, stop=True).then_inc(ranked, 1)

        @block.gpsimd
        def _(pool):
            pool.wait_ge(done, at["zero_rows"])
            pool.dma_start(slot_row_dram.rearrange("(p n) a -> p (n a)", p=P), zero_rows[:]).then_inc(zero_stored, 16)
            pool.wait_ge(zero_stored, 16)
            pool.wait_ge(done, at["slots"])
            for j in range(2):
                for t in range(T):
                    pool.indirect_dma_start(slot_row_dram, bass.IndirectOffsetOnAxis(ap=slot[:, j, t:t + 1], axis=0),
                                            const["rows"][:, t:t + 1], None).then_inc(scattered, 16)
            pool.wait_ge(scattered, 16 * 2 * T)


def experts_phase(nc, ins, const, gate2, tables, slot_row_dram, h2_dram, y_dram):
    ZERO_COLS = 256
    HALF = KD * F // 2
    PIECES = 6
    GATE, UP, DOWN = (0, 1), (2, 3), (4, 5)
    ON_POOL = (3, 5)
    with ExitStack() as stack:
        s = Scope(nc, stack, "moe")
        raw = s.sb("raw", [P, PIECES, HALF])
        high, low = s.sb("high", [P, PIECES, HALF], F32R), s.sb("low", [P, PIECES, HALF], F32R)
        row_blocks, row_blocks_f = s.sb("row_blocks", [BLOCKS + 1, P], U32), s.sb("row_blocks_f", [BLOCKS + 1, P])
        rows = s.sb("rows", [P, BLOCKS + 1], U32)
        row = [s.sb(f"row{u}", [P, 1], U32) for u in range(2)]
        h = [s.sb(f"h{u}", [P, D]) for u in range(2)]
        hT = [[s.sb(f"hT{u}_{part}", [P, KD, P], F32R) for part in ("high", "low")] for u in range(2)]
        sig, gated, act_h = s.sb("sig", [P, F]), s.sb("gated", [P, F]), s.sb("act_h", [P, F])
        act_hT = [s.sb(f"act_hT_{part}", [P, KF, P], F32R) for part in ("high", "low")]
        y = s.sb("y", [P, 2, D])
        zero = s.sb("zero", [P, ZERO_COLS])
        gate, up = s.ps("gate", [P, BANK]), s.ps("up", [P, BANK])
        turned = s.ps("turned", [P, KD * P])
        turned2 = s.ps("turned2", [P, BANK])
        down = s.ps("down", [P, D])
        rows_loaded, rows_float, rows_turned, rows_set, row_set = (s.sem("rows_loaded"), s.sem("rows_float"), s.sem("rows_turned"),
                                                                   s.sem("rows_set"), s.sem("row_set"))
        h_loaded, stored = s.sems("h_loaded", 2), s.sems("stored", 2)
        raw_loaded, high_done, low_done = s.sems("raw_loaded", PIECES), s.sems("high_done", PIECES), s.sems("low_done", PIECES)
        turn_done, hT_high, hT_low = s.sem("turn_done"), s.sem("hT_high"), s.sem("hT_low")
        gate_done, up_done, sig_done = s.sem("gate_done"), s.sem("up_done"), s.sem("sig_done")
        gated_done, act_done, turn2_done = s.sem("gated_done"), s.sem("act_done"), s.sem("turn2_done")
        act_hT_high, act_hT_low = s.sem("act_hT_high"), s.sem("act_hT_low")
        down_done, y_done = s.sem("down_done"), s.sem("y_done")
        zero_set, zero_stored = s.sem("zero_set"), s.sem("zero_stored")
        w_gate = ins["w_exp_gate"][0].rearrange("e (p k) n -> e p (k n)", k=KD)
        w_up = ins["w_exp_up"][0].rearrange("e (p k) n -> e p (k n)", k=KD)
        w_down = ins["w_exp_down"][0].rearrange("e (p k) n -> e p (k n)", k=KF)
        source = (w_gate, w_gate, w_up, w_up, w_down, w_down)
        block = stack.enter_context(nc.Block())

        def last_pair(eng):
            return eng.value_load(tables["blocks"][0:1, 0:1], min_val=SEQ // P - 1, max_val=BLOCKS // 2 - 1)

        def is_new(eng, n):
            return eng.value_load(tables["new"][0:1, ds(n, 1)], min_val=0, max_val=1) > 0

        def ordinal(eng, n):
            return eng.value_load(tables["ordinal"][0:1, ds(n, 1)], min_val=0, max_val=NE)

        def all_blocks(eng, body):
            more = last_pair(eng)
            body(0, 0, 0, True, False)
            with eng.Fori(0, more) as j:
                body(2 * j + 1, 1, j, False, False)
                body(2 * j + 2, 0, j + 1, False, False)
            body(2 * more + 1, 1, more, False, True)
            return more

        @block.sync
        def _(sp):
            def load(n, pieces):
                with sp.If(is_new(sp, n)):
                    e = sp.value_load(tables["expert"][0:1, ds(n, 1)], min_val=0, max_val=NE - 1)
                    o = ordinal(sp, n)
                    for c in pieces:
                        sp.wait_ge(low_done[c], o)
                        sp.dma_start(raw[:, c], source[c][ds(e, 1), :, (c % 2) * HALF:(c % 2 + 1) * HALF].rearrange(
                            "e p n -> (e p) n")).then_inc(raw_loaded[c], 16)

            def work(n, u, i, first, last):
                load(n, DOWN)
                if not last:
                    load(n + 2, GATE + UP)

            sp.dma_start(row_blocks[:], slot_row_dram.rearrange("(n p) a -> n (p a)", p=P)).then_inc(rows_loaded, 16)
            load(0, GATE + UP)
            load(1, GATE + UP)
            all_blocks(sp, work)
            sp.wait_ge(zero_set, 1)
            idle = sp.value_load(tables["blocks"][0:1, 1:2], min_val=0, max_val=BLOCKS - 2 * SEQ // P)
            with sp.Fori(0, idle + 1) as n:
                sp.dma_start(y_dram[ds((BLOCKS - n) * P, P), :].rearrange("p (r n) -> p r n", n=ZERO_COLS),
                             zero[:].unsqueeze(1).to_broadcast([P, D // ZERO_COLS, ZERO_COLS])).then_inc(zero_stored, 16)
            sp.wait_ge(zero_stored, 16 * idle + 16)
            sp.nop(nofuse=True)

        def split_low(eng, c, o):
            eng.wait_ge(high_done[c], o)
            eng.tensor_tensor(low[:, c], raw[:, c], high[:, c].bitcast(F32), ALU.subtract).then_inc(low_done[c], 1)

        @block.gpsimd
        def _(pool):
            def gather(n, u, i):
                pool.wait_ge(turn_done, n + 1)
                pool.tensor_copy(row[u][:], rows[:, ds(n, 1)]).then_inc(row_set, 1)
                pool.wait_ge(row_set, n + 1)
                pool.nop(nofuse=True)
                pool.indirect_dma_start(h[u][:], None, h2_dram, bass.IndirectOffsetOnAxis(ap=row[u][:], axis=0)).then_inc(h_loaded[u], 16)

            def split_down(n):
                with pool.If(is_new(pool, n)):
                    split_low(pool, DOWN[1], ordinal(pool, n))

            def work(n, u, i, first, last):
                if not first:
                    split_down(n - 1)
                if not last:
                    gather(n + 2, u, i + 1)
                    with pool.If(is_new(pool, n + 1)):
                        split_low(pool, UP[1], ordinal(pool, n + 1))

            for c in ON_POOL:
                pool.sem_inc(low_done[c], 1)
            pool.wait_ge(rows_set, 1)
            gather(0, 0, 0)
            gather(1, 1, 0)
            split_low(pool, UP[1], 1)
            more = all_blocks(pool, work)
            split_down(2 * more + 1)
            pool.wait_ge(h_loaded[0], 16 * more + 32)
            pool.nop(nofuse=True)

        @block.tensor
        def _(pe):
            def product(out, x, pieces, cols):
                k_half = HALF // cols
                for c in range(cols // BANK):
                    for k in range(2 * k_half):
                        at = (k % k_half) * cols + c * BANK
                        w_high = high[:, pieces[k // k_half], at:at + BANK]
                        w_low = low[:, pieces[k // k_half], at:at + BANK]
                        to = out[:, c * BANK:(c + 1) * BANK]
                        pe.matmul(to, x[0][:, k], w_high, start=(k == 0), stop=False)
                        pe.matmul(to, x[0][:, k], w_low, start=False, stop=False)
                        mm = pe.matmul(to, x[1][:, k], w_high, start=False, stop=(k == 2 * k_half - 1))
                return mm

            def split(pieces, o):
                for c in pieces:
                    pe.wait_ge(low_done[c], o + 1)

            def turn(n, u, i):
                pe.wait_ge(h_loaded[u], 16 * i + 16)
                pe.wait_ge(hT_low, n + 1)
                for k in range(KD):
                    mm = pe.transpose(turned[:, k * P:(k + 1) * P], h[u][:].rearrange("p (c k) -> p k c", k=KD)[:, k],
                                      const["ident"][:])
                mm.then_inc(turn_done, 1)

            def turn_hidden(n):
                pe.wait_ge(act_done, n + 2)
                pe.wait_ge(act_hT_low, n + 1)
                for k in range(KF):
                    mm = pe.transpose(turned2[:, k * P:(k + 1) * P], act_h[:].rearrange("p (f k) -> p k f", k=KF)[:, k],
                                      const["ident"][:])
                mm.then_inc(turn2_done, 1)

            def down_product(n):
                o = ordinal(pe, n)
                pe.wait_ge(act_hT_low, n + 2)
                split(DOWN, o)
                pe.wait_ge(y_done, n + 1)
                product(down, act_hT, DOWN, D).then_inc(down_done, 1)

            def work(n, u, i, first, last):
                o = ordinal(pe, n)
                if not first:
                    turn_hidden(n - 1)
                pe.wait_ge(hT_low, n + 2)
                split(GATE, o)
                pe.wait_ge(gated_done, n + 1)
                product(gate, hT[u], GATE, F).then_inc(gate_done, 1)
                if not last:
                    turn(n + 1, 1 - u, i + u)
                split(UP, o)
                pe.wait_ge(act_done, n + 1)
                product(up, hT[u], UP, F).then_inc(up_done, 1)
                if not first:
                    down_product(n - 1)

            pe.sem_inc(turn_done, 2)
            pe.sem_inc(up_done, 2)
            pe.sem_inc(down_done, 2)
            pe.wait_ge(rows_float, 1)
            pe.transpose(turned2[:, 0:BLOCKS + 1], row_blocks_f[:], const["ident"][0:BLOCKS + 1, 0:BLOCKS + 1]).then_inc(rows_turned, 1)
            turn(0, 0, 0)
            pe.wait_ge(rows_set, 1)
            more = all_blocks(pe, work)
            turn_hidden(2 * more + 1)
            down_product(2 * more + 1)

        @block.scalar
        def _(act):
            def split_high(c, o):
                act.wait_ge(raw_loaded[c], 16 * o)
                act.copy(high[:, c], raw[:, c]).then_inc(high_done[c], 1)

            def split_down(n):
                with act.If(is_new(act, n)):
                    o = ordinal(act, n)
                    act.wait_ge(down_done, n + 2)
                    for c in DOWN:
                        split_high(c, o)

            def split_gate_up(n):
                with act.If(is_new(act, n)):
                    o = ordinal(act, n)
                    act.wait_ge(gate_done, n)
                    for c in GATE:
                        split_high(c, o)
                    act.wait_ge(up_done, n + 2)
                    for c in UP:
                        split_high(c, o)

            def copy_hT(n, u):
                act.wait_ge(turn_done, n + 3)
                act.wait_ge(up_done, n + 1)
                act.copy(hT[u][0][:].rearrange("p k t -> p (k t)"), turned[:]).then_inc(hT_high, 1)

            def copy_act_hT(n):
                act.wait_ge(turn2_done, n + 1)
                act.wait_ge(down_done, n + 2)
                act.copy(act_hT[0][:].rearrange("p k t -> p (k t)"), turned2[:]).then_inc(act_hT_high, 1)

            def store(n, u):
                act.wait_ge(y_done, n + 2)
                act.dma_start(y_dram[ds(n * P, P), :], y[:, u]).then_inc(stored[u], 16)

            def work(n, u, i, first, last):
                if not first:
                    copy_act_hT(n - 1)
                    split_down(n - 1)
                act.wait_ge(gate_done, n + 1)
                act.wait_ge(gated_done, n + 1)
                act.activation(sig[:], gate[:], ACT.Sigmoid).then_inc(sig_done, 1)
                if not last:
                    copy_hT(n + 1, 1 - u)
                    split_gate_up(n + 1)
                if not first:
                    store(n - 1, 1 - u)

            for u in range(2):
                act.sem_inc(stored[u], 16)
            copy_hT(0, 0)
            for c in GATE + UP:
                split_high(c, 1)
            more = all_blocks(act, work)
            copy_act_hT(2 * more + 1)
            split_down(2 * more + 1)
            store(2 * more + 1, 1)
            for u in range(2):
                act.wait_ge(stored[u], 16 * more + 32)
            act.nop(nofuse=True)

        @block.vector
        def _(dve):
            def split_down(n):
                with dve.If(is_new(dve, n)):
                    split_low(dve, DOWN[0], ordinal(dve, n))

            def split_piece(n, pieces):
                with dve.If(is_new(dve, n)):
                    o = ordinal(dve, n)
                    for c in pieces:
                        split_low(dve, c, o)

            def copy_hT(n, u):
                dve.wait_ge(hT_high, n + 1)
                dve.tensor_tensor(hT[u][1][:].rearrange("p k t -> p (k t)"), turned[:],
                                  hT[u][0][:].rearrange("p k t -> p (k t)").bitcast(F32), ALU.subtract).then_inc(hT_low, 1)

            def copy_act_hT(n):
                dve.wait_ge(act_hT_high, n + 1)
                dve.tensor_tensor(act_hT[1][:].rearrange("p k t -> p (k t)"), turned2[:],
                                  act_hT[0][:].rearrange("p k t -> p (k t)").bitcast(F32), ALU.subtract).then_inc(act_hT_low, 1)

            def take(n, u, i):
                dve.wait_ge(down_done, n + 3)
                dve.wait_ge(stored[u], 16 * i + 16)
                dve.tensor_tensor(y[:, u], down[:], gate2[:], ALU.mult).then_inc(y_done, 1)

            def work(n, u, i, first, last):
                if not first:
                    copy_act_hT(n - 1)
                    split_down(n - 1)
                dve.wait_ge(sig_done, n + 1)
                dve.tensor_tensor(gated[:], sig[:], gate[:], ALU.mult).then_inc(gated_done, 1)
                if not last:
                    copy_hT(n + 1, 1 - u)
                    split_piece(n + 1, GATE)
                dve.wait_ge(up_done, n + 3)
                dve.wait_ge(gated_done, n + 2)
                if not first:
                    dve.wait_ge(turn2_done, n)
                dve.tensor_tensor(act_h[:], gated[:], up[:], ALU.mult).then_inc(act_done, 1)
                if not last:
                    split_piece(n + 1, UP[:1])
                if not first:
                    take(n - 1, 1 - u, i - 1 + u)

            dve.memset(zero[:], 0.0).then_inc(zero_set, 1)
            for c in GATE + UP[:1] + DOWN[:1]:
                dve.sem_inc(low_done[c], 1)
            dve.sem_inc(hT_low, 1)
            dve.sem_inc(gated_done, 1)
            dve.sem_inc(act_done, 1)
            dve.sem_inc(act_hT_low, 1)
            dve.sem_inc(y_done, 1)
            dve.wait_ge(rows_loaded, 16)
            dve.tensor_copy(row_blocks_f[:], row_blocks[:]).then_inc(rows_float, 1)
            dve.wait_ge(rows_turned, 1)
            dve.tensor_copy(rows[:], turned2[:, 0:BLOCKS + 1]).then_inc(rows_set, 1)
            copy_hT(0, 0)
            for c in GATE + UP[:1]:
                split_low(dve, c, 1)
            more = all_blocks(dve, work)
            copy_act_hT(2 * more + 1)
            split_down(2 * more + 1)
            take(2 * more + 1, 1, more)


def final_phase(nc, ins, const, weight, slot, x2_dram, y_dram, out):
    with ExitStack() as stack:
        s = Scope(nc, stack, "fin")
        B = 3
        ya = [s.sb(f"ya{u}", [P, D]) for u in range(B)]
        yb = [s.sb(f"yb{u}", [P, D]) for u in range(B)]
        x, res = s.sb("x", [P, B, D]), s.sb("res", [P, B, D])
        g, junk = s.sb("g", [P, D]), s.sb("junk", [P, D])
        ssq, rms, rstd = s.sb("ssq", [P, TILES]), s.sb("rms", [P, TILES]), s.sb("rstd", [P, TILES])
        x_loaded, y_loaded, g_loaded, stored = s.sems("x_loaded", B), s.sems("y_loaded", B), s.sem("g_loaded"), s.sems("stored", B)
        first_done, sum_done, x3_done, ssq_done = s.sem("first_done"), s.sem("sum_done"), s.sem("x3_done"), s.sem("ssq_done")
        rms_done, rstd_done, res_done = s.sem("rms_done"), s.sem("rstd_done"), s.sem("res_done")
        block = stack.enter_context(nc.Block())

        @block.gpsimd
        def _(pool):
            for t in range(TILES):
                if t >= B:
                    pool.wait_ge(x3_done, t - B + 1)
                for j, y in enumerate((ya, yb)):
                    pool.indirect_dma_start(y[t % B][:], None, y_dram,
                                            bass.IndirectOffsetOnAxis(ap=slot[:, j, t:t + 1], axis=0)).then_inc(y_loaded[t % B], 16)

        @block.sync
        def _(sp):
            sp.dma_start(g[:], ins["norm_f_g"].unsqueeze(0).partition_broadcast(P)).then_inc(g_loaded, 16)
            for t in range(TILES):
                if t >= B:
                    sp.wait_ge(res_done, t - B + 1)
                    sp.dma_start(out[0, (t - B) * P:(t - B + 1) * P, :], res[:, t % B]).then_inc(stored[t % B], 16)
                sp.dma_start(x[:, t % B], x2_dram[t * P:(t + 1) * P, :]).then_inc(x_loaded[t % B], 16)
            for t in range(TILES - B, TILES):
                sp.wait_ge(res_done, t + 1)
                sp.dma_start(out[0, t * P:(t + 1) * P, :], res[:, t % B]).then_inc(stored[t % B], 16)
            for u in range(B):
                sp.wait_ge(stored[u], 16 * len(range(u, TILES, B)))

        @block.scalar
        def _(act):
            def first(t):
                act.wait_ge(y_loaded[t % B], 32 * (t // B + 1))
                act.mul(ya[t % B][:], ya[t % B][:], weight[:, 0, t:t + 1]).then_inc(first_done, 1)

            first(0)
            for t in range(TILES):
                if t + 1 < TILES:
                    first(t + 1)
                act.wait_ge(x3_done, t + 1)
                act.activation(junk[:], x[:, t % B], ACT.Square, accum_out=ssq[:, t:t + 1]).then_inc(ssq_done, 1)
                act.wait_ge(ssq_done, t + 1)
                act.activation(rms[:, t:t + 1], ssq[:, t:t + 1], ACT.Sqrt, bias=const["eps"][:],
                               scale=1.0 / D).then_inc(rms_done, 1)

        @block.vector
        def _(dve):
            def combine(t):
                u = t % B
                dve.wait_ge(first_done, t + 1)
                dve.scalar_tensor_tensor(yb[u][:], yb[u][:], weight[:, 1, t:t + 1], ya[u][:], ALU.mult, ALU.add).then_inc(sum_done, 1)
                dve.wait_ge(sum_done, t + 1)
                dve.wait_ge(x_loaded[u], 16 * (t // B + 1))
                dve.tensor_tensor(x[:, u], x[:, u], yb[u][:], ALU.add).then_inc(x3_done, 1)

            def normalise(t):
                u = t % B
                dve.wait_ge(rms_done, t + 1)
                dve.reciprocal(rstd[:, t:t + 1], rms[:, t:t + 1]).then_inc(rstd_done, 1)
                dve.wait_ge(rstd_done, t + 1)
                if t >= B:
                    dve.wait_ge(stored[u], 16 * (t // B))
                dve.scalar_tensor_tensor(res[:, u], x[:, u], rstd[:, t:t + 1], g[:], ALU.mult, ALU.mult).then_inc(res_done, 1)

            dve.wait_ge(g_loaded, 16)
            combine(0)
            for t in range(TILES):
                if t + 1 < TILES:
                    combine(t + 1)
                normalise(t)


def hybrid_layer_kernel(nc, ins, out):
    Scope.numbers = []
    o_dram = nc.dram_tensor("o_rows", [SEQ, SBW], F32, kind="Internal").ap()
    opT_dram = nc.dram_tensor("opT_rows", [POOLW, SEQ], F32, kind="Internal").ap()
    mT_dram = nc.dram_tensor("mT_rows", [D, SEQ], F32, kind="Internal").ap()
    x2_dram = nc.dram_tensor("x2_rows", [SEQ, D], F32, kind="Internal").ap()
    h2_dram = nc.dram_tensor("h2_rows", [SEQ, D], F32, kind="Internal").ap()
    y_dram = nc.dram_tensor("y_rows", [(BLOCKS + 1) * P, D], F32, kind="Internal").ap()
    slot_row_dram = nc.dram_tensor("slot_rows", [SLOTS, 1], U32, kind="Internal").ap()
    with ExitStack() as stack:
        s = Scope(nc, stack, "all")
        const = {
            "ident": s.sb("ident", [P, P]), "step": s.sb("step", [P, P]), "corner": s.sb("corner", [P, P]),
            "before": s.sb("before", [P, P]), "ones": s.sb("ones", [P, P]), "causal": s.sb("causal", [P, BANK]),
            "eps": s.sb("eps", [P, 1]), "iota": s.sb("iota", [P, 64]), "rows": s.sb("rows", [P, TILES], U32),
        }
        gate2 = s.sb("gate2", [P, D])
        logits = s.sb("logits", [P, TILES, EG + NE])
        weight, slot = s.sb("weight", [P, 2, TILES]), s.sb("slot", [P, 2, TILES], U32)
        constants_phase(nc, const)
        with nc.sbuf_tensor("mod2", [P, 3 * D], F32) as mod2:
            with nc.sbuf_tensor("hT", [P, KD, SEQ], F32) as hT:
                with nc.sbuf_tensor("mod1", [P, 2 * D], F32) as mod1:
                    modulation_phase(nc, ins, mod1, mod2, gate2)
                    norm1_phase(nc, ins, const, mod1, hT)
                attention_phase(nc, ins, const, hT, o_dram)
                clear_phase(nc)
                pool_phase(nc, ins, const, hT, opT_dram)
                branches_phase(nc, ins, const, hT, o_dram, opT_dram, mT_dram)
            output_phase(nc, ins, const, mod2, logits, mT_dram, x2_dram, h2_dram)
        tables = {name: s.sb(f"block_{name}", [P, n], I32)
                  for name, n in (("expert", BLOCKS + 1), ("new", BLOCKS + 1), ("ordinal", BLOCKS + 1), ("blocks", 2))}
        dispatch_phase(nc, const, logits, weight, slot, tables, slot_row_dram)
        experts_phase(nc, ins, const, gate2, tables, slot_row_dram, h2_dram, y_dram)
        final_phase(nc, ins, const, weight, slot, x2_dram, y_dram, out)


_INS = ["x", "c", "norm1_g", "norm2_g", "w_ada", "b_ada", "w_in", "pool_w", "pool_scale", "w_branch_sb",
        "w_branch_pool", "w_out", "w_route_group", "b_route_group", "w_route_expert", "b_route_expert",
        "w_exp_gate", "w_exp_up", "w_exp_down", "norm_f_g"]


def kernel(**inputs):
    import numpy as np
    import concourse.bacc as bacc
    from concourse.bass_utils import run_bass_kernel_spmd

    nc = bacc.Bacc("TRN2", target_bir_lowering=False, num_devices=1)
    arrays, ins = {}, {}
    for name in _INS:
        a = np.asarray(inputs[name])
        if name == "x":
            a = a[:, ::-1]
        a = np.ascontiguousarray(a)
        arrays[f"in_{name}"] = a
        ins[name] = nc.dram_tensor(f"in_{name}", a.shape, mybir.dt.from_np(a.dtype), kind="ExternalInput").ap()
    out = nc.dram_tensor("out_rows", (1, SEQ, D), F32, kind="ExternalOutput").ap()
    hybrid_layer_kernel(nc, ins, out)
    result = run_bass_kernel_spmd(nc, [arrays], core_ids=[0])
    return np.ascontiguousarray(result.results[0]["out_rows"][:, ::-1])
```

```python
from contextlib import ExitStack

import concourse.bass as bass
from concourse import mybir

ALU = mybir.AluOpType
ACT = mybir.ActivationFunctionType
AX_X = mybir.AxisListType.X
F32 = mybir.dt.float32
I32 = mybir.dt.int32
U32 = mybir.dt.uint32
F32R = mybir.dt.float32r
ds = bass.ds

P = 128
SEQ, D = 2048, 1024
KD = D // P
TILES = SEQ // P
BANK = 512
HD = 64
SBW = D // 2
PAIRS = SBW // P
POOLW = D // 2
GROUPS = 4
WINDOWS = (2, 4, 8, 16)
PAD = 16
EPS = 1e-6
EG, EPG = 4, 8
NE = EG * EPG
F = D // 2
KF = F // P
BLOCKS = 2 * SEQ // P + NE
K_OFF, V_OFF, P_OFF, GS_OFF, GP_OFF = SBW, 2 * SBW, 3 * SBW, 3 * SBW + POOLW, 3 * SBW + POOLW + D


class Scope:

    numbers = []

    def __init__(self, nc, stack, tag):
        self.nc, self.stack, self.tag = nc, stack, tag

    def sb(self, name, shape, dt=F32):
        return self.stack.enter_context(self.nc.sbuf_tensor(f"{self.tag}_{name}", shape, dt))

    def ps(self, name, shape, dt=F32):
        return self.stack.enter_context(self.nc.psum_tensor(f"{self.tag}_{name}", shape, dt))

    def sem(self, name):
        handle = self.stack.enter_context(self.nc.semaphore(f"{self.tag}_{name}"))
        self.numbers.append(handle.num)
        return handle

    def sems(self, name, n):
        return [self.sem(f"{name}{k}") for k in range(n)]


def clear_phase(nc):
    numbers = sorted(Scope.numbers)
    first, end = numbers[0], numbers[-1] + 1
    assert numbers == list(range(first, end))
    with nc.Block() as block:
        @block.gpsimd
        def _(pool):
            pool.sem_clear(range(first, end))


def constants_phase(nc, const):
    with ExitStack() as stack:
        s = Scope(nc, stack, "cst")
        filled, cut, ints, floats = s.sem("filled"), s.sem("cut"), s.sem("ints"), s.sem("floats")
        iota_i = s.sb("iota_i", [P, P], I32)
        block = stack.enter_context(nc.Block())

        @block.gpsimd
        def _(pool):
            pool.memset(const["ident"][:], 0.0).then_inc(filled, 1)
            pool.memset(const["before"][:], 1.0).then_inc(filled, 1)
            pool.memset(const["ones"][:], 1.0).then_inc(filled, 1)
            pool.memset(const["causal"][:], 0.0).then_inc(filled, 1)
            pool.memset(const["eps"][:], EPS).then_inc(filled, 1)
            pool.wait_ge(filled, 5)
            pool.affine_select(out=const["ident"][:], in_=const["ident"][:], compare_op=ALU.not_equal,
                               fill=1.0, base=0, pattern=[[-1, P]], channel_multiplier=1).then_inc(cut, 1)
            pool.affine_select(out=const["before"][:], in_=const["before"][:], compare_op=ALU.is_gt,
                               fill=0.0, base=0, pattern=[[1, P]], channel_multiplier=-1).then_inc(cut, 1)
            pool.affine_select(out=const["causal"][:, 0:P], in_=const["causal"][:, 0:P],
                               compare_op=ALU.is_gt, fill=1.0, base=0, pattern=[[1, P]],
                               channel_multiplier=-1).then_inc(cut, 1)
            pool.iota(iota_i[:], [[1, P]], base=0, channel_multiplier=0).then_inc(ints, 1)
            pool.iota(const["rows"][:], [[P, TILES]], base=0, channel_multiplier=1).then_inc(ints, 1)
            pool.wait_ge(ints, 2)
            pool.tensor_copy(const["iota"][:], iota_i[:]).then_inc(floats, 1)
            pool.wait_ge(cut, 3)
            pool.wait_ge(floats, 1)


def modulation_phase(nc, ins, const, mod1, c_act):
    N = 2 * D // BANK
    with ExitStack() as stack:
        s = Scope(nc, stack, "ada")
        w = s.sb("w", [P, N, KD, BANK])
        c_col, c_sig = s.sb("c_col", [P, KD]), s.sb("c_sig", [P, KD])
        c_wide = s.sb("c_wide", [P, KD, P])
        g = s.sb("g", [P, D])
        out = s.ps("out", [P, N, BANK])
        w_loaded = s.sems("w_loaded", N)
        c_loaded, b_loaded, g_loaded = s.sem("c_loaded"), s.sem("b_loaded"), s.sem("g_loaded")
        sig_done, act_done, wide_done = s.sem("sig_done"), s.sem("act_done"), s.sem("wide_done")
        product_done, added, scaled = s.sem("product_done"), s.sem("added"), s.sem("scaled")
        w_ada = ins["w_ada"][0].rearrange("(p k) n -> p k n", k=KD)
        block = stack.enter_context(nc.Block())

        @block.sync
        def _(sp):
            for n in range(N):
                sp.dma_start(w[:, n], w_ada[:, :, n * BANK:(n + 1) * BANK]).then_inc(w_loaded[n], 16)
            sp.dma_start(mod1[:], ins["b_ada"][0:1, 0:2 * D].partition_broadcast(P)).then_inc(b_loaded, 16)
            sp.dma_start(g[:], ins["norm1_g"][0:1].partition_broadcast(P)).then_inc(g_loaded, 16)

        @block.scalar
        def _(act):
            act.dma_start(c_col[:], ins["c"][0].rearrange("(p k) -> p k", k=KD)).then_inc(c_loaded, 16)
            act.wait_ge(c_loaded, 16)
            act.activation(c_sig[:], c_col[:], ACT.Sigmoid).then_inc(sig_done, 1)

        @block.tensor
        def _(pe):
            pe.wait_ge(wide_done, KD)
            for n in range(N):
                pe.wait_ge(w_loaded[n], 16)
                for k in range(KD):
                    mm = pe.matmul(out[:, n], c_wide[:, k], w[:, n, k], start=(k == 0), stop=(k == KD - 1))
                mm.then_inc(product_done, 1)

        @block.vector
        def _(dve):
            dve.wait_ge(sig_done, 1)
            dve.tensor_tensor(c_act[:], c_col[:], c_sig[:], ALU.mult).then_inc(act_done, 1)
            dve.wait_ge(act_done, 1)
            for k in range(KD):
                dve.tensor_scalar(c_wide[:, k], const["ones"][:], c_act[:, k:k + 1], None, ALU.mult).then_inc(wide_done, 1)
            dve.wait_ge(b_loaded, 16)
            for n in range(N):
                dve.wait_ge(product_done, n + 1)
                part = mod1[:, n * BANK:(n + 1) * BANK]
                dve.tensor_tensor(part, part, out[:, n], ALU.add).then_inc(added, 1)
            dve.wait_ge(added, N)
            dve.wait_ge(g_loaded, 16)
            scale = mod1[:, D:2 * D]
            dve.scalar_tensor_tensor(scale, scale, 1.0, g[:], ALU.add, ALU.mult).then_inc(scaled, 1)
            dve.wait_ge(scaled, 1)


def front_phase(nc, ins, const, mod1, c_act, mod2, gate2, hT, opT_dram):
    CHUNKS, TC = SEQ // BANK, BANK // P
    RING = 3
    L = BANK + PAD
    with ExitStack() as stack:
        s = Scope(nc, stack, "fr")
        PARTS = ("high", "low")
        x, h = s.sb("x", [P, 2, D]), s.sb("h", [P, 2, D])
        junk = s.sb("junk", [P, D])
        ssq, rms, rstd = s.sb("ssq", [P, 2]), s.sb("rms", [P, 2]), s.sb("rstd", [P, 2])
        raw = s.sb("raw", [P, GROUPS, KD, P])
        w = [s.sb(f"w_{part}", [P, GROUPS, KD, P], F32R) for part in PARTS]
        w2, p_scale = s.sb("w2", [P, GROUPS, P]), s.sb("p_scale", [P, GROUPS])
        piece = [s.sb(f"piece_{part}", [P, RING, BANK], F32R) for part in PARTS]
        pT = s.sb("pT", [P, 2, GROUPS, L])
        sums, mean, inv = s.sb("sums", [P, 2, L]), s.sb("mean", [P, 2, BANK]), s.sb("inv", [P, PAD])
        opT = s.sb("opT", [P, 2, BANK])
        turned = s.ps("turned", [P, KD * P])
        proj, mapped = s.ps("proj", [P, GROUPS, BANK]), s.ps("mapped", [P, 2, BANK])
        x_loaded, raw_loaded, small_loaded, stored = s.sems("x_loaded", 2), s.sems("raw_loaded", GROUPS), s.sem("small_loaded"), s.sems("stored", 2)
        ssq_done, rms_done, rstd_done, scaled, h_done = (s.sem("ssq_done"), s.sem("rms_done"), s.sem("rstd_done"),
                                                         s.sem("scaled"), s.sem("h_done"))
        turn_done, hT_done, w_high, w_low = s.sem("turn_done"), s.sem("hT_done"), s.sem("w_high"), s.sem("w_low")
        piece_high, piece_low, piece_used = s.sem("piece_high"), s.sem("piece_low"), s.sem("piece_used")
        pT_done, filled, sums_done, mean_done = s.sem("pT_done"), s.sem("filled"), s.sem("sums_done"), s.sem("mean_done")
        map_done, opT_done = s.sem("map_done"), s.sem("opT_done")
        shift, scale = mod1[:, 0:D], mod1[:, D:2 * D]
        w_in = ins["w_in"][0].rearrange("(k p) n -> p k n", p=P)
        ADA = 2 * D // TILES
        assert ADA == P
        ada = raw
        g2 = x[:, 0]
        ada_loaded, g2_loaded, bias_loaded, zeroed = s.sems("ada_loaded", 4), s.sem("g2_loaded"), s.sem("bias_loaded"), s.sem("zeroed")
        DVE_STEPS, POOL_STEPS = KD, 5
        mac_dve, mac_pool = s.sem("mac_dve"), s.sem("mac_pool")
        mod_summed, mod_done, scale2_done = s.sem("mod_summed"), s.sem("mod_done"), s.sem("scale2_done")
        w_ada = ins["w_ada"][0].rearrange("(p k) n -> p k n", k=KD)
        block = stack.enter_context(nc.Block())

        def rest(at, n):
            return mod2[:, at:at + n] if at < 3 * D else gate2[:, at - 3 * D:at - 3 * D + n]

        def schedule(norm=None, project=None, pool=None, project_end=None, pool_end=None,
                     project_first=False, sums=None):
            for i in range(CHUNKS + 2):
                for q in range(TC):
                    if project_first and 0 <= i - 1 < CHUNKS:
                        project(i - 1, q)
                    if i < CHUNKS and norm:
                        norm(i * TC + q)
                    if not project_first and 0 <= i - 1 < CHUNKS and project:
                        project(i - 1, q)
                    if 0 <= i - 1 < CHUNKS and sums:
                        sums((i - 1) * TC + q)
                    if 0 <= i - 2 < CHUNKS and pool:
                        pool(i - 2, q)
                if 0 <= i - 1 < CHUNKS and project_end:
                    project_end(i - 1)
                if 0 <= i - 2 < CHUNKS and pool_end:
                    pool_end(i - 2)

        def behind(work):
            return {"pool": lambda i, q: work(i, q - 2) if q >= 2 else None,
                    "pool_end": lambda i: [work(i, g) for g in (GROUPS - 2, GROUPS - 1)]}

        def tokens(i):
            c = CHUNKS - 1 - i
            return slice(c * BANK, (c + 1) * BANK)

        @block.sync
        def _(sp):
            def load_x(n):
                if n >= 2:
                    sp.wait_ge(scaled, n - 1)
                t = TILES - 1 - n
                sp.dma_start(x[:, n % 2], ins["x"][0, t * P:(t + 1) * P, :]).then_inc(x_loaded[n % 2], 16)
                if n < GROUPS:
                    sp.dma_start(raw[:, n], w_in[:, :, P_OFF + n * P:P_OFF + (n + 1) * P]).then_inc(raw_loaded[n], 16)
                if n == GROUPS:
                    sp.dma_start(w2[:], ins["pool_w"][0].rearrange("g c n -> c g n")).then_inc(small_loaded, 16)
                    sp.dma_start(p_scale[:], ins["pool_scale"][0].rearrange("(g p) -> p g", p=P),
                                 allow_slow_non_contiguous=True).then_inc(small_loaded, 16)

            def load_ada(j):
                if j == 0:
                    sp.wait_ge(w_low, GROUPS)
                for u, (summed, count) in enumerate(((mac_dve, DVE_STEPS), (mac_pool, POOL_STEPS))):
                    if j >= 2:
                        sp.wait_ge(summed, (j - 1) * count)
                    at, slot = 2 * D + (2 * j + u) * ADA, 2 * (j % 2) + u
                    sp.dma_start(ada[:, slot], w_ada[:, :, at:at + ADA]).then_inc(ada_loaded[slot], 16)

            load_x(0)
            load_x(1)
            sp.wait_ge(zeroed, 2)
            sp.dma_start(mod2[0:1], ins["b_ada"][0:1, 2 * D:5 * D]).then_inc(bias_loaded, 16)
            sp.dma_start(gate2[0:1], ins["b_ada"][0:1, 5 * D:]).then_inc(bias_loaded, 16)

            def project(i, q):
                j = i * TC + q
                if j == 0:
                    load_ada(0)
                    load_ada(1)
                if j + 2 < TILES:
                    load_ada(j + 2)

            schedule(norm=lambda n: load_x(n + 2) if n + 2 < TILES else None, project=project)
            sp.wait_ge(scaled, TILES)
            sp.dma_start(g2, ins["norm2_g"][0:1].partition_broadcast(P)).then_inc(g2_loaded, 16)

        @block.tensor
        def _(pe):
            def turn(n):
                pe.wait_ge(h_done, n + 1)
                if n:
                    pe.wait_ge(hT_done, n)
                for k in range(KD):
                    mm = pe.transpose(turned[:, k * P:(k + 1) * P], h[:, n % 2, k * P:(k + 1) * P], const["ident"][:])
                mm.then_inc(turn_done, 1)

            def project(i, q):
                if i == 0 and q == 0:
                    pe.wait_ge(w_low, GROUPS)
                if i and q == 0:
                    pe.wait_ge(pT_done, i * (GROUPS + 1) - 1)
                for k in (2 * q, 2 * q + 1):
                    n = i * KD + k
                    pe.wait_ge(piece_low, n + 1)
                    for g in range(GROUPS):
                        for a, b in ((0, 0), (0, 1), (1, 0)):
                            mm = pe.matmul(proj[:, g], w[a][:, g, k], piece[b][:, n % RING],
                                           start=(k == 0 and a + b == 0), stop=(k == KD - 1 and a == 1))
                    mm.then_inc(piece_used, 1)

            def pool(i, q):
                if q:
                    map_group(i, q - 1)
                if i == CHUNKS - 1:
                    for n in (2 * q, 2 * q + 1):
                        if n == 0:
                            pe.wait_ge(mac_dve, TILES * DVE_STEPS)
                            pe.wait_ge(mac_pool, TILES * POOL_STEPS)
                            pe.wait_ge(hT_done, TILES)
                        if n >= 2:
                            pe.wait_ge(mod_done, n - 1)
                        pe.matmul(turned[:, (n % 2) * BANK:(n % 2 + 1) * BANK], const["ones"][:], rest(n * BANK, BANK),
                                  start=True, stop=True).then_inc(mod_summed, 1)

            def map_group(i, g):
                n = i * GROUPS + g
                if n == 0:
                    pe.wait_ge(small_loaded, 32)
                pe.wait_ge(mean_done, n + 1)
                if n >= 2:
                    pe.wait_ge(opT_done, n - 1)
                pe.matmul(mapped[:, n % 2], w2[:, g], mean[:, n % 2], start=True, stop=True).then_inc(map_done, 1)

            schedule(norm=turn, project=project, pool=pool, pool_end=lambda i: map_group(i, GROUPS - 1))

        @block.scalar
        def _(act):
            def square(n):
                act.wait_ge(x_loaded[n % 2], 16 * (n // 2 + 1))
                if n >= 2:
                    act.wait_ge(rstd_done, n - 1)
                act.activation(junk[:], x[:, n % 2], ACT.Square, accum_out=ssq[:, n % 2:n % 2 + 1]).then_inc(ssq_done, 1)
                act.wait_ge(ssq_done, n + 1)
                act.activation(rms[:, n % 2:n % 2 + 1], ssq[:, n % 2:n % 2 + 1], ACT.Sqrt, bias=const["eps"][:],
                               scale=1.0 / D).then_inc(rms_done, 1)

            def norm(n):
                if n + 1 < TILES:
                    square(n + 1)
                if n < GROUPS:
                    act.wait_ge(raw_loaded[n], 16)
                    act.copy(w[0][:, n], raw[:, n]).then_inc(w_high, 1)
                t = TILES - 1 - n
                act.wait_ge(turn_done, n + 1)
                act.copy(hT[:, :, t * P:(t + 1) * P], turned[:].rearrange("p (k t) -> p k t", k=KD)).then_inc(hT_done, 1)

            def project(i, q):
                act.wait_ge(hT_done, (i + 1) * TC)
                for k in (2 * q, 2 * q + 1):
                    n = i * KD + k
                    if n >= RING:
                        act.wait_ge(piece_used, n - RING + 1)
                    act.copy(piece[0][:, n % RING], hT[:, k, tokens(i)]).then_inc(piece_high, 1)

            def take(i):
                act.wait_ge(piece_used, (i + 1) * KD)
                if i >= 2:
                    act.wait_ge(mean_done, (i - 1) * GROUPS)
                for g in range(GROUPS):
                    act.copy(pT[:, i % 2, g, 0:BANK], proj[:, g]).then_inc(pT_done, 1)
                if i:
                    act.wait_ge(pT_done, i * (GROUPS + 1) - 1)
                    act.copy(pT[:, i % 2, :, BANK:L], pT[:, 1 - i % 2, :, 0:PAD]).then_inc(pT_done, 1)

            def finish(i, g):
                n = i * GROUPS + g
                if n == 0:
                    act.wait_ge(small_loaded, 32)
                if n >= 2:
                    act.wait_ge(stored[n % 2], 16 * (n // 2))
                act.wait_ge(map_done, n + 1)
                act.mul(opT[:, n % 2], mapped[:, n % 2], p_scale[:, g:g + 1]).then_inc(opT_done, 1)
                act.wait_ge(opT_done, n + 1)
                act.dma_start(opT_dram[g * P:(g + 1) * P, tokens(i)], opT[:, n % 2]).then_inc(stored[n % 2], 16)

            def follow(i, q):
                if q >= 2:
                    finish(i, q - 2)
                if i == CHUNKS - 1:
                    for n in (2 * q, 2 * q + 1):
                        act.wait_ge(mod_summed, n + 1)
                        act.copy(rest(n * BANK, BANK), turned[:, (n % 2) * BANK:(n % 2 + 1) * BANK]).then_inc(mod_done, 1)

            square(0)
            schedule(norm=norm, project=project, project_end=take, project_first=True, pool=follow,
                     pool_end=behind(finish)["pool_end"])
            act.wait_ge(hT_done, TILES)
            for u in range(2):
                act.wait_ge(stored[u], 8 * CHUNKS * GROUPS)

        @block.gpsimd
        def _(pool):
            pool.memset(mod2[:], 0.0).then_inc(zeroed, 1)
            pool.memset(gate2[:], 0.0).then_inc(zeroed, 1)
            pool.memset(pT[:, 0, :, BANK:L], 0.0).then_inc(filled, 1)
            for j in range(PAD):
                pool.memset(inv[:, j:j + 1], 1.0 / (PAD - j)).then_inc(filled, 1)
            pool.wait_ge(bias_loaded, 32)
            steps = 0

            def add(out, a, b, op=ALU.add):
                nonlocal steps
                steps += 1
                pool.tensor_tensor(out, a, b, op).then_inc(mac_pool, 1)
                pool.wait_ge(mac_pool, steps)

            for n in range(TILES):
                pool.wait_ge(ada_loaded[2 * (n % 2) + 1], 16 * (n // 2 + 1))
                slot, half = ada[:, 2 * (n % 2) + 1], KD // 2
                add(slot, slot, c_act[:].unsqueeze(2).to_broadcast([P, KD, ADA]), ALU.mult)
                while half:
                    add(slot[:, 0:half], slot[:, 0:half], slot[:, half:2 * half])
                    half //= 2
                part = rest((2 * n + 1) * ADA, ADA)
                add(part, part, slot[:, 0])

        @block.vector
        def _(dve):
            done = 0

            def chained(ins_):
                nonlocal done
                done += 1
                ins_.then_inc(sums_done, 1)
                dve.wait_ge(sums_done, done)

            def low(out, source, high, sem):
                dve.tensor_tensor(out, source, high.bitcast(F32), ALU.subtract).then_inc(sem, 1)

            def norm(n):
                u = n % 2
                dve.wait_ge(rms_done, n + 1)
                dve.reciprocal(rstd[:, u:u + 1], rms[:, u:u + 1]).then_inc(rstd_done, 1)
                dve.wait_ge(rstd_done, n + 1)
                if n >= 2:
                    dve.wait_ge(turn_done, n - 1)
                dve.scalar_tensor_tensor(h[:, u], x[:, u], rstd[:, u:u + 1], scale, ALU.mult, ALU.mult).then_inc(scaled, 1)
                dve.wait_ge(scaled, n + 1)
                dve.tensor_tensor(h[:, u], h[:, u], shift, ALU.add).then_inc(h_done, 1)

            def sum_rows(n):
                slot = 2 * (n % 2)
                if n == 0:
                    dve.wait_ge(bias_loaded, 32)
                dve.wait_ge(ada_loaded[slot], 16 * (n // 2 + 1))
                part = rest(2 * n * ADA, ADA)
                for k in range(KD):
                    if k:
                        dve.wait_ge(mac_dve, KD * n + k)
                    dve.scalar_tensor_tensor(part, ada[:, slot, k], c_act[:, k:k + 1], part, ALU.mult, ALU.add).then_inc(mac_dve, 1)

            def norm_ahead(n):
                if n + 1 < TILES:
                    norm(n + 1)
                if n < GROUPS:
                    dve.wait_ge(w_high, n + 1)
                    low(w[1][:, n], raw[:, n], w[0][:, n], w_low)

            def project(i, q):
                for k in (2 * q, 2 * q + 1):
                    n = i * KD + k
                    dve.wait_ge(piece_high, n + 1)
                    low(piece[1][:, n % RING], hT[:, k, tokens(i)], piece[0][:, n % RING], piece_low)

            def means(i, g):
                n = i * GROUPS + g
                width = WINDOWS[g]
                if n == 0:
                    dve.wait_ge(filled, 1 + PAD)
                if g == 0:
                    dve.wait_ge(pT_done, (i + 1) * (GROUPS + 1) - 1)
                if n:
                    dve.wait_ge(mean_done, n)
                p = pT[:, i % 2, g]
                src, length = p, L
                for level in range(g + 1):
                    out = sums[:, level % 2]
                    length -= 1 << level
                    chained(dve.tensor_tensor(out[:, 0:length], src[:, 0:length], src[:, 1 << level:length + (1 << level)], ALU.add))
                    src = out
                if n >= 2:
                    dve.wait_ge(map_done, n - 1)
                m = mean[:, n % 2]
                whole = BANK - (width - 1 if i == 0 else 0)
                op = dve.scalar_tensor_tensor(m[:, 0:whole], src[:, 0:whole], 1.0 / width, p[:, 0:whole], ALU.mult, ALU.subtract)
                if i == 0:
                    chained(op)
                    chained(dve.tensor_tensor(m[:, whole:BANK], src[:, whole:BANK], inv[:, PAD - (width - 1):PAD], ALU.mult))
                    op = dve.tensor_tensor(m[:, whole:BANK], m[:, whole:BANK], p[:, whole:BANK], ALU.subtract)
                op.then_inc(mean_done, 1)

            norm(0)
            schedule(norm=norm_ahead, project=project, pool=means, sums=sum_rows, project_first=True)
            dve.wait_ge(g2_loaded, 16)
            dve.wait_ge(mod_done, 3 * D // BANK)
            scale2 = mod2[:, 2 * D:3 * D]
            dve.scalar_tensor_tensor(scale2, scale2, 1.0, g2, ALU.add, ALU.mult).then_inc(scale2_done, 1)
            dve.wait_ge(scale2_done, 1)


def attention_phase(nc, ins, const, hT, o_dram, w_loaded):
    CHUNK = BANK // P
    CHUNKS = SEQ // BANK
    RING = 3
    steps = []
    for q in range(TILES):
        for k in range(q, TILES, CHUNK):
            steps.append((q, k, min(CHUNK, TILES - k), k == q, k + CHUNK >= TILES))
    N = len(steps)
    PIECES = CHUNKS * KD
    last_step = {q: n for n, (q, _, _, _, last) in enumerate(steps) if last}
    PIECES_AT = (24, 27, 30)
    with ExitStack() as stack:
        s = Scope(nc, stack, "att")
        PARTS = ("high", "low")
        raw = s.sb("raw", [P, KD, P])
        w = [s.sb(f"w_{part}", [P, 3, KD, P], F32R) for part in PARTS]
        piece = [s.sb(f"piece_{part}", [P, RING, BANK], F32R) for part in PARTS]
        q_sides = [s.sb(f"q_sides{h}", [P, SEQ], F32R) for h in range(2)]
        k_twice = [s.sb(f"k_twice{h}", [P, SEQ], F32R) for h in range(2)]
        k_low = s.sb("k_low", [P, SEQ], F32R)
        vT = s.sb("vT", [P, SEQ + 1])
        dv = s.sb("dv", [P, TILES, P])
        stay = s.sb("stay", [P, 2, 2, BANK])
        prod = s.sb("prod", [P, 2, 2, BANK])
        dvT = prod[:, 0]
        prodT = [[s.sb(f"prodT{u}{h}", [P, BANK]) for h in range(2)] for u in range(2)]
        o = s.sb("o", [P, 2, P])
        z = s.ps("z", [P, 4, BANK])
        turned = s.ps("turned", [P, 2, BANK])
        acc = s.ps("acc", [P, 2, BANK])
        banks = ((z[:, 0], z[:, 1], z[:, 2]), (z[:, 3], turned[:, 0], turned[:, 1]))
        w0_loaded, w_high, w_low, v_pad = s.sem("w0_loaded"), s.sem("w_high"), s.sem("w_low"), s.sem("v_pad")
        piece_high, piece_low, piece_used = s.sem("piece_high"), s.sem("piece_low"), s.sem("piece_used")
        high_done, low_done = s.sem("high_done"), s.sem("low_done")
        dvT_done, dv_turned, dv_done = s.sem("dvT_done"), s.sem("dv_turned"), s.sem("dv_done")
        z_done, stay_done, prod_done = s.sem("z_done"), s.sem("stay_done"), s.sem("prod_done")
        turn_done, prodT_done, pv_done = s.sem("turn_done"), s.sem("prodT_done"), s.sem("pv_done")
        o_done, o_stored = s.sem("o_done"), s.sems("o_stored", 2)
        w_in = ins["w_in"][0].rearrange("(k p) n -> p k n", p=P)
        block = stack.enter_context(nc.Block())

        def at(g, n, h):
            return g * (2 * N) + (2 * n + h + 1)

        def side(h, other=False):
            a = HD * (1 - h if other else h)
            return slice(a, a + HD)

        @block.gpsimd
        def _(pool):
            with pool.Fori(1, PAIRS) as g:
                for j, off in enumerate((0, K_OFF, V_OFF)):
                    pool.wait_ge(w_low, g * 3 + j)
                    pool.dma_start(raw[:], w_in[:, :, ds(g * P + off, P)]).then_inc(w_loaded, 16)
                    pool.wait_ge(w_loaded, g * 48 + (16 * (j + 1) - 48))
                    pool.wait_ge(piece_used, g * PIECES + RING)
                    pool.nop(nofuse=True)
                    pool.tensor_copy(w[0][:, j], raw[:]).then_inc(w_high, 1)
                    pool.wait_ge(w_high, g * 3 + (j + 1))
                    pool.tensor_tensor(w[1][:, j], raw[:], w[0][:, j].bitcast(F32), ALU.subtract).then_inc(w_low, 1)

        @block.tensor
        def _(pe):
            pe.sem_inc(piece_used, RING)
            pe.wait_ge(v_pad, 1)
            with pe.Fori(0, PAIRS) as g:
                pe.wait_ge(w_low, g * 3 + 3)
                def turn_dv(c):
                    pe.wait_ge(dvT_done, g * CHUNKS + (c + 1))
                    if c >= 2:
                        pe.wait_ge(dv_done, g * CHUNKS + (c - 1))
                    for t in range(CHUNK):
                        mm = pe.transpose(acc[:, c % 2, t * P:(t + 1) * P], dvT[:, c % 2, t * P:(t + 1) * P], const["ident"][:])
                    mm.then_inc(dv_turned, 1)

                for c in range(CHUNKS):
                    if c >= 2:
                        pe.wait_ge(high_done, g * (7 * CHUNKS) + 7 * (c - 1))
                        pe.wait_ge(low_done, g * (4 * CHUNKS) + 4 * (c - 1))
                    for k in range(KD):
                        n = c * KD + k
                        pe.wait_ge(piece_low, g * PIECES + (n + 1))
                        for j in range(3):
                            for a, b in ((0, 0), (0, 1), (1, 0)):
                                mm = pe.matmul(banks[c % 2][j], w[a][:, j, k], piece[b][:, n % RING],
                                               start=(k == 0 and a + b == 0), stop=(k == KD - 1 and a == 1))
                        mm.then_inc(piece_used, 1)
                    if c >= 2:
                        if c == 2:
                            pe.wait_ge(o_done, g * TILES + 1)
                        turn_dv(c - 2)
                pe.wait_ge(high_done, g * (7 * CHUNKS) + 7 * (CHUNKS - 1))
                pe.wait_ge(low_done, g * (4 * CHUNKS) + 4 * (CHUNKS - 1))

                def scores(n):
                    q, k, m, _, _ = steps[n]
                    for h in range(2):
                        if n >= 2:
                            pe.wait_ge(stay_done, at(g, n - 2, h))
                        out, queries, keys = z[:, 2 * (n % 2) + h, 0:m * P], slice(q * P, (q + 1) * P), slice(k * P, (k + m) * P)
                        pe.matmul(out, q_sides[h][:, queries], k_twice[h][:, keys], start=True, stop=False)
                        pe.matmul(out, q_sides[h][side(h), queries], k_low[side(h), keys], start=False, stop=True).then_inc(z_done, 1)

                def turn(n):
                    m = steps[n][2]
                    for h in range(2):
                        pe.wait_ge(prod_done, at(g, n, h))
                        if n >= 1:
                            pe.wait_ge(prodT_done, at(g, n - 1, h))
                        for b in range(m):
                            mm = pe.transpose(turned[:, h, b * P:(b + 1) * P], prod[:, h, n % 2, b * P:(b + 1) * P],
                                              const["ident"][:])
                        mm.then_inc(turn_done, 1)

                def weigh(n):
                    q, k, m, first, last = steps[n]
                    for h in range(2):
                        if first and q:
                            pe.wait_ge(o_done, g * TILES + (q + 1))
                        pe.wait_ge(prodT_done, at(g, n, h))
                        if first:
                            pe.matmul(acc[:, h, 0:HD], vT[side(h), q * P:q * P + 1].to_broadcast([HD, P]),
                                      const["ident"][side(h), side(h)], start=True, stop=False)
                        for b in range(m):
                            mm = pe.matmul(acc[:, h, 0:HD], prodT[n % 2][h][:, b * P:(b + 1) * P],
                                           dv[:, k + b, h * HD:(h + 1) * HD], start=False, stop=(last and b == m - 1))
                        mm.then_inc(pv_done, 1)

                scores(0)
                pe.wait_ge(high_done, g * (7 * CHUNKS) + 7 * CHUNKS)
                pe.wait_ge(low_done, g * (4 * CHUNKS) + 4 * CHUNKS)
                turn_dv(CHUNKS - 2)
                turn_dv(CHUNKS - 1)
                pe.wait_ge(dv_done, g * CHUNKS + CHUNKS)
                for n in range(N):
                    if n + 1 < N:
                        scores(n + 1)
                    turn(n)
                    if n >= 1:
                        weigh(n - 1)
                weigh(N - 1)

        def projections(eng, g, split_piece, take):
            for n in range(RING, PIECES):
                if n % KD == RING and n > KD:
                    take(g, n // KD - 1)
                split_piece(g, n)
            take(g, CHUNKS - 1)

        def columns(n):
            return hT[:, n % KD, (n // KD) * BANK:(n // KD + 1) * BANK]

        @block.scalar
        def _(act):
            def split_piece(g, n):
                act.wait_ge(piece_used, g * PIECES + (n + 1))
                act.copy(piece[0][:, n % RING], columns(n)).then_inc(piece_high, 1)

            def take(g, c):
                tokens = slice(c * BANK, (c + 1) * BANK)
                act.wait_ge(piece_used, g * PIECES + (RING + KD * (c + 1)))
                q_bank, k_bank, v_bank = banks[c % 2]
                for h in range(2):
                    act.copy(q_sides[h][side(h), tokens], q_bank[side(h)]).then_inc(high_done, 1)
                for h in range(2):
                    act.copy(k_twice[h][side(h), tokens], k_bank[side(h)]).then_inc(high_done, 1)
                for h in range(2):
                    act.copy(k_twice[h][side(h, other=True), tokens], k_bank[side(h)]).then_inc(high_done, 1)
                act.copy(vT[:, tokens], v_bank).then_inc(high_done, 1)
                if c >= 2:
                    copy_dv(g, c - 2)

            def copy_dv(g, c):
                act.wait_ge(dv_turned, g * CHUNKS + (c + 1))
                act.copy(dv[:, c * CHUNK:(c + 1) * CHUNK].rearrange("p t n -> p (t n)"), acc[:, c % 2]).then_inc(dv_done, 1)

            for j, off in enumerate((0, K_OFF, V_OFF)):
                if j:
                    act.wait_ge(w_low, j)
                act.dma_start(raw[:], w_in[:, :, off:off + P]).then_inc(w0_loaded, 16)
                act.wait_ge(w0_loaded, 16 * (j + 1))
                act.copy(w[0][:, j], raw[:]).then_inc(w_high, 1)
            for n in range(RING):
                split_piece(0, n)
            with act.Fori(0, PAIRS) as g:
                projections(act, g, split_piece, take)

                def stays(n):
                    m = steps[n][2]
                    for h in range(2):
                        act.wait_ge(z_done, at(g, n, h))
                        if n >= 2:
                            act.wait_ge(prod_done, at(g, n - 2, h))
                        act.activation(stay[:, h, n % 2, 0:m * P], z[:, 2 * (n % 2) + h, 0:m * P], ACT.Sigmoid,
                                       scale=-HD ** -0.5).then_inc(stay_done, 1)

                stays(0)
                copy_dv(g, CHUNKS - 2)
                copy_dv(g, CHUNKS - 1)
                for n in range(N):
                    if n in PIECES_AT:
                        with act.If(g < PAIRS - 1):
                            split_piece(g + 1, PIECES_AT.index(n))
                    if n + 1 < N:
                        stays(n + 1)
                    m = steps[n][2]
                    for h in range(2):
                        act.wait_ge(turn_done, at(g, n, h))
                        if n >= 2:
                            act.wait_ge(pv_done, at(g, n - 2, h))
                        act.copy(prodT[n % 2][h][:, 0:m * P], turned[:, h, 0:m * P]).then_inc(prodT_done, 1)

        @block.vector
        def _(dve):
            def low(out, source, high):
                return dve.tensor_tensor(out, source, high.bitcast(F32), ALU.subtract)

            def split_piece(g, n):
                dve.wait_ge(piece_high, g * PIECES + (n + 1))
                low(piece[1][:, n % RING], columns(n), piece[0][:, n % RING]).then_inc(piece_low, 1)

            def take(g, c):
                tokens = slice(c * BANK, (c + 1) * BANK)
                q_bank, k_bank, _ = banks[c % 2]
                dve.wait_ge(high_done, g * (7 * CHUNKS) + (7 * c + 2))
                for h in range(2):
                    low(q_sides[h][side(h, other=True), tokens], q_bank[side(h)], q_sides[h][side(h), tokens]).then_inc(low_done, 1)
                dve.wait_ge(high_done, g * (7 * CHUNKS) + (7 * c + 6))
                for h in range(2):
                    low(k_low[side(h), tokens], k_bank[side(h)], k_twice[h][side(h), tokens]).then_inc(low_done, 1)

                if c >= 1:
                    step_v(g, c - 1)

            def step_v(g, c):
                dve.wait_ge(high_done, g * (7 * CHUNKS) + 7 * min(c + 2, CHUNKS))
                if c >= 2:
                    dve.wait_ge(dv_turned, g * CHUNKS + (c - 1))
                dve.tensor_tensor(dvT[:, c % 2], vT[:, c * BANK + 1:(c + 1) * BANK + 1], vT[:, c * BANK:(c + 1) * BANK],
                                  ALU.subtract).then_inc(dvT_done, 1)

            dve.sem_inc(o_done, 1)
            dve.memset(vT[:, SEQ:SEQ + 1], 0.0).then_inc(v_pad, 1)
            dve.wait_ge(v_pad, 1)
            for j in range(3):
                dve.wait_ge(w_high, j + 1)
                low(w[1][:, j], raw[:], w[0][:, j]).then_inc(w_low, 1)
            for n in range(RING):
                split_piece(0, n)
            with dve.Fori(0, PAIRS) as g:
                projections(dve, g, split_piece, take)
                step_v(g, CHUNKS - 1)
                dve.wait_ge(dv_turned, g * CHUNKS + CHUNKS)

                def copy_o(q):
                    dve.wait_ge(pv_done, at(g, last_step[q], 1))
                    dve.wait_ge(o_stored[q % 2], g * (8 * TILES) + 16 * (q // 2 + 1))
                    dve.tensor_copy(o[:, q % 2].rearrange("p (h n) -> p h n", h=2), acc[:, :, 0:HD]).then_inc(o_done, 1)

                for n, (q, k, m, first, last) in enumerate(steps):
                    if n in PIECES_AT:
                        with dve.If(g < PAIRS - 1):
                            split_piece(g + 1, PIECES_AT.index(n))
                    for h in range(2):
                        dve.wait_ge(stay_done, at(g, n, h))
                        if n >= 2:
                            dve.wait_ge(turn_done, at(g, n - 2, h))
                        start = 1.0
                        if n >= 1:
                            dve.wait_ge(prod_done, at(g, n - 1, h))
                        if not first:
                            start = prod[:, h, (n - 1) % 2, BANK - 1:BANK]
                        mask = const["causal"][:, 0:m * P] if first else const["causal"][:, P:P + 1].to_broadcast([P, m * P])
                        dve.tensor_tensor_scan(prod[:, h, n % 2, 0:m * P], stay[:, h, n % 2, 0:m * P], mask, start,
                                               ALU.mult, ALU.max).then_inc(prod_done, 1)
                    for q_done, n_done in last_step.items():
                        if n_done == n - 2:
                            copy_o(q_done)
                for q_done, n_done in last_step.items():
                    if n_done >= N - 2:
                        copy_o(q_done)

        @block.sync
        def _(sp):
            sp.sem_inc(o_stored[0], 16)
            sp.sem_inc(o_stored[1], 16)
            with sp.Fori(0, PAIRS) as g:
                for q in range(TILES):
                    sp.wait_ge(o_done, g * TILES + (q + 2))
                    sp.dma_start(o_dram[q * P:(q + 1) * P, ds(g * P, P)], o[:, q % 2]).then_inc(o_stored[q % 2], 16)
            for u in range(2):
                sp.wait_ge(o_stored[u], 16 + 8 * TILES * PAIRS)


def branches_phase(nc, ins, const, hT, o_dram, opT_dram, mT_dram):
    NB, TB, KS = SEQ // BANK, BANK // P, SBW // P
    UNITS = 2 * KD
    with ExitStack() as stack:
        s = Scope(nc, stack, "mix")
        PARTS = ("high", "low")
        raw_g, raw_b = s.sb("raw_g", [P, 2, KD, P]), s.sb("raw_b", [P, 2, KS, P])
        wg = [[s.sb(f"wg{j}_{part}", [P, KD, P], F32R) for part in PARTS] for j in range(2)]
        wb = [[s.sb(f"wb{j}_{part}", [P, KS, P], F32R) for part in PARTS] for j in range(2)]
        o, op = s.sb("o", [P, 2, SBW]), s.sb("op", [P, 2, BANK])
        hTb = [s.sb(f"hT_{part}", [P, KD, BANK], F32R) for part in PARTS]
        oT = [s.sb(f"oT_{part}", [P, KS, BANK], F32R) for part in PARTS]
        opT = [s.sb(f"opT_{part}", [P, KS, BANK], F32R) for part in PARTS]
        gate, part = s.sb("gate", [P, 2, BANK]), s.sb("part", [P, 2, BANK])
        mT = s.sb("mT", [P, BANK])
        gate_ps, branch_ps, turned = s.ps("gate_ps", [P, 2, BANK]), s.ps("branch_ps", [P, 2, BANK]), s.ps("turned", [P, 2, BANK])
        w_loaded, o_loaded, op_loaded, stored = s.sems("w_loaded", 2), s.sems("o_loaded", 2), s.sems("op_loaded", 2), s.sem("stored")
        w_high, wg_low, w_low = s.sem("w_high"), s.sem("wg_low"), s.sem("w_low")
        hT_high, hT_low, oT_high, oT_low = s.sem("hT_high"), s.sem("hT_low"), s.sem("oT_high"), s.sem("oT_low")
        opT_high, opT_low = s.sem("opT_high"), s.sem("opT_low")
        turn_done, gate_mm, branch_mm = s.sem("turn_done"), s.sem("gate_mm"), s.sem("branch_mm")
        gate_done, part_done, mT_done = s.sem("gate_done"), s.sem("part_done"), s.sem("mT_done")
        w_in = ins["w_in"][0].rearrange("(k p) n -> p k n", p=P)
        w_sb = ins["w_branch_sb"][0].rearrange("(k p) n -> p k n", p=P)
        w_pl = ins["w_branch_pool"][0].rearrange("(k p) n -> p k n", p=P)
        block = stack.enter_context(nc.Block())

        @block.sync
        def _(sp):
            with sp.Fori(0, NB) as b:
                with sp.Fori(0, KD) as d:
                    for j, (off, wbr) in enumerate(((GS_OFF, w_sb), (GP_OFF, w_pl))):
                        sp.wait_ge(w_low, b * UNITS + 2 * d + (j + 1))
                        sp.dma_start(raw_g[:, j], w_in[:, :, ds(d * P + off, P)]).then_inc(w_loaded[j], 16)
                        sp.dma_start(raw_b[:, j], wbr[:, :, ds(d * P, P)]).then_inc(w_loaded[j], 16)

        @block.gpsimd
        def _(pool):
            with pool.Fori(0, NB) as b:
                for t in range(TB):
                    pool.wait_ge(turn_done, b * TB + (t + 1))
                    pool.dma_start(o[:, t % 2], o_dram[ds(b * BANK + t * P, P), :]).then_inc(o_loaded[t % 2], 16)
                for k in range(KS):
                    pool.wait_ge(opT_low, b * KS + (k + 1))
                    pool.dma_start(op[:, k % 2], opT_dram[k * P:(k + 1) * P, ds(b * BANK, BANK)]).then_inc(op_loaded[k % 2], 16)

        @block.tensor
        def _(pe):
            def product(to, w, x, blocks, before=None):
                for k in range(blocks):
                    if before:
                        before(k)
                    pe.matmul(to, w[0][:, k], x[0][:, k], start=(k == 0), stop=False)
                    pe.matmul(to, w[0][:, k], x[1][:, k], start=False, stop=False)
                    mm = pe.matmul(to, w[1][:, k], x[0][:, k], start=False, stop=(k == blocks - 1))
                return mm

            def unit(b, d, j, first, between=None):
                n = b * UNITS + 2 * d + j
                pe.wait_ge(w_low, n + 3)
                pe.wait_ge(gate_done, n + 1)
                before = (lambda k: pe.wait_ge(hT_low, b * KD + (k + 1))) if first and j == 0 else None
                product(gate_ps[:, j], wg[j], hTb, KD, before).then_inc(gate_mm, 1)
                if between:
                    between(b)
                pe.wait_ge(part_done, n + 1)
                if first:
                    pe.wait_ge((oT_low, opT_low)[j], b * KS + (TB + (0, 2)[j]))
                product(branch_ps[:, j], wb[j], (oT, opT)[j], KS).then_inc(branch_mm, 1)

            pe.sem_inc(turn_done, 2)
            pe.sem_inc(branch_mm, 2)
            pe.sem_inc(gate_mm, 1)
            def turn(b):
                for t in range(TB):
                    pe.wait_ge(o_loaded[t % 2], b * (8 * TB) + 16 * (t // 2 + 1))
                    if t >= 2:
                        pe.wait_ge(oT_low, b * TB + (t - 1))
                    for k in range(KS):
                        mm = pe.transpose(turned[:, t % 2, k * P:(k + 1) * P], o[:, t % 2, k * P:(k + 1) * P], const["ident"][:])
                    mm.then_inc(turn_done, 1)

            with pe.Fori(0, NB) as b:
                unit(b, 0, 0, True, between=turn)
                unit(b, 0, 1, True)
                with pe.Fori(1, KD) as d:
                    for j in range(2):
                        unit(b, d, j, False)

        def all_units(eng, split_hT, start, unit, split, finish, hT_before):
            def tokens(b, more):
                start(b)
                with eng.Fori(0, KD - 1) as d:
                    for j in range(2):
                        unit(b, d, j)
                        split(b * UNITS + 2 * d + (j + 2), j, b * KD + d + 1)
                    finish(b, d)
                unit(b, KD - 1, 0)
                if not hT_before:
                    unit(b, KD - 1, 1)
                if more:
                    split_hT(b + 1)
                    split(b * UNITS + UNITS, 0, b * KD + KD)
                if hT_before:
                    unit(b, KD - 1, 1)
                if more:
                    split(b * UNITS + (UNITS + 1), 1, b * KD + KD)
                finish(b, KD - 1)

            split_hT(0)
            with eng.Fori(0, NB - 1) as b:
                tokens(b, True)
            tokens(NB - 1, False)

        def columns(b, k):
            return hT[:, k, b * BANK:(b + 1) * BANK] if isinstance(b, int) else hT[:, k, ds(b * BANK, BANK)]

        @block.scalar
        def _(act):
            def split(n, j, i):
                act.wait_ge(w_loaded[j], i * 32 + 32)
                act.wait_ge(branch_mm, n + 1)
                act.copy(wg[j][0][:], raw_g[:, j]).then_inc(w_high, 1)
                act.copy(wb[j][0][:], raw_b[:, j]).then_inc(w_high, 1)

            def split_hT(b):
                act.wait_ge(gate_mm, b * UNITS + 1)
                for k in range(KD):
                    act.copy(hTb[0][:, k], columns(b, k)).then_inc(hT_high, 1)

            def start(b):
                act.wait_ge(branch_mm, b * UNITS + 2)
                for t in range(TB):
                    act.wait_ge(turn_done, b * TB + (t + 3))
                    act.copy(oT[0][:, :, t * P:(t + 1) * P], turned[:, t % 2].rearrange("p (k t) -> p k t", k=KS)).then_inc(oT_high, 1)
                for k in range(KS):
                    act.wait_ge(op_loaded[k % 2], b * (8 * KS) + 16 * (k // 2 + 1))
                    act.copy(opT[0][:, k], op[:, k % 2]).then_inc(opT_high, 1)

            def unit(b, d, j):
                n = b * UNITS + 2 * d + j
                act.wait_ge(gate_mm, n + 2)
                act.wait_ge(part_done, n + 1)
                act.activation(gate[:, j], gate_ps[:, j], ACT.Sigmoid).then_inc(gate_done, 1)

            def finish(b, d):
                act.wait_ge(mT_done, b * KD + d + 2)
                act.dma_start(mT_dram[ds(d * P, P) if not isinstance(d, int) else slice(d * P, (d + 1) * P), ds(b * BANK, BANK)],
                              mT[:]).then_inc(stored, 16)

            act.sem_inc(stored, 16)
            act.sem_inc(gate_done, 2)
            for j in range(2):
                split(j, j, 0)
            all_units(act, split_hT, start, unit, split, finish, False)
            act.wait_ge(stored, 16 + 16 * KD * NB)

        @block.vector
        def _(dve):
            def low(out, source, high, done):
                dve.tensor_tensor(out, source, high.bitcast(F32), ALU.subtract).then_inc(done, 1)

            def split(n, j, i):
                dve.wait_ge(w_high, 2 * n + 1)
                dve.tensor_tensor(wg[j][1][:], raw_g[:, j], wg[j][0][:].bitcast(F32), ALU.subtract).then_inc(wg_low, 1)
                dve.wait_ge(w_high, 2 * n + 2)
                dve.wait_ge(wg_low, n + 1)
                dve.tensor_tensor(wb[j][1][:], raw_b[:, j], wb[j][0][:].bitcast(F32), ALU.subtract).then_inc(w_low, 1)

            def split_hT(b):
                for k in range(KD):
                    dve.wait_ge(hT_high, b * KD + (k + 1))
                    low(hTb[1][:, k], columns(b, k), hTb[0][:, k], hT_low)

            def start(b):
                for t in range(TB):
                    dve.wait_ge(oT_high, b * TB + (t + 1))
                    low(oT[1][:, :, t * P:(t + 1) * P], turned[:, t % 2].rearrange("p (k t) -> p k t", k=KS),
                        oT[0][:, :, t * P:(t + 1) * P], oT_low)
                for k in range(KS):
                    dve.wait_ge(opT_high, b * KS + (k + 1))
                    low(opT[1][:, k], op[:, k % 2], opT[0][:, k], opT_low)

            def unit(b, d, j):
                n = b * UNITS + 2 * d + j
                dve.wait_ge(gate_done, n + 3)
                dve.wait_ge(branch_mm, n + 3)
                dve.wait_ge(mT_done, b * KD + d + 1)
                dve.tensor_tensor(part[:, j], gate[:, j], branch_ps[:, j], ALU.mult).then_inc(part_done, 1)
                if j == 1:
                    dve.wait_ge(part_done, n + 3)
                    dve.wait_ge(stored, b * (16 * KD) + d * 16 + 16)
                    dve.tensor_tensor(mT[:], part[:, 0], part[:, 1], ALU.add).then_inc(mT_done, 1)

            dve.sem_inc(w_low, 2)
            dve.sem_inc(opT_low, 2)
            dve.sem_inc(part_done, 2)
            dve.sem_inc(mT_done, 1)
            for j in range(2):
                split(j, j, 0)
            all_units(dve, split_hT, start, unit, split, lambda b, d: None, True)


def output_phase(nc, ins, const, mod2, logits, mT_dram, x2_dram, h2_dram):
    with ExitStack() as stack:
        s = Scope(nc, stack, "out")
        PARTS = ("high", "low")
        raw_w = s.sb("raw_w", [P, 2, D])
        w = [s.sb(f"w_{part}", [P, KD, D], F32R) for part in PARTS]
        raw_m = s.sb("raw_m", [P, 2, KD, P])
        mT = [[s.sb(f"mT{u}_{part}", [P, KD, P], F32R) for part in PARTS] for u in range(2)]
        x, h, scaled_out = s.sb("x", [P, 2, D]), s.sb("h", [P, 2, D]), s.sb("scaled_out", [P, D])
        hT = [s.sb(f"hT{u}", [P, KD, P]) for u in range(2)]
        wr = s.sb("wr", [P, KD, EG + NE])
        bias = s.sb("bias", [P, EG + NE])
        junk = s.sb("junk", [P, D])
        ssq, rms, rstd = s.sb("ssq", [P, 2]), s.sb("rms", [P, 2]), s.sb("rstd", [P, 2])
        proj = s.ps("proj", [P, 2, D])
        turned = s.ps("turned", [P, KD * P])
        routed = s.ps("routed", [P, 2, BANK])
        w_loaded, m_loaded, x_loaded, wr_loaded = s.sems("w_loaded", 2), s.sems("m_loaded", 2), s.sems("x_loaded", 2), s.sem("wr_loaded")
        w_high, w_low, m_high, m_low = s.sem("w_high"), s.sem("w_low"), s.sem("m_high"), s.sem("m_low")
        x2_stored, h_stored = s.sems("x2_stored", 2), s.sems("h_stored", 2)
        proj_done, gate_done, x2_done = s.sem("proj_done"), s.sem("gate_done"), s.sem("x2_done")
        ssq_done, rms_done, rstd_done, h_done = s.sem("ssq_done"), s.sem("rms_done"), s.sem("rstd_done"), s.sem("h_done")
        normed, turn_done, hT_done, route_done, logits_done = (s.sem("normed"), s.sem("turn_done"), s.sem("hT_done"),
                                                               s.sem("route_done"), s.sem("logits_done"))
        gate1, shift, scale = mod2[:, 0:D], mod2[:, D:2 * D], mod2[:, 2 * D:3 * D]
        w_out = ins["w_out"][0].rearrange("(k p) n -> p k n", p=P)
        merged = mT_dram.rearrange("(k p) t -> p k t", p=P)
        block = stack.enter_context(nc.Block())

        @block.gpsimd
        def _(pool):
            def load(i, u):
                pool.wait_ge(m_low, 2 * i + (u + 1))
                pool.dma_start(raw_m[:, u], merged[:, :, ds(i * (2 * P) + u * P, P)]).then_inc(m_loaded[u], 16)
                pool.wait_ge(normed, 2 * i + (u + 1))
                pool.wait_ge(x2_stored[u], i * 16 + 16)
                pool.dma_start(x[:, u], ins["x"][0, ds(i * (2 * P) + u * P, P), :]).then_inc(x_loaded[u], 16)

            with pool.Fori(0, TILES // 2) as i:
                for u in range(2):
                    load(i, u)

        @block.sync
        def _(sp):
            for k in range(KD):
                if k >= 2:
                    sp.wait_ge(w_low, k - 1)
                sp.dma_start(raw_w[:, k % 2], w_out[:, k]).then_inc(w_loaded[k % 2], 16)
            sp.dma_start(wr[:, :, 0:EG], ins["w_route_group"][0].rearrange("(k p) n -> p k n", p=P)).then_inc(wr_loaded, 16)
            for g in range(EG):
                sp.dma_start(wr[:, :, EG + g * EPG:EG + (g + 1) * EPG],
                             ins["w_route_expert"][0, g].rearrange("(k p) n -> p k n", p=P)).then_inc(wr_loaded, 16)
            sp.dma_start(bias[:, 0:EG], ins["b_route_group"][0:1].partition_broadcast(P)).then_inc(wr_loaded, 16)
            sp.dma_start(bias[:, EG:], ins["b_route_expert"][0:1].rearrange("a g e -> a (g e)").partition_broadcast(P)).then_inc(wr_loaded, 16)
            for u in range(2):
                sp.sem_inc(x2_stored[u], 16)
                sp.sem_inc(h_stored[u], 16)
            with sp.Fori(0, TILES // 2) as i:
                for u in range(2):
                    sp.wait_ge(x2_done, 2 * i + (u + 2))
                    sp.dma_start(x2_dram[ds(i * (2 * P) + u * P, P), :], x[:, u]).then_inc(x2_stored[u], 16)
                    sp.wait_ge(h_done, 2 * i + (u + 1))
                    sp.dma_start(h2_dram[ds(i * (2 * P) + u * P, P), :], h[:, u]).then_inc(h_stored[u], 16)
            for u in range(2):
                sp.wait_ge(x2_stored[u], 16 + 8 * TILES)
                sp.wait_ge(h_stored[u], 16 + 8 * TILES)

        @block.tensor
        def _(pe):
            def project(i, u, first=False):
                pe.wait_ge(m_low, 2 * i + (u + 3))
                pe.wait_ge(gate_done, 2 * i + (u + 1))
                for k in range(KD):
                    if first:
                        pe.wait_ge(w_low, k + 1)
                    for a, b in ((0, 0), (0, 1), (1, 0)):
                        for c in range(D // BANK):
                            mm = pe.matmul(proj[:, u, c * BANK:(c + 1) * BANK], mT[u][a][:, k], w[b][:, k, c * BANK:(c + 1) * BANK],
                                           start=(k == 0 and a + b == 0), stop=(k == KD - 1 and a == 1))
                mm.then_inc(proj_done, 1)

            def turn(i, u):
                pe.wait_ge(h_done, 2 * i + (u + 1))
                pe.wait_ge(hT_done, 2 * i + (u + 1))
                for k in range(KD):
                    mm = pe.transpose(turned[:, k * P:(k + 1) * P], h[:, u, k * P:(k + 1) * P], const["ident"][:])
                mm.then_inc(turn_done, 1)

            def route(i, u):
                pe.wait_ge(hT_done, 2 * i + (u + 2))
                pe.wait_ge(logits_done, 2 * i + (u + 1))
                for k in range(KD):
                    mm = pe.matmul(routed[:, u, 0:EG + NE], hT[u][:, k], wr[:, k], start=(k == 0), stop=(k == KD - 1))
                mm.then_inc(route_done, 1)

            for sem in (proj_done, turn_done, route_done):
                pe.sem_inc(sem, 2)
            project(0, 0, first=True)
            project(0, 1)
            turn(0, 0)
            pe.wait_ge(wr_loaded, 16 * (EG + 3))
            with pe.Fori(1, TILES // 2) as i:
                project(i, 0)
                turn(i - 1, 1)
                route(i - 1, 0)
                project(i, 1)
                turn(i, 0)
                route(i - 1, 1)
            turn(TILES // 2 - 1, 1)
            route(TILES // 2 - 1, 0)
            route(TILES // 2 - 1, 1)

        @block.scalar
        def _(act):
            def split(i, u):
                act.wait_ge(m_loaded[u], i * 16 + 16)
                act.wait_ge(proj_done, 2 * i + (u + 1))
                act.copy(mT[u][0][:], raw_m[:, u]).then_inc(m_high, 1)

            def square(i, u):
                act.wait_ge(x2_done, 2 * i + (u + 2))
                act.activation(junk[:], x[:, u], ACT.Square, accum_out=ssq[:, u:u + 1]).then_inc(ssq_done, 1)
                act.wait_ge(ssq_done, 2 * i + (u + 1))
                act.activation(rms[:, u:u + 1], ssq[:, u:u + 1], ACT.Sqrt, bias=const["eps"][:],
                               scale=1.0 / D).then_inc(rms_done, 1)

            def copy_hT(i, u):
                act.wait_ge(turn_done, 2 * i + (u + 3))
                act.wait_ge(route_done, 2 * i + (u + 1))
                act.copy(hT[u][:].rearrange("p k t -> p (k t)"), turned[:]).then_inc(hT_done, 1)

            act.sem_inc(hT_done, 1)
            split(0, 0)
            for k in range(KD):
                act.wait_ge(w_loaded[k % 2], 16 * (k // 2 + 1))
                act.copy(w[0][:, k], raw_w[:, k % 2]).then_inc(w_high, 1)
            split(0, 1)
            square(0, 0)
            split(1, 0)
            with act.Fori(0, TILES // 2 - 2) as i:
                square(i, 1)
                copy_hT(i, 0)
                split(i + 1, 1)
                square(i + 1, 0)
                copy_hT(i, 1)
                split(i + 2, 0)
            i = TILES // 2 - 2
            square(i, 1)
            copy_hT(i, 0)
            split(i + 1, 1)
            square(i + 1, 0)
            copy_hT(i, 1)
            square(i + 1, 1)
            copy_hT(i + 1, 0)
            copy_hT(i + 1, 1)

        @block.vector
        def _(dve):
            def low(out, source, high, done):
                dve.tensor_tensor(out, source, high.bitcast(F32), ALU.subtract).then_inc(done, 1)

            def split(i, u):
                dve.wait_ge(m_high, 2 * i + (u + 1))
                low(mT[u][1][:], raw_m[:, u], mT[u][0][:], m_low)

            def add(i, u):
                dve.wait_ge(proj_done, 2 * i + (u + 3))
                dve.wait_ge(x2_done, 2 * i + (u + 1))
                dve.tensor_tensor(scaled_out[:], proj[:, u], gate1, ALU.mult).then_inc(gate_done, 1)
                dve.wait_ge(gate_done, 2 * i + (u + 3))
                dve.wait_ge(x_loaded[u], i * 16 + 16)
                dve.tensor_tensor(x[:, u], x[:, u], scaled_out[:], ALU.add).then_inc(x2_done, 1)

            def normalise(i, u):
                dve.wait_ge(rms_done, 2 * i + (u + 1))
                dve.reciprocal(rstd[:, u:u + 1], rms[:, u:u + 1]).then_inc(rstd_done, 1)
                dve.wait_ge(rstd_done, 2 * i + (u + 1))
                dve.wait_ge(turn_done, 2 * i + (u + 1))
                dve.wait_ge(h_stored[u], i * 16 + 16)
                dve.scalar_tensor_tensor(h[:, u], x[:, u], rstd[:, u:u + 1], scale, ALU.mult, ALU.mult).then_inc(normed, 1)
                dve.wait_ge(normed, 2 * i + (u + 3))
                dve.tensor_tensor(h[:, u], h[:, u], shift, ALU.add).then_inc(h_done, 1)

            def take(i, u):
                dve.wait_ge(route_done, 2 * i + (u + 3))
                dve.tensor_tensor(logits[:, ds(2 * i + u, 1), :].rearrange("p a n -> p (a n)"), routed[:, u, 0:EG + NE],
                                  bias[:], ALU.add).then_inc(logits_done, 1)

            dve.sem_inc(m_low, 2)
            dve.sem_inc(gate_done, 2)
            dve.sem_inc(x2_done, 1)
            dve.sem_inc(normed, 2)
            dve.sem_inc(logits_done, 2)
            split(0, 0)
            for k in range(KD):
                dve.wait_ge(w_high, k + 1)
                low(w[1][:, k], raw_w[:, k % 2], w[0][:, k], w_low)
            split(0, 1)
            dve.wait_ge(wr_loaded, 16 * (EG + 3))
            add(0, 0)
            normalise(0, 0)
            split(1, 0)
            add(0, 1)
            normalise(0, 1)
            split(1, 1)
            with dve.Fori(1, TILES // 2 - 1) as i:
                add(i, 0)
                normalise(i, 0)
                split(i + 1, 0)
                take(i - 1, 0)
                add(i, 1)
                normalise(i, 1)
                split(i + 1, 1)
                take(i - 1, 1)
            i = TILES // 2 - 1
            add(i, 0)
            normalise(i, 0)
            take(i - 1, 0)
            add(i, 1)
            normalise(i, 1)
            take(i - 1, 1)
            take(i, 0)
            take(i, 1)
            dve.wait_ge(logits_done, 2 + TILES)


def dispatch_phase(nc, const, logits, weight, slot, tables):
    T = TILES
    with ExitStack() as stack:
        s = Scope(nc, stack, "dsp")
        gl, el = logits[:, :, 0:EG], logits[:, :, EG:].rearrange("p t (g e) -> p t g e", g=EG)
        gmax, gsum, p_group, index = s.sb("gmax", [P, T, 1]), s.sb("gsum", [P, T, 1]), s.sb("p_group", [P, T, 1]), s.sb("index", [P, T, 1])
        tmp4, g_hot = s.sb("tmp4", [P, T, EG]), s.sb("g_hot", [P, T, EG])
        inner, tmp8 = s.sb("inner", [P, T, EPG]), s.sb("tmp8", [P, T, EPG])
        e_hot = s.sb("e_hot", [P, 2, T, EPG])
        best = s.sb("best", [P, 2, T, 1])
        gap = s.sb("gap", [P, 2, T])
        hot = s.sb("hot", [P, 2, T, NE])
        either, earlier = s.sb("either", [P, T, NE]), s.sb("earlier", [P, T + 1, NE])
        place, picked = s.sb("place", [P, T, NE]), s.sb("picked", [P, 2, T, NE])
        count_i, filled_i = s.sb("count_i", [P, NE], I32), s.sb("filled_i", [P, NE], I32)
        filled, end, base = s.sb("filled", [P, NE]), s.sb("end", [P, NE]), s.sb("base", [P, NE])
        slot_f = s.sb("slot_f", [P, 2, T])
        over = s.sb("over", [P, BLOCKS, NE])
        expert_f, new_f, ordinal_f = s.sb("expert_f", [P, BLOCKS]), s.sb("new_f", [P, BLOCKS]), s.sb("ordinal_f", [P, BLOCKS])
        slot_block, slot_block_f, slot_place = s.sb("slot_block", [P, 2, T], U32), s.sb("slot_block_f", [P, 2, T]), s.sb("slot_place", [P, 2, T])
        token = s.sb("token", [P, T])
        place_hot, block_hot = s.sb("place_hot", [P, 2, T, P]), s.sb("block_hot", [P, 2, T, BLOCKS + 1])
        rank, total = s.ps("rank", [P, BANK]), s.ps("total", [P, BANK])
        slot_rows = s.ps("slot_rows", [P, BANK])
        done, exp_done, weight_done, ranked, rows_found = (s.sem("done"), s.sem("exp_done"), s.sem("weight_done"),
                                                           s.sem("ranked"), s.sem("rows_found"))
        at = {}
        count = [0]
        block = stack.enter_context(nc.Block())

        @block.vector
        def _(dve):
            def step(ins_, name=None):
                count[0] += 1
                ins_.then_inc(done, 1)
                dve.wait_ge(done, count[0])
                if name:
                    at[name] = count[0]

            def first_best(values, top, n, hot_out):
                tmp = (tmp4 if n == EG else tmp8)[:]
                step(dve.tensor_tensor(tmp, values, top.to_broadcast([P, T, n]), ALU.is_equal))
                places = const["iota"][:, 0:n].unsqueeze(1).to_broadcast([P, T, n])
                step(dve.scalar_tensor_tensor(hot_out, places, -float(n), tmp, ALU.add, ALU.mult))
                step(dve.tensor_reduce(index[:], hot_out, AX_X, ALU.min))
                step(dve.tensor_scalar(index[:], index[:], float(n), None, ALU.add))
                step(dve.tensor_tensor(hot_out, places, index[:].to_broadcast([P, T, n]), ALU.is_equal))

            step(dve.tensor_copy(token[:], const["rows"][:]))
            step(dve.tensor_reduce(gmax[:], gl, AX_X, ALU.max))
            step(dve.tensor_tensor(tmp4[:], gl, gmax[:].to_broadcast([P, T, EG]), ALU.subtract), "group_gap")
            dve.wait_ge(exp_done, 1)
            step(dve.tensor_reduce(gsum[:], tmp4[:], AX_X, ALU.add))
            step(dve.reciprocal(p_group[:], gsum[:]))
            first_best(gl, gmax[:], EG, g_hot[:])
            step(dve.tensor_tensor(inner[:], el[:, :, 0], g_hot[:, :, 0:1].to_broadcast([P, T, EPG]), ALU.mult))
            for g in range(1, EG):
                step(dve.tensor_tensor(tmp8[:], el[:, :, g], g_hot[:, :, g:g + 1].to_broadcast([P, T, EPG]), ALU.mult))
                step(dve.tensor_tensor(inner[:], inner[:], tmp8[:], ALU.add))
            for j in range(2):
                step(dve.tensor_reduce(best[:, j], inner[:], AX_X, ALU.max))
                first_best(inner[:], best[:, j], EPG, e_hot[:, j])
                if j == 0:
                    step(dve.scalar_tensor_tensor(inner[:], e_hot[:, 0], -1e30, inner[:], ALU.mult, ALU.add))
            for j in range(2):
                step(dve.tensor_tensor(gap[:, j], best[:, j, :, 0], best[:, 1 - j, :, 0], ALU.subtract), "best_gap")
            for j in range(2):
                for g in range(EG):
                    step(dve.tensor_tensor(hot[:, j, :, g * EPG:(g + 1) * EPG], e_hot[:, j],
                                           g_hot[:, :, g:g + 1].to_broadcast([P, T, EPG]), ALU.mult))
            step(dve.tensor_tensor(either[:], hot[:, 0], hot[:, 1], ALU.add))
            step(dve.memset(earlier[:, 0], 0.0))
            for t in range(T):
                step(dve.tensor_tensor(earlier[:, t + 1], earlier[:, t], either[:, t], ALU.add), "counted")
            dve.wait_ge(weight_done, 1)
            for j in range(2):
                step(dve.tensor_tensor(weight[:, j], gap[:, j], p_group[:, :, 0], ALU.mult))
            dve.wait_ge(ranked, 1)
            step(dve.tensor_scalar(count_i[:], total[:, 0:NE], float(P - 1), None, ALU.add))
            step(dve.tensor_scalar(filled_i[:], count_i[:], 7, None, ALU.arith_shift_right))
            step(dve.tensor_copy(filled[:], filled_i[:]))
            zero = const["causal"][:, P:P + 1]
            step(dve.tensor_tensor_scan(end[:], filled[:], zero.to_broadcast([P, NE]), 0.0, ALU.add, ALU.add))
            step(dve.tensor_tensor(base[:], end[:], filled[:], ALU.subtract))
            step(dve.scalar_tensor_tensor(place[:], base[:].unsqueeze(1).to_broadcast([P, T, NE]), float(P),
                                          rank[:].rearrange("p (t e) -> p t e", t=T), ALU.mult, ALU.add))
            for j in range(2):
                step(dve.tensor_tensor(picked[:, j], place[:], hot[:, j], ALU.mult))
                step(dve.tensor_reduce(slot_f[:, j].unsqueeze(2), picked[:, j], AX_X, ALU.add))
                step(dve.tensor_copy(slot[:, j], slot_f[:, j]))
                step(dve.tensor_scalar(slot_block[:, j], slot[:, j], 7, None, ALU.arith_shift_right))
                step(dve.tensor_copy(slot_block_f[:, j], slot_block[:, j]))
                step(dve.scalar_tensor_tensor(slot_place[:, j], slot_block_f[:, j], -float(P), slot_f[:, j], ALU.mult, ALU.add))
                step(dve.tensor_tensor(place_hot[:, j], const["iota"][:].unsqueeze(1).to_broadcast([P, T, P]),
                                       slot_place[:, j].unsqueeze(2).to_broadcast([P, T, P]), ALU.is_equal))
                step(dve.tensor_tensor(block_hot[:, j], const["iota"][:, 0:BLOCKS + 1].unsqueeze(1).to_broadcast([P, T, BLOCKS + 1]),
                                       slot_block_f[:, j].unsqueeze(2).to_broadcast([P, T, BLOCKS + 1]), ALU.is_equal))
                step(dve.tensor_tensor(block_hot[:, j], block_hot[:, j], token[:].unsqueeze(2).to_broadcast([P, T, BLOCKS + 1]),
                                       ALU.mult), f"hot{j}")
            n = BLOCKS
            step(dve.tensor_tensor(over[:], end[:].unsqueeze(1).to_broadcast([P, n, NE]),
                                   const["iota"][:, 0:n].unsqueeze(2).to_broadcast([P, n, NE]), ALU.is_le))
            step(dve.tensor_reduce(expert_f[:].unsqueeze(2), over[:], AX_X, ALU.add))
            step(dve.tensor_scalar(expert_f[:], expert_f[:], float(NE - 1), None, ALU.min))
            step(dve.tensor_copy(tables["expert"][:, 0:n], expert_f[:]))
            step(dve.memset(new_f[:], 1.0))
            step(dve.tensor_tensor(new_f[:, 1:n], expert_f[:, 1:n], expert_f[:, 0:n - 1], ALU.not_equal))
            step(dve.scalar_tensor_tensor(new_f[:], const["iota"][:, 0:n], end[:, NE - 1:NE], new_f[:], ALU.is_lt, ALU.mult))
            for name in ("expert", "new", "ordinal"):
                step(dve.memset(tables[name][:, n:n + 1], 0))
            step(dve.tensor_copy(tables["new"][:, 0:n], new_f[:]))
            step(dve.tensor_tensor_scan(ordinal_f[:], new_f[:], zero.to_broadcast([P, n]), 0.0, ALU.add, ALU.add))
            step(dve.tensor_copy(tables["ordinal"][:, 0:n], ordinal_f[:]))
            step(dve.tensor_scalar(count_i[:, 0:1], end[:, NE - 1:NE], -1.0, None, ALU.add))
            step(dve.tensor_scalar(tables["blocks"][:, 0:1], count_i[:, 0:1], 1, None, ALU.arith_shift_right))
            step(dve.tensor_scalar(tables["blocks"][:, 1:2], tables["blocks"][:, 0:1], -2.0, BLOCKS - 2.0, ALU.mult, ALU.add))
            dve.wait_ge(rows_found, 1)
            step(dve.tensor_copy(tables["rows"][:], slot_rows[:, 0:BLOCKS + 1]))

        @block.scalar
        def _(act):
            act.wait_ge(done, at["group_gap"])
            act.activation(tmp4[:], tmp4[:], ACT.Exp).then_inc(exp_done, 1)
            act.wait_ge(done, at["best_gap"])
            act.activation(gap[:], gap[:], ACT.Sigmoid).then_inc(weight_done, 1)

        @block.tensor
        def _(pe):
            pe.wait_ge(done, at["counted"])
            pe.matmul(rank[:], const["before"][:], either[:].rearrange("p t e -> p (t e)"), start=True, stop=False)
            pe.matmul(rank[:], const["ones"][:], earlier[:, 0:T].rearrange("p t e -> p (t e)"), start=False, stop=True)
            pe.matmul(total[:, 0:NE], const["ones"][:], earlier[:, T], start=True, stop=True).then_inc(ranked, 1)
            for j in range(2):
                pe.wait_ge(done, at[f"hot{j}"])
                for t in range(T):
                    mm = pe.matmul(slot_rows[:, 0:BLOCKS + 1], place_hot[:, j, t], block_hot[:, j, t],
                                   start=(j == 0 and t == 0), stop=(j == 1 and t == T - 1))
            mm.then_inc(rows_found, 1)


def experts_phase(nc, ins, const, gate2, tables, h2_dram, y_dram):
    ZERO_COLS = 256
    HALF = KD * F // 2
    PIECES = 6
    GATE, UP, DOWN = (0, 1), (2, 3), (4, 5)
    ON_POOL = (3, 5)
    with ExitStack() as stack:
        s = Scope(nc, stack, "moe")
        raw = s.sb("raw", [P, PIECES, HALF])
        high, low = s.sb("high", [P, PIECES, HALF], F32R), s.sb("low", [P, PIECES, HALF], F32R)
        row = [s.sb(f"row{u}", [P, 1], U32) for u in range(2)]
        h = [s.sb(f"h{u}", [P, D]) for u in range(2)]
        hT = [[s.sb(f"hT{u}_{part}", [P, KD, P], F32R) for part in ("high", "low")] for u in range(2)]
        sig, gated, act_h = s.sb("sig", [P, F]), s.sb("gated", [P, F]), s.sb("act_h", [P, F])
        act_hT = [s.sb(f"act_hT_{part}", [P, KF, P], F32R) for part in ("high", "low")]
        y = s.sb("y", [P, 2, D])
        zero = s.sb("zero", [P, ZERO_COLS])
        gate, up = s.ps("gate", [P, BANK]), s.ps("up", [P, BANK])
        turned = s.ps("turned", [P, KD * P])
        turned2 = s.ps("turned2", [P, BANK])
        down = s.ps("down", [P, D])
        row_set = s.sem("row_set")
        h_loaded, stored = s.sems("h_loaded", 2), s.sems("stored", 2)
        raw_loaded, high_done, low_done = s.sems("raw_loaded", PIECES), s.sems("high_done", PIECES), s.sems("low_done", PIECES)
        turn_done, hT_high, hT_low = s.sem("turn_done"), s.sem("hT_high"), s.sem("hT_low")
        gate_done, up_done, sig_done = s.sem("gate_done"), s.sem("up_done"), s.sem("sig_done")
        gated_done, act_done, turn2_done = s.sem("gated_done"), s.sem("act_done"), s.sem("turn2_done")
        act_hT_high, act_hT_low = s.sem("act_hT_high"), s.sem("act_hT_low")
        down_done, y_done = s.sem("down_done"), s.sem("y_done")
        zero_set, zero_stored = s.sem("zero_set"), s.sem("zero_stored")
        w_gate = ins["w_exp_gate"][0].rearrange("e (p k) n -> e p (k n)", k=KD)
        w_up = ins["w_exp_up"][0].rearrange("e (p k) n -> e p (k n)", k=KD)
        w_down = ins["w_exp_down"][0].rearrange("e (p k) n -> e p (k n)", k=KF)
        source = (w_gate, w_gate, w_up, w_up, w_down, w_down)
        block = stack.enter_context(nc.Block())

        def last_pair(eng):
            return eng.value_load(tables["blocks"][0:1, 0:1], min_val=SEQ // P - 1, max_val=BLOCKS // 2 - 1)

        def is_new(eng, n):
            return eng.value_load(tables["new"][0:1, ds(n, 1)], min_val=0, max_val=1) > 0

        def ordinal(eng, n):
            return eng.value_load(tables["ordinal"][0:1, ds(n, 1)], min_val=0, max_val=NE)

        def all_blocks(eng, body):
            more = last_pair(eng)
            body(0, 0, 0, True, False)
            with eng.Fori(0, more) as j:
                body(2 * j + 1, 1, j, False, False)
                body(2 * j + 2, 0, j + 1, False, False)
            body(2 * more + 1, 1, more, False, True)
            return more

        @block.sync
        def _(sp):
            def load(n, pieces):
                with sp.If(is_new(sp, n)):
                    e = sp.value_load(tables["expert"][0:1, ds(n, 1)], min_val=0, max_val=NE - 1)
                    o = ordinal(sp, n)
                    for c in pieces:
                        sp.wait_ge(low_done[c], o)
                        sp.dma_start(raw[:, c], source[c][ds(e, 1), :, (c % 2) * HALF:(c % 2 + 1) * HALF].rearrange(
                            "e p n -> (e p) n")).then_inc(raw_loaded[c], 16)

            def work(n, u, i, first, last):
                load(n, DOWN)
                if not last:
                    load(n + 2, GATE + UP)

            load(0, GATE + UP)
            load(1, GATE + UP)
            all_blocks(sp, work)
            sp.wait_ge(zero_set, 1)
            idle = sp.value_load(tables["blocks"][0:1, 1:2], min_val=0, max_val=BLOCKS - 2 * SEQ // P)
            with sp.Fori(0, idle + 1) as n:
                sp.dma_start(y_dram[ds((BLOCKS - n) * P, P), :].rearrange("p (r n) -> p r n", n=ZERO_COLS),
                             zero[:].unsqueeze(1).to_broadcast([P, D // ZERO_COLS, ZERO_COLS])).then_inc(zero_stored, 16)
            sp.wait_ge(zero_stored, 16 * idle + 16)
            sp.nop(nofuse=True)

        def split_low(eng, c, o):
            eng.wait_ge(high_done[c], o)
            eng.tensor_tensor(low[:, c], raw[:, c], high[:, c].bitcast(F32), ALU.subtract).then_inc(low_done[c], 1)

        @block.gpsimd
        def _(pool):
            def gather(n, u, i):
                pool.wait_ge(turn_done, n + 1)
                pool.tensor_copy(row[u][:], tables["rows"][:, n:n + 1] if isinstance(n, int) else tables["rows"][:, ds(n, 1)]).then_inc(row_set, 1)
                pool.wait_ge(row_set, n + 1)
                pool.nop(nofuse=True)
                pool.indirect_dma_start(h[u][:], None, h2_dram, bass.IndirectOffsetOnAxis(ap=row[u][:], axis=0)).then_inc(h_loaded[u], 16)

            def split_down(n):
                with pool.If(is_new(pool, n)):
                    split_low(pool, DOWN[1], ordinal(pool, n))

            def work(n, u, i, first, last):
                if not first:
                    split_down(n - 1)
                if not last:
                    gather(n + 2, u, i + 1)
                    with pool.If(is_new(pool, n + 1)):
                        split_low(pool, UP[1], ordinal(pool, n + 1))

            for c in ON_POOL:
                pool.sem_inc(low_done[c], 1)
            gather(0, 0, 0)
            gather(1, 1, 0)
            split_low(pool, UP[1], 1)
            more = all_blocks(pool, work)
            split_down(2 * more + 1)
            pool.wait_ge(h_loaded[0], 16 * more + 32)
            pool.nop(nofuse=True)

        @block.tensor
        def _(pe):
            def product(out, x, pieces, cols):
                k_half = HALF // cols
                for c in range(cols // BANK):
                    for k in range(2 * k_half):
                        at = (k % k_half) * cols + c * BANK
                        w_high = high[:, pieces[k // k_half], at:at + BANK]
                        w_low = low[:, pieces[k // k_half], at:at + BANK]
                        to = out[:, c * BANK:(c + 1) * BANK]
                        pe.matmul(to, x[0][:, k], w_high, start=(k == 0), stop=False)
                        pe.matmul(to, x[0][:, k], w_low, start=False, stop=False)
                        mm = pe.matmul(to, x[1][:, k], w_high, start=False, stop=(k == 2 * k_half - 1))
                return mm

            def split(pieces, o):
                for c in pieces:
                    pe.wait_ge(low_done[c], o + 1)

            def turn(n, u, i):
                pe.wait_ge(h_loaded[u], 16 * i + 16)
                pe.wait_ge(hT_low, n + 1)
                for k in range(KD):
                    mm = pe.transpose(turned[:, k * P:(k + 1) * P], h[u][:].rearrange("p (c k) -> p k c", k=KD)[:, k],
                                      const["ident"][:])
                mm.then_inc(turn_done, 1)

            def turn_hidden(n):
                pe.wait_ge(act_done, n + 2)
                pe.wait_ge(act_hT_low, n + 1)
                for k in range(KF):
                    mm = pe.transpose(turned2[:, k * P:(k + 1) * P], act_h[:].rearrange("p (f k) -> p k f", k=KF)[:, k],
                                      const["ident"][:])
                mm.then_inc(turn2_done, 1)

            def down_product(n):
                o = ordinal(pe, n)
                pe.wait_ge(act_hT_low, n + 2)
                split(DOWN, o)
                pe.wait_ge(y_done, n + 1)
                product(down, act_hT, DOWN, D).then_inc(down_done, 1)

            def work(n, u, i, first, last):
                o = ordinal(pe, n)
                if not first:
                    turn_hidden(n - 1)
                pe.wait_ge(hT_low, n + 2)
                split(GATE, o)
                pe.wait_ge(gated_done, n + 1)
                product(gate, hT[u], GATE, F).then_inc(gate_done, 1)
                if not last:
                    turn(n + 1, 1 - u, i + u)
                split(UP, o)
                pe.wait_ge(act_done, n + 1)
                product(up, hT[u], UP, F).then_inc(up_done, 1)
                if not first:
                    down_product(n - 1)

            pe.sem_inc(turn_done, 2)
            pe.sem_inc(up_done, 2)
            pe.sem_inc(down_done, 2)
            turn(0, 0, 0)
            more = all_blocks(pe, work)
            turn_hidden(2 * more + 1)
            down_product(2 * more + 1)

        @block.scalar
        def _(act):
            def split_high(c, o):
                act.wait_ge(raw_loaded[c], 16 * o)
                act.copy(high[:, c], raw[:, c]).then_inc(high_done[c], 1)

            def split_down(n):
                with act.If(is_new(act, n)):
                    o = ordinal(act, n)
                    act.wait_ge(down_done, n + 2)
                    for c in DOWN:
                        split_high(c, o)

            def split_gate_up(n):
                with act.If(is_new(act, n)):
                    o = ordinal(act, n)
                    act.wait_ge(gate_done, n)
                    for c in GATE:
                        split_high(c, o)
                    act.wait_ge(up_done, n + 2)
                    for c in UP:
                        split_high(c, o)

            def copy_hT(n, u):
                act.wait_ge(turn_done, n + 3)
                act.wait_ge(up_done, n + 1)
                act.copy(hT[u][0][:].rearrange("p k t -> p (k t)"), turned[:]).then_inc(hT_high, 1)

            def copy_act_hT(n):
                act.wait_ge(turn2_done, n + 1)
                act.wait_ge(down_done, n + 2)
                act.copy(act_hT[0][:].rearrange("p k t -> p (k t)"), turned2[:]).then_inc(act_hT_high, 1)

            def store(n, u):
                act.wait_ge(y_done, n + 2)
                act.dma_start(y_dram[ds(n * P, P), :], y[:, u]).then_inc(stored[u], 16)

            def work(n, u, i, first, last):
                if not first:
                    copy_act_hT(n - 1)
                    split_down(n - 1)
                act.wait_ge(gate_done, n + 1)
                act.wait_ge(gated_done, n + 1)
                act.activation(sig[:], gate[:], ACT.Sigmoid).then_inc(sig_done, 1)
                if not last:
                    copy_hT(n + 1, 1 - u)
                    split_gate_up(n + 1)
                if not first:
                    store(n - 1, 1 - u)

            for u in range(2):
                act.sem_inc(stored[u], 16)
            copy_hT(0, 0)
            for c in GATE + UP:
                split_high(c, 1)
            more = all_blocks(act, work)
            copy_act_hT(2 * more + 1)
            split_down(2 * more + 1)
            store(2 * more + 1, 1)
            for u in range(2):
                act.wait_ge(stored[u], 16 * more + 32)
            act.nop(nofuse=True)

        @block.vector
        def _(dve):
            def split_down(n):
                with dve.If(is_new(dve, n)):
                    split_low(dve, DOWN[0], ordinal(dve, n))

            def split_piece(n, pieces):
                with dve.If(is_new(dve, n)):
                    o = ordinal(dve, n)
                    for c in pieces:
                        split_low(dve, c, o)

            def copy_hT(n, u):
                dve.wait_ge(hT_high, n + 1)
                dve.tensor_tensor(hT[u][1][:].rearrange("p k t -> p (k t)"), turned[:],
                                  hT[u][0][:].rearrange("p k t -> p (k t)").bitcast(F32), ALU.subtract).then_inc(hT_low, 1)

            def copy_act_hT(n):
                dve.wait_ge(act_hT_high, n + 1)
                dve.tensor_tensor(act_hT[1][:].rearrange("p k t -> p (k t)"), turned2[:],
                                  act_hT[0][:].rearrange("p k t -> p (k t)").bitcast(F32), ALU.subtract).then_inc(act_hT_low, 1)

            def take(n, u, i):
                dve.wait_ge(down_done, n + 3)
                dve.wait_ge(stored[u], 16 * i + 16)
                dve.tensor_tensor(y[:, u], down[:], gate2[:], ALU.mult).then_inc(y_done, 1)

            def work(n, u, i, first, last):
                if not first:
                    copy_act_hT(n - 1)
                    split_down(n - 1)
                dve.wait_ge(sig_done, n + 1)
                dve.tensor_tensor(gated[:], sig[:], gate[:], ALU.mult).then_inc(gated_done, 1)
                if not last:
                    copy_hT(n + 1, 1 - u)
                    split_piece(n + 1, GATE)
                dve.wait_ge(up_done, n + 3)
                dve.wait_ge(gated_done, n + 2)
                if not first:
                    dve.wait_ge(turn2_done, n)
                dve.tensor_tensor(act_h[:], gated[:], up[:], ALU.mult).then_inc(act_done, 1)
                if not last:
                    split_piece(n + 1, UP[:1])
                if not first:
                    take(n - 1, 1 - u, i - 1 + u)

            dve.memset(zero[:], 0.0).then_inc(zero_set, 1)
            for c in GATE + UP[:1] + DOWN[:1]:
                dve.sem_inc(low_done[c], 1)
            dve.sem_inc(hT_low, 1)
            dve.sem_inc(gated_done, 1)
            dve.sem_inc(act_done, 1)
            dve.sem_inc(act_hT_low, 1)
            dve.sem_inc(y_done, 1)
            copy_hT(0, 0)
            for c in GATE + UP[:1]:
                split_low(dve, c, 1)
            more = all_blocks(dve, work)
            copy_act_hT(2 * more + 1)
            split_down(2 * more + 1)
            take(2 * more + 1, 1, more)


def final_phase(nc, ins, const, weight, slot, x2_dram, y_dram, out):
    with ExitStack() as stack:
        s = Scope(nc, stack, "fin")
        B = 3
        ya = [s.sb(f"ya{u}", [P, D]) for u in range(B)]
        yb = [s.sb(f"yb{u}", [P, D]) for u in range(B)]
        x, res = s.sb("x", [P, B, D]), s.sb("res", [P, B, D])
        g, junk = s.sb("g", [P, D]), s.sb("junk", [P, D])
        ssq, rms, rstd = s.sb("ssq", [P, TILES]), s.sb("rms", [P, TILES]), s.sb("rstd", [P, TILES])
        x_loaded, y_loaded, g_loaded, stored = s.sems("x_loaded", B), s.sems("y_loaded", B), s.sem("g_loaded"), s.sems("stored", B)
        first_done, sum_done, x3_done, ssq_done = s.sem("first_done"), s.sem("sum_done"), s.sem("x3_done"), s.sem("ssq_done")
        rms_done, rstd_done, res_done = s.sem("rms_done"), s.sem("rstd_done"), s.sem("res_done")
        block = stack.enter_context(nc.Block())

        @block.gpsimd
        def _(pool):
            for t in range(TILES):
                if t >= B:
                    pool.wait_ge(x3_done, t - B + 1)
                for j, y in enumerate((ya, yb)):
                    pool.indirect_dma_start(y[t % B][:], None, y_dram,
                                            bass.IndirectOffsetOnAxis(ap=slot[:, j, t:t + 1], axis=0)).then_inc(y_loaded[t % B], 16)

        @block.sync
        def _(sp):
            sp.dma_start(g[:], ins["norm_f_g"].unsqueeze(0).partition_broadcast(P)).then_inc(g_loaded, 16)
            for t in range(TILES):
                if t >= B:
                    sp.wait_ge(res_done, t - B + 1)
                    sp.dma_start(out[0, (t - B) * P:(t - B + 1) * P, :], res[:, t % B]).then_inc(stored[t % B], 16)
                sp.dma_start(x[:, t % B], x2_dram[t * P:(t + 1) * P, :]).then_inc(x_loaded[t % B], 16)
            for t in range(TILES - B, TILES):
                sp.wait_ge(res_done, t + 1)
                sp.dma_start(out[0, t * P:(t + 1) * P, :], res[:, t % B]).then_inc(stored[t % B], 16)
            for u in range(B):
                sp.wait_ge(stored[u], 16 * len(range(u, TILES, B)))

        @block.scalar
        def _(act):
            def first(t):
                act.wait_ge(y_loaded[t % B], 32 * (t // B + 1))
                act.mul(ya[t % B][:], ya[t % B][:], weight[:, 0, t:t + 1]).then_inc(first_done, 1)

            first(0)
            for t in range(TILES):
                if t + 1 < TILES:
                    first(t + 1)
                act.wait_ge(x3_done, t + 1)
                act.activation(junk[:], x[:, t % B], ACT.Square, accum_out=ssq[:, t:t + 1]).then_inc(ssq_done, 1)
                act.wait_ge(ssq_done, t + 1)
                act.activation(rms[:, t:t + 1], ssq[:, t:t + 1], ACT.Sqrt, bias=const["eps"][:],
                               scale=1.0 / D).then_inc(rms_done, 1)

        @block.vector
        def _(dve):
            def combine(t):
                u = t % B
                dve.wait_ge(first_done, t + 1)
                dve.scalar_tensor_tensor(yb[u][:], yb[u][:], weight[:, 1, t:t + 1], ya[u][:], ALU.mult, ALU.add).then_inc(sum_done, 1)
                dve.wait_ge(sum_done, t + 1)
                dve.wait_ge(x_loaded[u], 16 * (t // B + 1))
                dve.tensor_tensor(x[:, u], x[:, u], yb[u][:], ALU.add).then_inc(x3_done, 1)

            def normalise(t):
                u = t % B
                dve.wait_ge(rms_done, t + 1)
                dve.reciprocal(rstd[:, t:t + 1], rms[:, t:t + 1]).then_inc(rstd_done, 1)
                dve.wait_ge(rstd_done, t + 1)
                if t >= B:
                    dve.wait_ge(stored[u], 16 * (t // B))
                dve.scalar_tensor_tensor(res[:, u], x[:, u], rstd[:, t:t + 1], g[:], ALU.mult, ALU.mult).then_inc(res_done, 1)

            dve.wait_ge(g_loaded, 16)
            combine(0)
            for t in range(TILES):
                if t + 1 < TILES:
                    combine(t + 1)
                normalise(t)


def hybrid_layer_kernel(nc, ins, out):
    Scope.numbers = []
    o_dram = nc.dram_tensor("o_rows", [SEQ, SBW], F32, kind="Internal").ap()
    opT_dram = nc.dram_tensor("opT_rows", [POOLW, SEQ], F32, kind="Internal").ap()
    mT_dram = nc.dram_tensor("mT_rows", [D, SEQ], F32, kind="Internal").ap()
    x2_dram = nc.dram_tensor("x2_rows", [SEQ, D], F32, kind="Internal").ap()
    h2_dram = nc.dram_tensor("h2_rows", [SEQ, D], F32, kind="Internal").ap()
    y_dram = nc.dram_tensor("y_rows", [(BLOCKS + 1) * P, D], F32, kind="Internal").ap()
    with ExitStack() as stack:
        s = Scope(nc, stack, "all")
        const = {
            "ident": s.sb("ident", [P, P]),
            "before": s.sb("before", [P, P]), "ones": s.sb("ones", [P, P]), "causal": s.sb("causal", [P, BANK]),
            "eps": s.sb("eps", [P, 1]), "iota": s.sb("iota", [P, P]), "rows": s.sb("rows", [P, TILES], U32),
        }
        gate2 = s.sb("gate2", [P, D])
        w_loaded = s.sem("w_loaded")
        Scope.numbers = []
        c_act = s.sb("c_act", [P, KD])
        logits = s.sb("logits", [P, TILES, EG + NE])
        weight, slot = s.sb("weight", [P, 2, TILES]), s.sb("slot", [P, 2, TILES], U32)
        constants_phase(nc, const)
        with nc.sbuf_tensor("mod2", [P, 3 * D], F32) as mod2:
            with nc.sbuf_tensor("hT", [P, KD, SEQ], F32) as hT:
                with nc.sbuf_tensor("mod1", [P, 2 * D], F32) as mod1:
                    modulation_phase(nc, ins, const, mod1, c_act)
                    front_phase(nc, ins, const, mod1, c_act, mod2, gate2, hT, opT_dram)
                attention_phase(nc, ins, const, hT, o_dram, w_loaded)
                clear_phase(nc)
                branches_phase(nc, ins, const, hT, o_dram, opT_dram, mT_dram)
            output_phase(nc, ins, const, mod2, logits, mT_dram, x2_dram, h2_dram)
        tables = {name: s.sb(f"block_{name}", [P, n], I32)
                  for name, n in (("expert", BLOCKS + 1), ("new", BLOCKS + 1), ("ordinal", BLOCKS + 1), ("blocks", 2))}
        tables["rows"] = s.sb("slot_rows", [P, BLOCKS + 1], U32)
        dispatch_phase(nc, const, logits, weight, slot, tables)
        experts_phase(nc, ins, const, gate2, tables, h2_dram, y_dram)
        final_phase(nc, ins, const, weight, slot, x2_dram, y_dram, out)


_INS = ["x", "c", "norm1_g", "norm2_g", "w_ada", "b_ada", "w_in", "pool_w", "pool_scale", "w_branch_sb",
        "w_branch_pool", "w_out", "w_route_group", "b_route_group", "w_route_expert", "b_route_expert",
        "w_exp_gate", "w_exp_up", "w_exp_down", "norm_f_g"]


def kernel(**inputs):
    import numpy as np
    import concourse.bacc as bacc
    from concourse.bass_utils import run_bass_kernel_spmd

    nc = bacc.Bacc("TRN2", target_bir_lowering=False, num_devices=1)
    arrays, ins = {}, {}
    for name in _INS:
        a = np.asarray(inputs[name])
        if name == "x":
            a = a[:, ::-1]
        a = np.ascontiguousarray(a)
        arrays[f"in_{name}"] = a
        ins[name] = nc.dram_tensor(f"in_{name}", a.shape, mybir.dt.from_np(a.dtype), kind="ExternalInput").ap()
    out = nc.dram_tensor("out_rows", (1, SEQ, D), F32, kind="ExternalOutput").ap()
    hybrid_layer_kernel(nc, ins, out)
    result = run_bass_kernel_spmd(nc, [arrays], core_ids=[0])
    return np.ascontiguousarray(result.results[0]["out_rows"][:, ::-1])
```
